# Optimizing a Trainium2 kernel written in Bass

```python
import math
import jax, jax.numpy as jnp
from jax import lax
import numpy as np

D_MODEL = 2048
BATCH = 1
SEQ = 256
DEPTH = 1

N_MIXERS = 3
HEAD_DIM = 64
N_HEADS = D_MODEL // HEAD_DIM
BRANCH = N_HEADS * HEAD_DIM
N_KV_A = N_HEADS // 8
KV_A = N_KV_A * HEAD_DIM
WINDOW = 128
BLOCK = 128
NORM_EPS = 1e-6
NEG = -1e30

A_COLS = BRANCH + 2 * KV_A + BRANCH
B_COLS = 4 * BRANCH
C_COLS = 4 * BRANCH + N_HEADS


def _n_layers_of(kind):
    return sum(1 for i in range(DEPTH) if i % N_MIXERS == kind)

def _alibi_slopes(n):
    return jnp.asarray(2.0 ** (-8.0 * np.arange(1, n + 1, dtype=np.float32) / n), dtype=jnp.float32)

def rmsnorm(x, g):
    xf = x.astype(jnp.float32)
    r = lax.rsqrt(jnp.mean(xf * xf, axis=-1, keepdims=True) + NORM_EPS)
    return (xf * r * g.astype(jnp.float32)).astype(x.dtype)

def swa_sink_mixer(h, w_in, sinks):
    B, S, _ = h.shape
    nb = S // BLOCK
    G = N_HEADS // N_KV_A
    q, k, v, z = jnp.split(h @ w_in, [BRANCH, BRANCH + KV_A, BRANCH + 2 * KV_A], axis=-1)
    q = q.reshape(B, nb, BLOCK, N_KV_A, G, HEAD_DIM).astype(jnp.float32)
    k = k.reshape(B, nb, BLOCK, N_KV_A, HEAD_DIM).astype(jnp.float32)
    v = v.reshape(B, nb, BLOCK, N_KV_A, HEAD_DIM).astype(jnp.float32)

    def band(a):
        prev = jnp.concatenate([jnp.zeros_like(a[:, :1]), a[:, :-1]], axis=1)
        return jnp.concatenate([prev, a], axis=2)

    kb, vb = band(k), band(v)
    scores = jnp.einsum('bnqhgd,bnkhd->bnhgqk', q, kb) * (HEAD_DIM ** -0.5)
    qi = jnp.arange(BLOCK)[:, None]
    kj = jnp.arange(2 * BLOCK)[None, :]
    dist = (qi + BLOCK - kj).astype(jnp.float32)
    s_pos = jnp.arange(nb)[:, None, None] * BLOCK - BLOCK + kj[None]
    valid = (dist >= 0) & (dist < WINDOW) & (s_pos >= 0)
    slopes = _alibi_slopes(N_HEADS).reshape(N_KV_A, G)
    scores = scores - slopes[:, :, None, None] * dist
    scores = jnp.where(valid[None, :, None, None], scores, NEG)
    sink = sinks.astype(jnp.float32).reshape(N_KV_A, G)
    sink_col = jnp.broadcast_to(sink[None, None, :, :, None, None], scores.shape[:-1] + (1,))
    p = jax.nn.softmax(jnp.concatenate([scores, sink_col], axis=-1), axis=-1)[..., :-1]
    o = jnp.einsum('bnhgqk,bnkhd->bnqhgd', p, vb).reshape(B, S, BRANCH)
    return o, z

def stick_breaking_mixer(h, w_in):
    B, S, _ = h.shape
    nb = S // BLOCK
    q, k, v, z = jnp.split(h @ w_in, 4, axis=-1)
    q = q.reshape(B, nb, BLOCK, N_HEADS, HEAD_DIM).transpose(1, 0, 3, 2, 4).astype(jnp.float32)
    k = k.reshape(B, S, N_HEADS, HEAD_DIM).astype(jnp.float32)
    v = v.reshape(B, S, N_HEADS, HEAD_DIM).astype(jnp.float32)
    s_pos = jnp.arange(S)
    scale = HEAD_DIM ** -0.5

    def block(args):
        qb, n = args
        t_pos = n * BLOCK + jnp.arange(BLOCK)
        logits = jnp.einsum('bhqd,bshd->bhqs', qb, k) * scale
        before = s_pos[None, :] < t_pos[:, None]
        log_fail = jnp.where(before, jax.nn.log_sigmoid(-logits), 0.0)
        incl = lax.cumsum(log_fail, axis=3, reverse=True)
        suffix = jnp.concatenate([incl[..., 1:], jnp.zeros_like(incl[..., :1])], axis=-1)
        a = jnp.where(before, jnp.exp(jax.nn.log_sigmoid(logits) + suffix), 0.0)
        return jnp.einsum('bhqs,bshd->bqhd', a, v)

    o = lax.map(block, (q, jnp.arange(nb)))
    o = o.transpose(1, 0, 2, 3, 4).reshape(B, S, BRANCH)
    return o, z

def forgetting_mixer(h, w_in, b_f):
    B, S, _ = h.shape
    nb = S // BLOCK
    q, k, v, z, f_logit = jnp.split(h @ w_in, [BRANCH, 2 * BRANCH, 3 * BRANCH, 4 * BRANCH], axis=-1)
    log_f = jax.nn.log_sigmoid(f_logit.astype(jnp.float32) + b_f.astype(jnp.float32))
    cum = lax.cumsum(log_f, axis=1).transpose(0, 2, 1)
    q = q.reshape(B, nb, BLOCK, N_HEADS, HEAD_DIM).transpose(1, 0, 3, 2, 4).astype(jnp.float32)
    cq = cum.reshape(B, N_HEADS, nb, BLOCK).transpose(2, 0, 1, 3)
    k = k.reshape(B, S, N_HEADS, HEAD_DIM).astype(jnp.float32)
    v = v.reshape(B, S, N_HEADS, HEAD_DIM).astype(jnp.float32)
    s_pos = jnp.arange(S)
    scale = HEAD_DIM ** -0.5

    def block(args):
        qb, cqb, n = args
        t_pos = n * BLOCK + jnp.arange(BLOCK)
        logits = jnp.einsum('bhqd,bshd->bhqs', qb, k) * scale + cqb[..., :, None] - cum[:, :, None, :]
        causal = s_pos[None, :] <= t_pos[:, None]
        p = jax.nn.softmax(jnp.where(causal, logits, NEG), axis=-1)
        return jnp.einsum('bhqs,bshd->bqhd', p, v)

    o = lax.map(block, (q, cq, jnp.arange(nb)))
    o = o.transpose(1, 0, 2, 3, 4).reshape(B, S, BRANCH)
    return o, z

def first_inputs(seed: int = 0) -> dict:
    key = jax.random.key(seed)
    ks = jax.random.split(key, 12)
    n_a, n_b, n_c = _n_layers_of(0), _n_layers_of(1), _n_layers_of(2)
    f32 = jnp.float32
    nrm = jax.random.normal
    return {
        "x": nrm(ks[0], (BATCH, SEQ, D_MODEL), f32),
        "g_pre": 1.0 + 0.02 * nrm(ks[1], (DEPTH, D_MODEL), f32),
        "g_post": 1.0 + 0.02 * nrm(ks[2], (DEPTH, D_MODEL), f32),
        "w_in_a": nrm(ks[3], (n_a, D_MODEL, A_COLS), f32) * D_MODEL ** -0.5,
        "w_out_a": nrm(ks[4], (n_a, BRANCH, D_MODEL), f32) * BRANCH ** -0.5,
        "sinks_a": 0.5 * nrm(ks[5], (n_a, N_HEADS), f32),
        "w_in_b": nrm(ks[6], (n_b, D_MODEL, B_COLS), f32) * D_MODEL ** -0.5,
        "w_out_b": nrm(ks[7], (n_b, BRANCH, D_MODEL), f32) * BRANCH ** -0.5,
        "w_in_c": nrm(ks[8], (n_c, D_MODEL, C_COLS), f32) * D_MODEL ** -0.5,
        "b_f_c": 1.0 + 5.0 * jax.random.uniform(ks[9], (n_c, N_HEADS), f32),
        "w_out_c": nrm(ks[10], (n_c, BRANCH, D_MODEL), f32) * BRANCH ** -0.5,
    }

def first_block(x, g_pre, g_post, w_in_a, w_out_a, sinks_a, w_in_b, w_out_b, w_in_c, b_f_c, w_out_c):
    for i in range(DEPTH):
        kind, j = i % N_MIXERS, i // N_MIXERS
        h = rmsnorm(x, g_pre[i])
        if kind == 0:
            o, z = swa_sink_mixer(h, w_in_a[j], sinks_a[j])
            w_out = w_out_a[j]
        elif kind == 1:
            o, z = stick_breaking_mixer(h, w_in_b[j])
            w_out = w_out_b[j]
        else:
            o, z = forgetting_mixer(h, w_in_c[j], b_f_c[j])
            w_out = w_out_c[j]
        y = (o.astype(z.dtype) * jax.nn.silu(z)) @ w_out
        x = x + rmsnorm(y, g_post[i])
    return x


HEAD_DIM_2 = 128
MOBA_HEADS = 8
MOBA_BLOCK = 256
MOBA_TOPK = 3
DSA_HEADS = 8
IDX_HEADS = 16
IDX_DIM = 64
DSA_TOPK_MAX = 256
D_FF = 4 * D_MODEL
ROPE_THETA = 10000.0
Q_CHUNK = 32
RMS_EPS = 1e-6
MOBA_W = MOBA_HEADS * HEAD_DIM_2
DSA_W = DSA_HEADS * HEAD_DIM_2
IN_SIZES = (3 * MOBA_W, 3 * DSA_W, IDX_HEADS * IDX_DIM, IDX_DIM, IDX_HEADS, D_MODEL, D_MODEL)
D_IN = 3 * MOBA_W + 3 * DSA_W + IDX_HEADS * IDX_DIM + IDX_DIM + IDX_HEADS + 2 * D_MODEL


def _rmsnorm(x, g):
    xf = x.astype(jnp.float32)
    y = xf * lax.rsqrt(jnp.mean(xf * xf, axis=-1, keepdims=True) + RMS_EPS)
    return (y * g.astype(jnp.float32)).astype(x.dtype)

def _rope(x):
    T, dh = x.shape[1], x.shape[-1]
    half = dh // 2
    inv_freq = jnp.power(ROPE_THETA, -jnp.arange(half, dtype=jnp.float32) / half)
    ang = jnp.arange(T, dtype=jnp.float32)[:, None] * inv_freq[None, :]
    cos = jnp.cos(ang)[None, :, None, :]
    sin = jnp.sin(ang)[None, :, None, :]
    xf = x.astype(jnp.float32)
    x1, x2 = xf[..., :half], xf[..., half:]
    return jnp.concatenate([x1 * cos - x2 * sin, x2 * cos + x1 * sin], axis=-1).astype(x.dtype)

def _moba_attention(q, k, v):
    B, T, H, D = q.shape
    scale = D ** -0.5
    nb = -(-T // MOBA_BLOCK)
    pad = nb * MOBA_BLOCK - T
    kpad = jnp.pad(k, ((0, 0), (0, pad), (0, 0), (0, 0)))
    vpad = jnp.pad(v, ((0, 0), (0, pad), (0, 0), (0, 0)))
    kb = kpad.reshape(B, nb, MOBA_BLOCK, H, D)
    vb = vpad.reshape(B, nb, MOBA_BLOCK, H, D)
    k_mean = jnp.mean(kb.astype(jnp.float32), axis=2)
    gate = jnp.einsum('bthd,bnhd->bthn', q.astype(jnp.float32), k_mean)
    qblk = jnp.arange(T) // MOBA_BLOCK
    past = jnp.arange(nb)[None, :] < qblk[:, None]
    gate = jnp.where(past[None, :, None, :], gate, -jnp.inf)
    n_sel = max(1, min(MOBA_TOPK, nb - 1))
    _, sel_idx = lax.top_k(gate, n_sel)
    sel_ok = sel_idx < qblk[None, :, None, None]
    kbt = jnp.transpose(kb, (0, 3, 1, 2, 4))
    vbt = jnp.transpose(vb, (0, 3, 1, 2, 4))
    b_ix = jnp.arange(B)[:, None, None, None]
    h_ix = jnp.arange(H)[None, None, :, None]

    def chunk(start):
        qc = lax.dynamic_slice_in_dim(q, start, Q_CHUNK, axis=1)
        idx = lax.dynamic_slice_in_dim(sel_idx, start, Q_CHUNK, axis=1)
        ok = lax.dynamic_slice_in_dim(sel_ok, start, Q_CHUNK, axis=1)
        kg = kbt[b_ix, h_ix, idx]
        vg = vbt[b_ix, h_ix, idx]
        s_sel = jnp.einsum('bchd,bchsjd->bchsj', qc, kg).astype(jnp.float32) * scale
        s_sel = jnp.where(ok[..., None], s_sel, -jnp.inf).reshape(B, Q_CHUNK, H, n_sel * MOBA_BLOCK)
        blk_start = (start // MOBA_BLOCK) * MOBA_BLOCK
        ko = lax.dynamic_slice_in_dim(kpad, blk_start, MOBA_BLOCK, axis=1)
        vo = lax.dynamic_slice_in_dim(vpad, blk_start, MOBA_BLOCK, axis=1)
        s_own = jnp.einsum('bchd,bjhd->bchj', qc, ko).astype(jnp.float32) * scale
        qpos = start + jnp.arange(Q_CHUNK)
        kpos = blk_start + jnp.arange(MOBA_BLOCK)
        causal = kpos[None, :] <= qpos[:, None]
        s_own = jnp.where(causal[None, :, None, :], s_own, -jnp.inf)
        p = jax.nn.softmax(jnp.concatenate([s_sel, s_own], axis=-1), axis=-1).astype(v.dtype)
        p_sel = p[..., :n_sel * MOBA_BLOCK].reshape(B, Q_CHUNK, H, n_sel, MOBA_BLOCK)
        p_own = p[..., n_sel * MOBA_BLOCK:]
        return (jnp.einsum('bchsj,bchsjd->bchd', p_sel, vg)
                + jnp.einsum('bchj,bjhd->bchd', p_own, vo))

    starts = jnp.arange(T // Q_CHUNK, dtype=jnp.int32) * Q_CHUNK
    outs = lax.map(chunk, starts)
    return jnp.moveaxis(outs, 0, 1).reshape(B, T, H, D)

def _dsa_attention(q, k, v, q_idx, k_idx, w_idx):
    B, T, H, D = q.shape
    scale = D ** -0.5
    idx_scale = (IDX_DIM ** -0.5) * (IDX_HEADS ** -0.5)
    topk = min(DSA_TOPK_MAX, T // 4)
    kidx_f = k_idx.astype(jnp.float32)
    b_ix = jnp.arange(B)[:, None, None]

    def chunk(start):
        qc = lax.dynamic_slice_in_dim(q, start, Q_CHUNK, axis=1)
        qi = lax.dynamic_slice_in_dim(q_idx, start, Q_CHUNK, axis=1).astype(jnp.float32)
        wi = lax.dynamic_slice_in_dim(w_idx, start, Q_CHUNK, axis=1).astype(jnp.float32)
        rel = jax.nn.relu(jnp.einsum('bchi,bsi->bchs', qi, kidx_f))
        score = jnp.einsum('bch,bchs->bcs', wi, rel) * idx_scale
        qpos = start + jnp.arange(Q_CHUNK)
        admissible = jnp.arange(T)[None, :] <= qpos[:, None]
        score = jnp.where(admissible[None], score, -jnp.inf)
        _, idx = lax.top_k(score, topk)
        ok = idx <= qpos[None, :, None]
        kg = k[b_ix, idx]
        vg = v[b_ix, idx]
        s = jnp.einsum('bchd,bckhd->bchk', qc, kg).astype(jnp.float32) * scale
        s = jnp.where(ok[:, :, None, :], s, -jnp.inf)
        p = jax.nn.softmax(s, axis=-1).astype(v.dtype)
        return jnp.einsum('bchk,bckhd->bchd', p, vg)

    starts = jnp.arange(T // Q_CHUNK, dtype=jnp.int32) * Q_CHUNK
    outs = lax.map(chunk, starts)
    return jnp.moveaxis(outs, 0, 1).reshape(B, T, H, D)

def second_inputs(seed: int = 0) -> dict:
    key = jax.random.key(seed)
    ks = jax.random.split(key, 16)
    f32 = jnp.float32

    def nrm(k, shape, fan_in, mult=1.0):
        return jax.random.normal(k, shape, f32) * (mult * fan_in ** -0.5)

    def gain(k):
        return 1.0 + 0.02 * jax.random.normal(k, (DEPTH, D_MODEL), f32)

    return {
        'x': jax.random.normal(ks[0], (BATCH, SEQ, D_MODEL), f32),
        'c': jax.random.normal(ks[1], (BATCH, D_MODEL), f32),
        'w_ada': nrm(ks[2], (DEPTH, D_MODEL, 6 * D_MODEL), D_MODEL),
        'b_ada': 0.02 * jax.random.normal(ks[3], (DEPTH, 6 * D_MODEL), f32),
        'g_pre_mix': gain(ks[4]),
        'g_post_mix': gain(ks[5]),
        'w_in': nrm(ks[6], (DEPTH, D_MODEL, D_IN), D_MODEL),
        'w_moba_out': nrm(ks[7], (DEPTH, MOBA_W, D_MODEL), MOBA_W),
        'w_dsa_out': nrm(ks[8], (DEPTH, DSA_W, D_MODEL), DSA_W),
        'w_o': nrm(ks[9], (DEPTH, D_MODEL, D_MODEL), D_MODEL),
        'g_pre_ffn': gain(ks[10]),
        'g_post_ffn': gain(ks[11]),
        'w_ff1': nrm(ks[12], (DEPTH, D_MODEL, D_FF), D_MODEL),
        'w_ff2': nrm(ks[13], (DEPTH, D_FF, D_MODEL), D_FF),
    }

def second_block(x, c, w_ada, b_ada, g_pre_mix, g_post_mix, w_in, w_moba_out, w_dsa_out, w_o,
              g_pre_ffn, g_post_ffn, w_ff1, w_ff2):
    B, T, _ = x.shape
    cs = jax.nn.silu(c)
    split_pts = [int(v) for v in np.cumsum(IN_SIZES)[:-1]]
    for l in range(DEPTH):
        mod = cs @ w_ada[l] + b_ada[l]
        sh1, sc1, gt1, sh2, sc2, gt2 = [m[:, None, :] for m in jnp.split(mod, 6, axis=-1)]

        h = _rmsnorm(x, g_pre_mix[l]) * (1.0 + sc1) + sh1
        proj = h @ w_in[l]
        p_moba, p_dsa, p_qi, p_ki, p_wi, ga, gb = jnp.split(proj, split_pts, axis=-1)
        qa, ka, va = [t.reshape(B, T, MOBA_HEADS, HEAD_DIM_2) for t in jnp.split(p_moba, 3, axis=-1)]
        qb, kb, vb = [t.reshape(B, T, DSA_HEADS, HEAD_DIM_2) for t in jnp.split(p_dsa, 3, axis=-1)]
        q_idx = _rope(p_qi.reshape(B, T, IDX_HEADS, IDX_DIM))
        k_idx = _rope(p_ki[:, :, None, :])[:, :, 0, :]
        ya = _moba_attention(_rope(qa), _rope(ka), va).reshape(B, T, MOBA_W) @ w_moba_out[l]
        yb = _dsa_attention(_rope(qb), _rope(kb), vb, q_idx, k_idx, p_wi).reshape(B, T, DSA_W) @ w_dsa_out[l]
        y = (jax.nn.sigmoid(ga) * ya + jax.nn.sigmoid(gb) * yb) @ w_o[l]
        x = x + gt1 * _rmsnorm(y, g_post_mix[l])

        h = _rmsnorm(x, g_pre_ffn[l]) * (1.0 + sc2) + sh2
        f = jnp.square(jax.nn.relu(h @ w_ff1[l])) @ w_ff2[l]
        x = x + gt2 * _rmsnorm(f, g_post_ffn[l])
    return x


def setup_inputs(seed=0):
    out = dict(first_inputs(seed))
    for name, value in second_inputs(seed + 1).items():
        if name != "x":
            out[name + "_2"] = value
    return out


def reference(
    x, g_pre, g_post, w_in_a, w_out_a, sinks_a, w_in_b, w_out_b, w_in_c, b_f_c, w_out_c, c_2,
    w_ada_2, b_ada_2, g_pre_mix_2, g_post_mix_2, w_in_2, w_moba_out_2, w_dsa_out_2, w_o_2,
    g_pre_ffn_2, g_post_ffn_2, w_ff1_2, w_ff2_2,
):
    x = first_block(
        x, g_pre, g_post, w_in_a, w_out_a, sinks_a, w_in_b, w_out_b, w_in_c, b_f_c, w_out_c,
    )
    return second_block(
        x, c_2, w_ada_2, b_ada_2, g_pre_mix_2, g_post_mix_2, w_in_2, w_moba_out_2, w_dsa_out_2,
        w_o_2, g_pre_ffn_2, g_post_ffn_2, w_ff1_2, w_ff2_2,
    )


_drawn_inputs = setup_inputs


def setup_inputs(seed=0):
    import zlib

    import numpy as np

    out = dict(_drawn_inputs(seed))
    spreads = {}
    factors = {'g_post': 2.715,
     'g_pre_mix_2': 2.948,
     'g_post_mix_2': 65.128,
     'g_pre_ffn_2': 69.134,
     'g_post_ffn_2': 120.921}
    for name, (base, spread) in spreads.items():
        noise = np.random.default_rng([zlib.crc32(name.encode()), seed]).standard_normal(out[name].shape)
        drawn = base * np.exp(spread * noise) if base else spread * noise
        out[name] = __import__('jax').numpy.asarray(drawn.astype(out[name].dtype))
    for name, factor in factors.items():
        out[name] = (out[name] * factor).astype(out[name].dtype)
    return out
```

```python
from contextlib import ExitStack

import numpy as np

import concourse.bass as bass
from concourse import mybir

F32 = mybir.dt.float32
F32R = mybir.dt.float32r
ALU = mybir.AluOpType
ACT = mybir.ActivationFunctionType
AX = mybir.AxisListType

P = 128
D = 2048
SEQ = 256
T = SEQ // P
KT = D // P
CH = 512
KG = 2
UNIT = KG * CH
SLOTS = 4
UPT = KT // KG
AHEAD = 3
EPS = 1e-6

HEADS_A = 32
DH_A = 64
KV_A = 4
GROUP_A = HEADS_A // KV_A
KV_COLS = KV_A * DH_A
WINDOW = 128
MASK_W = P + SEQ

HEADS_2 = 8
DH_2 = 128
IDX_HEADS = 16
IDX_DIM = 64
TOPK = min(256, SEQ // 4)
D_FF = 4 * D
W2 = HEADS_2 * DH_2
COL_QI = 6 * W2
COL_KI = COL_QI + IDX_HEADS * IDX_DIM
KI_COLS = IDX_DIM + IDX_HEADS
COL_GA = COL_KI + KI_COLS
COL_GB = COL_GA + D
SCALE_A = DH_A ** -0.5
SCALE_2 = DH_2 ** -0.5
IDX_SCALE = (IDX_DIM ** -0.5) * (IDX_HEADS ** -0.5)

MASKED = -1e30
FAR = 1e34
LOWEST = -3.4e38
PICKED = -3.0e38
PICKED_BELOW = -2.0e38

TURN_KV, TURN_Q, TURN_Z, TURN_OUT = 0, 1, 5, 9
TURN_KI, TURN_QI, TURN_GRP, TURN_GATE, TURN_YAB = 13, 14, 16, 28, 30
TURN_WO, TURN_FF1, TURN_FF2, TURNS = 40, 44, 60, 76
CHUNK_GATE, CHUNK_YAB, CHUNK_WO, CHUNK_FF1 = 28, 30, 44, 48

C_ID = 0
C_DIST = C_ID + P
C_CAUSAL = C_DIST + MASK_W
C_SLOPE = C_CAUSAL + MASK_W
C_COS = C_SLOPE + HEADS_A
C_SIN = C_COS + T * DH_2 // 2
C_COSI = C_SIN + T * DH_2 // 2
C_SINI = C_COSI + T * IDX_DIM // 2
C_ONE = C_SINI + T * IDX_DIM // 2
CONSTS = C_ONE + P

V_PRE, V_MIX, V_FFN, V_C = 0, KT, 2 * KT, 3 * KT
VECS = 4 * KT

SH1, SC1, GT1, SH2, SC2, GT2 = range(6)


def shape_constants():
    out = np.zeros((P, CONSTS), np.float32)
    out[:, C_ID:C_ID + P] = np.eye(P)
    q = np.arange(P)[:, None]
    query = np.concatenate([np.broadcast_to(q, (P, P)), np.broadcast_to(q + P, (P, SEQ))], axis=1)
    key = np.concatenate([np.arange(P), np.arange(SEQ)])[None, :]
    dist = query - key
    seen = (dist >= 0) & (dist < WINDOW)
    out[:, C_DIST:C_DIST + MASK_W] = np.where(seen, -dist / SCALE_A, -FAR)
    out[:, C_CAUSAL:C_CAUSAL + MASK_W] = np.where(dist >= 0, 0.0, MASKED)
    slopes = 2.0 ** (-8.0 * np.arange(1, HEADS_A + 1, dtype=np.float32) / HEADS_A)
    out[:, C_SLOPE:C_SLOPE + HEADS_A] = slopes.astype(np.float32)[None]
    for half, c_cos, c_sin in ((DH_2 // 2, C_COS, C_SIN), (IDX_DIM // 2, C_COSI, C_SINI)):
        power = -np.arange(half, dtype=np.float32) / np.float32(half)
        freq = np.power(10000.0, power.astype(np.float64)).astype(np.float32)
        angle = (np.arange(SEQ, dtype=np.float32)[:, None] * freq[None]).astype(np.float32)
        for c, table in ((c_cos, np.cos(angle)), (c_sin, np.sin(angle))):
            out[:, c:c + T * half] = table.astype(np.float32).reshape(T, P, half).transpose(1, 0, 2).reshape(P, -1)
    out[:, C_ONE:C_ONE + P] = 1.0
    return out


def two_block_kernel(nc, x_in, w_in_a, w_out_a, w_ada, w_in_2, w_moba, w_dsa, w_o, w_ff1, w_ff2,
                     b_ada, g_post, g_post_mix, g_post_ffn, sinks, vecs_in, consts_in, out):
    ctx = ExitStack()
    with ctx:
        def sb(name, shape, dt=F32, on=ctx):
            return on.enter_context(nc.sbuf_tensor(name, shape, dt))

        def sem(name):
            return ctx.enter_context(nc.semaphore(name))

        raw = sb("raw", [P, SLOTS, UNIT])
        w_hi = sb("w_hi", [P, SLOTS, UNIT], F32R)
        w_lo = sb("w_lo", [P, SLOTS, UNIT], F32R)
        x = sb("x", [P, T, D])
        h_hi = sb("h_hi", [P, KT, SEQ], F32R)
        h_lo = sb("h_lo", [P, KT, SEQ], F32R)
        post_gain = sb("post_gain", [P, D])
        acc_a = sb("acc_a", [P, D])
        acc_b = sb("acc_b", [P, D])
        ada_raw = sb("ada_raw", [P, 2, D // 2])
        consts = sb("consts", [P, CONSTS])
        vecs = sb("vecs", [P, VECS])
        cond = sb("cond", [P, KT])
        pre_gain = sb("pre_gain", [P, KT])
        pre_shift = sb("pre_shift", [P, KT])
        y_sq = sb("y_sq", [P, T, D // CH])
        y_var = sb("y_var", [P, T])
        y_rstd = sb("y_rstd", [P, T])
        x_sq = sb("x_sq", [P, T])
        x_rstd = sb("x_rstd", [P, T])

        with ExitStack() as a:
            o_gated_t = sb("o_gated_t", [P, KT, SEQ], on=a)
            o = sb("o", [P, T, D], on=a)
            v1 = sb("v1", [P, T, KV_COLS], on=a)
            k1_t = sb("k1_t", [P, KV_A, SEQ], on=a)
            k1_cur = sb("k1_cur", [P, SEQ], on=a)
            v1_cur = sb("v1_cur", [P, T, DH_A], on=a)
            q1_tok = sb("q1_tok", [P, T, CH], on=a)
            q1_t = sb("q1_t", [P, GROUP_A // 2, SEQ], on=a)
            bias1 = sb("bias1", [P, 2, MASK_W], on=a)
            s1 = sb("s1", [P, 2, MASK_W], on=a)
            p1_t = sb("p1_t", [P, MASK_W], on=a)
            z_silu = sb("z_silu", [P, T, CH], on=a)
            slope_cur = sb("slope_cur", [P, GROUP_A], on=a)
            sink_cur = sb("sink_cur", [P, GROUP_A], on=a)
            sink = sb("sink", [P, HEADS_A], on=a)
            sink_sc = sb("sink_sc", [P, HEADS_A], on=a)
            m1 = sb("m1", [P, 2, T], on=a)
            neg_m1 = sb("neg_m1", [P, T, HEADS_A], on=a)
            l1 = sb("l1", [P, T, HEADS_A], on=a)
            sink_e = sb("sink_e", [P, T, HEADS_A], on=a)
            neg_cur = sb("neg_cur", [P, GROUP_A, T], on=a)
            l_cur = sb("l_cur", [P, GROUP_A, T], on=a)
        with ExitStack() as a:
            sb("pad_o_gated_t", [P, KT, SEQ], on=a)
            y1 = sb("y1", [P, T, D], on=a)
            sq1 = sb("sq1", [P, CH], on=a)
        with ExitStack() as a:
            o_hi = sb("o_hi", [P, 2 * HEADS_2, SEQ], F32R, on=a)
            o_lo = sb("o_lo", [P, 2 * HEADS_2, SEQ], F32R, on=a)
            with ExitStack() as a2:
                rope_a = sb("rope_a", [P, CH], on=a2)
                rope_b = sb("rope_b", [P, CH], on=a2)
                rot = sb("rot", [P, T, CH], on=a2)
                q2_t = sb("q2_t", [P, 4, SEQ], on=a2)
                k2_t = sb("k2_t", [P, 4, SEQ], on=a2)
                v2 = sb("v2", [P, T, CH], on=a2)
                s2 = sb("s2", [P, 2, MASK_W], on=a2)
                p2_t = sb("p2_t", [P, MASK_W], on=a2)
                mask_cur = sb("mask_cur", [P, MASK_W], on=a2)
                masks = sb("masks", [P, 2, MASK_W], on=a2)
                score = sb("score", [P, MASK_W], on=a2)
                w_idx = sb("w_idx", [P, T, IDX_HEADS], on=a2)
                top8 = sb("top8", [P, T, 8], on=a2)
                m2 = sb("m2", [P, 2, T], on=a2)
                l2 = sb("l2", [P, 2, T], on=a2)
                l2_inv = sb("l2_inv", [P, T], on=a2)
            with ExitStack() as a2:
                y_t = sb("y_t", [P, KT, SEQ], on=a2)
                gate_a = sb("gate_a", [P, T, CH], on=a2)
                gate_b = sb("gate_b", [P, T, CH], on=a2)
                y_tok = sb("y_tok", [P, T, CH], on=a2)
        with ExitStack() as a:
            y2 = sb("y2", [P, T, D], on=a)
            sq2 = sb("sq2", [P, CH], on=a)
        with ExitStack() as a:
            f_t = sb("f_t", [P, D_FF // P, SEQ], on=a)
        f_tok = acc_b[:, 0:T * CH].rearrange("p (t n) -> p t n", t=T)
        norm_tmp = post_gain[:, 0:2 * KG * SEQ].rearrange("p (b n) -> p b n", b=2)

        ident = consts[:, C_ID:C_ID + P]
        dist8 = consts[:, C_DIST:C_DIST + MASK_W]
        causal = consts[:, C_CAUSAL:C_CAUSAL + MASK_W]
        ones = consts[:, C_ONE:C_ONE + P]

        banks = [ctx.enter_context(nc.psum_tensor(f"bank{n}", [P, CH], F32)) for n in range(8)]
        PAIR_A, PAIR_B = 0, 1
        pair = [banks[0:2], banks[2:4]]
        SCORES, TURNED, OUTS = 4, 6, 7

        raw_loaded = [sem(f"raw_loaded{s}") for s in range(SLOTS)]
        hi_ready = sem("hi_ready")
        lo_ready = sem("lo_ready")
        mm_done = sem("mm_done")
        front_done = sem("front_done")
        evicted = [[sem(f"evicted_{'ab'[p]}{t}") for t in range(T)] for p in range(2)]
        x_loaded = [sem(f"x_loaded{t}") for t in range(T)]
        consts_loaded = sem("consts_loaded")
        vecs_loaded = sem("vecs_loaded")
        sink_loaded = sem("sink_loaded")
        gain_loaded = [sem(f"gain_loaded{n}") for n in range(3)]
        acc_zero = sem("acc_zero")
        acc_init = [sem(f"acc_init{n}") for n in range(6)]
        ada_loaded = [sem("ada_loaded0"), sem("ada_loaded1")]
        ada_done = sem("ada_done")
        cond_sig = sem("cond_sig")
        cond_ready = sem("cond_ready")
        mod_cols = sem("mod_cols")
        mod_ready = sem("mod_ready")
        mod_rows = sem("mod_rows")
        gain_ready = sem("gain_ready")
        y_squared = sem("y_squared")
        y_scaled = sem("y_scaled")
        y_stat = sem("y_stat")
        y_root = sem("y_root")
        x_new = sem("x_new")
        x_squared = sem("x_squared")
        x_stat = sem("x_stat")
        x_root = sem("x_root")
        x_norm = [sem(f"x_norm{t}") for t in range(T)]
        n_turned = sem("n_turned")
        n_scaled = sem("n_scaled")
        h_hi_ready = sem("h_hi_ready")
        h_lo_ready = sem("h_lo_ready")
        kv_tok = sem("kv_tok")
        k1_turned = sem("k1_turned")
        k1_ready = sem("k1_ready")
        q1_ready = sem("q1_ready")
        q1_turned = sem("q1_turned")
        q1_t_ready = sem("q1_t_ready")
        kv_cur_ready = sem("kv_cur_ready")
        heads_cur = sem("heads_cur")
        sink_scaled = sem("sink_scaled")
        bias_ready = sem("bias_ready")
        s1_ready = sem("s1_ready")
        s1_seen = sem("s1_seen")
        s1_masked = sem("s1_masked")
        neg1_ready = sem("neg1_ready")
        p1_ready = sem("p1_ready")
        p1_turned = sem("p1_turned")
        p1_t_ready = sem("p1_t_ready")
        o1_ready = sem("o1_ready")
        o1_kept = sem("o1_kept")
        stats_kept = sem("stats_kept")
        sink_exp = sem("sink_exp")
        l1_step = sem("l1_step")
        z_sig = sem("z_sig")
        z_ready = sem("z_ready")
        o_step = sem("o_step")
        o_gated = sem("o_gated")
        og_turned = sem("og_turned")
        og_ready = sem("og_ready")
        rot_ready = sem("rot_ready")
        w_idx_ready = sem("w_idx_ready")
        i_turned = sem("i_turned")
        i_t_ready = sem("i_t_ready")
        i_scores = sem("i_scores")
        i_relu = sem("i_relu")
        i_added = sem("i_added")
        top_step = sem("top_step")
        mask_ready = sem("mask_ready")
        qk_turned = sem("qk_turned")
        qk_ready = sem("qk_ready")
        mask_set = sem("mask_set")
        s2_ready = sem("s2_ready")
        s2_seen = sem("s2_seen")
        s2_masked = sem("s2_masked")
        neg2_ready = sem("neg2_ready")
        p2_ready = sem("p2_ready")
        l2_ready = sem("l2_ready")
        p2_normed = sem("p2_normed")
        p2_turned = sem("p2_turned")
        p2_t_ready = sem("p2_t_ready")
        o2_ready = sem("o2_ready")
        o2_hi = sem("o2_hi")
        o2_kept = sem("o2_kept")
        gate_ready = [sem("gate_a_ready"), sem("gate_b_ready")]
        y_part = sem("y_part")
        y_tok_ready = sem("y_tok_ready")
        y_turned = sem("y_turned")
        y_t_ready = sem("y_t_ready")
        f_sq = sem("f_sq")
        f_turned = sem("f_turned")
        f_t_ready = [sem(f"f_t_ready{t}") for t in range(T)]
        f_hi_ready = sem("f_hi_ready")
        f_lo_ready = sem("f_lo_ready")
        stored = sem("stored")

        H_NORM0, H_OUT, H_NORM1, H_WO, H_NORM2 = range(0, 5 * UPT, UPT)

        w_a = w_in_a.rearrange("(k p) n -> p k n", p=P)
        w_oa = w_out_a.rearrange("(k p) n -> p k n", p=P)
        w_2 = w_in_2.rearrange("(k p) n -> p k n", p=P)
        w_m = w_moba.rearrange("(k p) n -> p k n", p=P)
        w_d = w_dsa.rearrange("(k p) n -> p k n", p=P)
        w_oo = w_o.rearrange("(k p) n -> p k n", p=P)
        w_f1 = w_ff1.rearrange("(k p) n -> p k n", p=P)
        w_f2 = w_ff2.rearrange("(k p) n -> p k n", p=P)
        w_ad = w_ada.rearrange("(k p) n -> p k n", p=P)

        def two(ap, k=2):
            return ap.rearrange("p (k n) -> p k n", k=k)

        def unit_of(turn, s):
            return turn * UPT + s

        block = ctx.enter_context(nc.Block())

        @block.sync
        def _(sp):
            def load(turn, s, src, first=False):
                if not first:
                    sp.wait_ge(lo_ready, unit_of(turn, s) - SLOTS + 1)
                dst = two(raw[:, s % SLOTS, :], src.shape[1])[:, :, 0:src.shape[2]]
                sp.dma_start(dst, src).then_inc(raw_loaded[s % SLOTS], 16)

            def load_chunk(turn, w, col, cols=CH, first=False):
                for s in range(UPT):
                    load(turn, s, w[:, KG * s:KG * s + KG, bass.ds(col, cols)], first and s < SLOTS)

            def load_pair(turn, col):
                for s in range(UPT):
                    w, k = (w_m, s) if s < UPT // 2 else (w_d, s - UPT // 2)
                    load(turn, s, w[:, KG * k:KG * k + KG, bass.ds(col, CH)])

            x_rows = x_in.rearrange("(t p) n -> t p n", p=P)
            for t in range(T):
                sp.dma_start(x[:, t, :], x_rows[t]).then_inc(x_loaded[t], 16)
            load_chunk(TURN_KV, w_a, D, first=True)
            with sp.Fori(0, D // CH) as i:
                load_chunk(i + TURN_Q, w_a, i * CH)
            with sp.Fori(0, D // CH) as i:
                load_chunk(i + TURN_Z, w_a, i * CH + D + 2 * KV_COLS)
            with sp.Fori(0, D // CH) as i:
                load_chunk(i + TURN_OUT, w_oa, i * CH)
            load_chunk(TURN_KI, w_2, COL_KI, KI_COLS)
            for c in range(2):
                load_chunk(TURN_QI + c, w_2, COL_QI + c * CH)
            for half in range(2):
                with sp.Fori(0, 2) as b:
                    for part in range(3):
                        load_chunk((b + 2 * half) * 3 + TURN_GRP + part, w_2,
                                   b * CH + (half * 3 + part) * W2)
            load_chunk(TURN_GATE, w_2, COL_GA)
            load_chunk(TURN_GATE + 1, w_2, COL_GB)
            with sp.Fori(0, D // CH - 1) as c:
                load_pair(c * 3 + TURN_YAB, c * CH)
                load_chunk(c * 3 + TURN_YAB + 1, w_2, c * CH + COL_GA + CH)
                load_chunk(c * 3 + TURN_YAB + 2, w_2, c * CH + COL_GB + CH)
            load_pair(TURN_YAB + 9, D - CH)
            with sp.Fori(0, D // CH) as i:
                load_chunk(i + TURN_WO, w_oo, i * CH)
            with sp.Fori(0, D_FF // CH) as i:
                load_chunk(i + TURN_FF1, w_f1, i * CH)
            with sp.Fori(0, TURNS - TURN_FF2) as i:
                for s in range(UPT):
                    load(i + TURN_FF2, s, w_f2[:, bass.ds(i * 4 + s // 2, 1), (s % 2) * UNIT:(s % 2 + 1) * UNIT])
            out_rows = out.rearrange("(t p) n -> t p n", p=P)
            for t in range(T):
                sp.wait_ge(x_new, 2 * T + t + 1)
                sp.dma_start(out_rows[t], x[:, t, :]).then_inc(stored, 16)
            sp.wait_ge(stored, 16 * T)

        @block.gpsimd
        def _(pool):
            def init_acc(acc, part, n):
                pool.memset(acc[:, :], 0.0).then_inc(acc_zero, 1)
                pool.wait_ge(acc_zero, n + 1)
                pool.dma_start(acc[0:1, :], b_ada[:, part * D:(part + 1) * D]).then_inc(acc_init[n], 16)

            def load_ada(m, slot, part, k, half, first=False):
                if not first:
                    pool.wait_ge(ada_done, m - 1)
                col = part * D + half * (D // 2)
                pool.dma_start(two(ada_raw[:, slot, :], 1), w_ad[:, bass.ds(k, 1), col:col + D // 2])\
                    .then_inc(ada_loaded[slot], 16)

            def load_four(m, part, k, first=False):
                for n in range(8):
                    load_ada(m + n, n % 2, part, k + n // 2, n % 2, first and n < 2)

            def bias(i, j):
                pool.wait_ge(s1_masked, i * GROUP_A + j + 1)
                pool.tensor_tensor(bias1[:, j % 2, :], dist8, slope_cur[:, j:j + 1].to_broadcast([P, MASK_W]), ALU.mult)\
                    .then_inc(bias_ready, 1)

            def load_gain(n, g):
                pool.dma_start(post_gain[:, :], g.partition_broadcast(P)).then_inc(gain_loaded[n], 16)

            pool.dma_start(sink[:, :], sinks.partition_broadcast(P)).then_inc(sink_loaded, 16)
            init_acc(acc_a, SC1, 0)
            init_acc(acc_b, SH1, 1)
            load_four(0, SC1, 0, first=True)
            load_four(8, SC1, 4)
            pool.wait_ge(h_lo_ready, H_NORM0 + UPT)
            load_gain(0, g_post)
            pool.wait_ge(consts_loaded, 16)
            with pool.Fori(0, D // CH - 1) as i:
                pool.wait_ge(heads_cur, i + 1)
                for j in range(GROUP_A):
                    bias(i, j)
            pool.wait_ge(heads_cur, D // CH)
            for j in range(GROUP_A):
                load_ada(16 + j, j % 2, SC1, 8 + j // 2, j % 2)
                bias(D // CH - 1, j)
            with pool.Fori(0, D // CH - 1) as c:
                load_four(c * 8 + 24, SH1, c * 4)
            with pool.Fori(0, 2) as it:
                for n in range(8):
                    load_ada(it * 8 + 48 + n, n % 2, (SC1, SH1)[n // 4], it * 2 + 12 + n // 2 % 2, n % 2)
            pool.wait_ge(mod_ready, 2)
            init_acc(acc_a, GT1, 2)
            pool.wait_ge(h_lo_ready, H_NORM1 + UPT)
            load_gain(1, g_post_mix)
            with pool.Fori(0, 4) as g:
                load_four(g * 8 + 64, GT1, g * 4)
            pool.wait_ge(gain_ready, 4)
            init_acc(acc_a, SC2, 3)
            init_acc(acc_b, SH2, 4)
            with pool.Fori(0, 4) as c:
                load_four(c * 16 + 96, SC2, c * 4)
                load_four(c * 16 + 104, SH2, c * 4)
            pool.wait_ge(mod_ready, 4)
            init_acc(acc_a, GT2, 5)
            pool.wait_ge(h_lo_ready, H_NORM2 + UPT)
            load_gain(2, g_post_ffn)
            with pool.Fori(0, 8) as it:
                for n in range(4):
                    load_ada(it * 4 + 160 + n, n % 2, GT2, it * 2 + n // 2, n % 2)

        @block.scalar
        def _(act):
            def split(turn, s, first=False):
                turn, s = turn + s // UPT, s % UPT
                act.wait_ge(raw_loaded[s % SLOTS], (turn * (UPT // SLOTS) + s // SLOTS + 1) * 16)
                if not first:
                    act.wait_ge(mm_done, unit_of(turn, s) - SLOTS + 1)
                act.activation(w_hi[:, s % SLOTS, :], raw[:, s % SLOTS, :], ACT.Copy).then_inc(hi_ready, 1)

            def norm(r, y=None, turn=0):
                if r:
                    act.wait_ge(y_stat, 2 * r)
                    act.activation(y_rstd[:, :], y_var[:, :], ACT.Sqrt).then_inc(y_root, 1)
                for t in range(T):
                    if r:
                        act.wait_ge(x_new, T * (r - 1) + t + 1)
                    else:
                        act.wait_ge(x_loaded[t], 16)
                    act.activation(y[:, t, :], x[:, t, :], ACT.Square, accum_out=x_sq[:, t:t + 1])\
                        .then_inc(x_squared, 1)
                act.wait_ge(x_stat, 2 * r + 1)
                act.activation(x_rstd[:, :], x_sq[:, :], ACT.Sqrt).then_inc(x_root, 1)
                act.wait_ge(x_stat, 2 * r + 2)
                act.activation(y[:, 0, :], x[:, 0, :], ACT.Copy, scale=x_rstd[:, 0:1]).then_inc(x_norm[0], 1)
                if turn:
                    act.wait_ge(mm_done, turn * UPT)
                for s in range(UPT):
                    act.wait_ge(n_scaled, UPT * r + s + 1)
                    act.activation(h_hi[:, KG * s:KG * s + KG, :], two(norm_tmp[:, s % 2, :]), ACT.Copy)\
                        .then_inc(h_hi_ready, 1)

            def round_h(src, turn, ready, count):
                act.wait_ge(ready, count)
                act.wait_ge(mm_done, turn * UPT)
                for s in range(UPT):
                    act.activation(h_hi[:, KG * s:KG * s + KG, :], src[:, KG * s:KG * s + KG, :], ACT.Copy)\
                        .then_inc(h_hi_ready, 1)

            def chunk_result(t, turn, chunk):
                if t == 0:
                    act.wait_ge(front_done, chunk + 1)
                else:
                    act.wait_ge(mm_done, unit_of(turn, UPT))

            def square_y(p, t, turn, chunk, n, col, scratch):
                chunk_result(t, turn, chunk)
                act.wait_ge(y_squared, n)
                act.activation(scratch[:, :], pair[p][t][:, :], ACT.Square, accum_out=y_sq[:, t, bass.ds(col, 1)])\
                    .then_inc(y_squared, 1)

            act.dma_start(consts[:, :], consts_in).then_inc(consts_loaded, 16)
            act.dma_start(vecs[:, :], vecs_in).then_inc(vecs_loaded, 16)
            act.wait_ge(vecs_loaded, 16)
            act.activation(cond[:, :], vecs[:, V_C:V_C + KT], ACT.Sigmoid).then_inc(cond_sig, 1)
            act.sem_inc(y_squared, 1)
            norm(0, y1)
            for s in range(AHEAD):
                split(TURN_KV, s, first=True)

            for s in range(UPT):
                split(TURN_KV, s + AHEAD, first=s + AHEAD < SLOTS)
            for t in range(T):
                chunk_result(t, TURN_KV, 0)
                kv = pair[PAIR_A][t][:, :]
                act.activation(q1_tok[:, t, :].rearrange("p (h r d) -> p h r d", h=KV_A, r=2),
                               kv[:, 0:KV_COLS].rearrange("p (h d) -> p h d", h=KV_A).unsqueeze(2)
                               .to_broadcast([P, KV_A, 2, DH_A]), ACT.Copy).then_inc(kv_tok, 1)
                act.activation(v1[:, t, :], kv[:, KV_COLS:2 * KV_COLS], ACT.Copy).then_inc(evicted[PAIR_A][t], 1)

            def keep_q1(i, turn):
                for t in range(T):
                    chunk_result(t, turn, turn)
                    act.activation(q1_tok[:, t, :], pair[PAIR_B][t][:, :], ACT.Copy).then_inc(evicted[PAIR_B][t], 1)

            def turn_q1(i):
                act.wait_ge(k1_ready, T)
                for t in range(T):
                    act.wait_ge(evicted[PAIR_A][t], 1)
                    act.wait_ge(q1_turned, i * T + t + 1)
                    act.activation(q1_t[:, :, t * P:t * P + P], two(banks[TURNED + t][:, :], 4), ACT.Copy)\
                        .then_inc(q1_t_ready, 1)
                act.activation(k1_cur[:, :], k1_t[:, bass.ds(i, 1), :], ACT.Copy).then_inc(kv_cur_ready, 1)
                act.activation(v1_cur[:, :, :], v1[:, :, bass.ds(i * DH_A, DH_A)], ACT.Copy).then_inc(kv_cur_ready, 1)

            def attn1(i, j):
                act.wait_ge(neg1_ready, i * GROUP_A + j + 1)
                act.activation(s1[:, j % 2, 0:P], s1[:, j % 2, 0:P], ACT.Exp, bias=neg_cur[:, j, 0:1], scale=SCALE_A,
                               accum_out=l_cur[:, j, 0:1])
                act.activation(s1[:, j % 2, P:MASK_W], s1[:, j % 2, P:MASK_W], ACT.Exp, bias=neg_cur[:, j, 1:2],
                               scale=SCALE_A, accum_out=l_cur[:, j, 1:2]).then_inc(p1_ready, 1)

            def q1_turn(i, turn):
                for s in range(UPT):
                    split(turn, s + AHEAD)
                    if s == 0:
                        turn_q1(i)
                    else:
                        attn1(i, s - 1)
                attn1(i, GROUP_A - 1)

            for s in range(UPT):
                split(TURN_Q, s + AHEAD)
                if s == 3:
                    for t in range(T):
                        act.wait_ge(k1_turned, t + 1)
                        act.activation(k1_t[:, :, t * P:t * P + P], two(banks[TURNED + t][:, :], KV_A), ACT.Copy)\
                            .then_inc(k1_ready, 1)
            keep_q1(0, TURN_Q)
            with act.Fori(0, D // CH - 1) as i:
                q1_turn(i, i + TURN_Q + 1)
                keep_q1(i + 1, i + TURN_Q + 1)
            q1_turn(D // CH - 1, TURN_Z)
            act.wait_ge(l1_step, 1)
            act.activation(sink_e[:, :, :], sink_e[:, :, :], ACT.Exp).then_inc(sink_exp, 1)

            def z_sigmoid(c, turn):
                for t in range(T):
                    chunk_result(t, turn, turn)
                    act.wait_ge(og_turned, c * T + t + 1)
                    act.activation(z_silu[:, t, :], pair[PAIR_A][t][:, :], ACT.Sigmoid).then_inc(z_sig, 1)

            def keep_og(c):
                for t in range(T):
                    act.wait_ge(og_turned, c * T + T + t + 1)
                    act.activation(o_gated_t[:, bass.ds(c * 4, 4), t * P:t * P + P], two(banks[TURNED + t][:, :], 4),
                                   ACT.Copy).then_inc(og_ready, 1)

            z_sigmoid(0, TURN_Z)
            with act.Fori(1, D // CH) as c:
                for s in range(UPT):
                    split(c + TURN_Z, s + AHEAD)
                    if s == 4:
                        keep_og(c - 1)
                z_sigmoid(c, c + TURN_Z)
            keep_og(D // CH - 1)
            round_h(o_gated_t, TURN_OUT, og_ready, T * (D // CH))

            with act.Fori(0, 2) as it:
                for b in range(2):
                    for s in range(UPT):
                        split(it * 2 + TURN_OUT + b, s + AHEAD)
                    for t in range(T):
                        square_y(b, t, it * 2 + TURN_OUT + b, it * 2 + TURN_OUT + b,
                                 it * 4 + 2 * b + t + 1, it * 2 + b, sq1)
            norm(1, y1, TURN_KI)

            def keep_turned(count, dst, heads=4):
                for t in range(T):
                    act.wait_ge(i_turned, count + t + 1)
                    act.activation(dst[:, :, t * P:t * P + P], two(banks[TURNED + t][:, 0:heads * P], heads), ACT.Copy)\
                        .then_inc(i_t_ready, 1)

            def index_relu(h):
                act.wait_ge(i_scores, h + 1)
                if h >= 2:
                    act.wait_ge(i_added, h - 1)
                act.activation(s2[:, h % 2, :], banks[SCORES + h % 2][:, 0:MASK_W], ACT.Relu).then_inc(i_relu, 1)

            ki_t = v2[:, 0:1, 0:SEQ]
            for s in range(UPT):
                split(TURN_KI, s + AHEAD)
            for s in range(UPT):
                split(TURN_QI, s + AHEAD)
                if s == 5:
                    keep_turned(0, ki_t, 1)
            for s in range(UPT):
                split(TURN_QI + 1, s + AHEAD)
                if s == 5:
                    keep_turned(T, q2_t)

            INDEX_AT = {1: (0, 1, 2), 2: (3, 4, 5), 3: (6, 7), 5: (8, 9, 10), 6: (11, 12, 13), 7: (14, 15)}

            def keep_qk(n, dst):
                for t in range(T):
                    act.wait_ge(qk_turned, n * T + t + 1)
                    act.activation(dst[:, :, t * P:t * P + P], two(banks[TURNED + t][:, :], 4), ACT.Copy)\
                        .then_inc(qk_ready, 1)

            def attn2(g, k):
                if 1 <= k <= 4:
                    act.wait_ge(p2_turned, g * 4 + k)
                    act.activation(p2_t[:, :], banks[TURNED][:, 0:MASK_W], ACT.Copy).then_inc(p2_t_ready, 1)
                if k < 4:
                    act.wait_ge(neg2_ready, g * 4 + k + 1)
                    act.activation(s2[:, k % 2, 0:P], s2[:, k % 2, 0:P], ACT.Exp, bias=m2[:, k % 2, 0:1], scale=SCALE_2,
                                   accum_out=l2[:, k % 2, 0:1])
                    act.activation(s2[:, k % 2, P:MASK_W], s2[:, k % 2, P:MASK_W], ACT.Exp, bias=m2[:, k % 2, 1:2],
                                   scale=SCALE_2, accum_out=l2[:, k % 2, 1:2]).then_inc(p2_ready, 1)
                if k >= 2:
                    act.wait_ge(o2_ready, g * 4 + k - 1)
                    act.activation(o_hi[:, bass.ds(g * 4 + k - 2, 1), :], banks[OUTS][:, 0:SEQ].unsqueeze(1), ACT.Copy)\
                        .then_inc(o2_hi, 1)

            def group_rest(g):
                for s in range(UPT):
                    split(g * 3 + TURN_GRP + 1, s + AHEAD)
                    if s == 4:
                        keep_qk(g * 2, q2_t)
                for s in range(UPT):
                    split(g * 3 + TURN_GRP + 2, s + AHEAD)
                    if s == 4:
                        keep_qk(g * 2 + 1, k2_t)
                for t in range(T):
                    chunk_result(t, g * 3 + TURN_GRP + 2, g * 3 + TURN_GRP + 2)
                    act.activation(v2[:, t, :], pair[PAIR_B][t][:, :], ACT.Copy).then_inc(evicted[PAIR_B][t], 1)

            def attn2_turn(g, turn):
                for s in range(UPT):
                    split(turn, s + AHEAD)
                    if 1 <= s <= 6:
                        attn2(g, s - 1)

            for s in range(UPT):
                split(TURN_GRP, s + AHEAD)
                if s == 4:
                    keep_turned(2 * T, k2_t)
                for h in INDEX_AT.get(s, ()):
                    index_relu(h)
            group_rest(0)
            with act.Fori(1, 4) as g:
                attn2_turn(g - 1, g * 3 + TURN_GRP)
                group_rest(g)

            def keep_gate(n, c, turn, chunk):
                dst = (gate_a, gate_b)[n]
                for t in range(T):
                    chunk_result(t, turn, chunk)
                    act.wait_ge(y_tok_ready, c * T + t + 1)
                    act.activation(dst[:, t, :], pair[n][t][:, :], ACT.Sigmoid).then_inc(evicted[n][t], 1)

            def keep_y(c):
                for t in range(T):
                    act.wait_ge(y_turned, c * T + T + t + 1)
                    act.activation(y_t[:, bass.ds(c * 4, 4), t * P:t * P + P], two(banks[TURNED + t][:, :], 4), ACT.Copy)\
                        .then_inc(y_t_ready, 1)

            attn2_turn(3, TURN_GATE)
            act.wait_ge(o2_kept, 2 * HEADS_2 + 1)
            keep_gate(0, 0, TURN_GATE, CHUNK_GATE)
            for s in range(UPT):
                split(TURN_GATE + 1, s + AHEAD)
            keep_gate(1, 0, TURN_GATE + 1, CHUNK_GATE + 1)
            with act.Fori(0, D // CH - 1) as c:
                for s in range(UPT):
                    split(c * 3 + TURN_YAB, s + AHEAD)
                for s in range(UPT):
                    split(c * 3 + TURN_YAB + 1, s + AHEAD)
                    if s == 4:
                        keep_y(c)
                keep_gate(0, c + 1, c * 3 + TURN_YAB + 1, c * 4 + CHUNK_YAB + 2)
                for s in range(UPT):
                    split(c * 3 + TURN_YAB + 2, s + AHEAD)
                keep_gate(1, c + 1, c * 3 + TURN_YAB + 2, c * 4 + CHUNK_YAB + 3)
            for s in range(UPT):
                split(TURN_YAB + 9, s + AHEAD)
            keep_y(D // CH - 1)
            round_h(y_t, TURN_WO, y_t_ready, T * (D // CH))

            with act.Fori(0, 2) as it:
                for b in range(2):
                    for s in range(UPT):
                        split(it * 2 + TURN_WO + b, s + AHEAD)
                    for t in range(T):
                        square_y(b, t, it * 2 + TURN_WO + b, it * 2 + CHUNK_WO + b,
                                 it * 4 + 2 * b + t + 9, it * 2 + b, sq2)
            norm(2, y2, TURN_FF1)

            def relu(p, c, turn):
                for t in range(T):
                    chunk_result(t, turn, c + CHUNK_FF1)
                    act.wait_ge(f_turned, c * T + t + 1)
                    act.activation(f_tok[:, t, :], pair[p][t][:, :], ACT.Relu).then_inc(evicted[p][t], 1)

            def keep_f(c):
                act.wait_ge(f_turned, c * T + 1 + T)
                act.activation(f_t[:, bass.ds(c * 4, 4), 0:P], two(banks[TURNED][:, :], 4), ACT.Copy)\
                    .then_inc(f_t_ready[0], 1)

            def ff1_turn(c):
                for s in range(UPT):
                    split(c + TURN_FF1, s + AHEAD)
                    if s == 4:
                        keep_f(c - 1)

            for s in range(UPT):
                split(TURN_FF1, s + AHEAD)
            relu(PAIR_A, 0, TURN_FF1)
            with act.Fori(0, 7) as it:
                for b in range(2):
                    ff1_turn(it * 2 + 1 + b)
                    relu(1 - b, it * 2 + 1 + b, it * 2 + 1 + b + TURN_FF1)
            ff1_turn(15)
            relu(PAIR_B, 15, TURN_FF1 + 15)
            keep_f(15)

            def round_f(c, b):
                act.wait_ge(mm_done, TURN_FF2 * UPT if isinstance(c, int) and c == 0 else (c + TURN_FF2 - 1) * UPT)
                act.activation(h_hi[:, 4 * b:4 * b + 4, :], f_t[:, bass.ds(c * 4, 4), :], ACT.Copy)\
                    .then_inc(f_hi_ready, 1)

            for t in range(T):
                act.wait_ge(f_t_ready[t], D_FF // CH)
            round_f(0, 0)

            def ff2_turn(c, b, last=False):
                for s in range(UPT):
                    if not last or s + AHEAD < UPT:
                        split(c + TURN_FF2, s + AHEAD)
                    if s == 4 and not last:
                        round_f(c + 1, 1 - b)

            with act.Fori(0, 7) as it:
                for b in range(2):
                    ff2_turn(it * 2 + b, b)
            ff2_turn(14, 0)
            ff2_turn(15, 1, last=True)
            act.wait_ge(mm_done, TURNS * UPT)
            for t in range(T):
                for c in range(D // CH):
                    act.wait_ge(y_squared, 17 + t * 4 + c)
                    act.activation(f_tok[:, 0, :], banks[t * 4 + c][:, :], ACT.Square, accum_out=y_sq[:, t, c:c + 1])\
                        .then_inc(y_squared, 1)
            act.wait_ge(y_stat, 6)
            act.activation(y_rstd[:, :], y_var[:, :], ACT.Sqrt).then_inc(y_root, 1)

        @block.vector
        def _(dve):
            def split(turn, s):
                turn, s = turn + s // UPT, s % UPT
                dve.wait_ge(hi_ready, unit_of(turn, s) + 1)
                dve.tensor_tensor(w_lo[:, s % SLOTS, :], raw[:, s % SLOTS, :], w_hi[:, s % SLOTS, :].bitcast(F32),
                                  ALU.subtract).then_inc(lo_ready, 1)

            def add_ada(m, slot, acc, k, half, loads):
                dve.wait_ge(ada_loaded[slot], loads)
                dve.wait_ge(ada_done, m - 1)
                part = acc[:, half * (D // 2):(half + 1) * (D // 2)]
                dve.scalar_tensor_tensor(part, ada_raw[:, slot, :], cond[:, bass.ds(k, 1)], part, ALU.mult, ALU.add)\
                    .then_inc(ada_done, 1)

            def ada(m, n, acc, k):
                add_ada(m + n, n % 2, acc, k, n % 2, (m + n - n % 2) * 8 + 16)

            def add_residual(r, y):
                dve.wait_ge(y_root, 2 * r)
                for t in range(T):
                    dve.scalar_tensor_tensor(x[:, t, :], y[:, t, :], y_rstd[:, t:t + 1], x[:, t, :], ALU.mult, ALU.add)\
                        .then_inc(x_new, 1)

            def norm(r, y, gain, shift):
                if r:
                    dve.wait_ge(y_squared, 8 * r + 1)
                    dve.tensor_reduce(y_var[:, :], y_sq[:, :, :], AX.X, ALU.add).then_inc(y_stat, 1)
                    dve.wait_ge(y_stat, 2 * r - 1)
                    dve.tensor_scalar(y_var[:, :], y_var[:, :], 1.0 / D, EPS, ALU.mult, ALU.add).then_inc(y_stat, 1)
                    dve.wait_ge(y_root, 2 * r - 1)
                    dve.reciprocal(y_rstd[:, :], y_rstd[:, :]).then_inc(y_root, 1)
                    add_residual(r, y)
                dve.wait_ge(x_squared, T * (r + 1))
                dve.tensor_scalar(x_sq[:, :], x_sq[:, :], 1.0 / D, EPS, ALU.mult, ALU.add).then_inc(x_stat, 1)
                dve.wait_ge(x_root, r + 1)
                dve.reciprocal(x_rstd[:, :], x_rstd[:, :]).then_inc(x_stat, 1)
                dve.wait_ge(x_stat, 2 * r + 2)
                dve.tensor_scalar(y[:, 1, :], x[:, 1, :], x_rstd[:, 1:2], None, ALU.mult).then_inc(x_norm[1], 1)
                if r:
                    dve.wait_ge(mod_ready, 2 * r)
                else:
                    dve.wait_ge(vecs_loaded, 16)

                def low(s):
                    dve.wait_ge(h_hi_ready, 2 * UPT * r + s + 1)
                    dve.tensor_tensor(h_lo[:, KG * s:KG * s + KG, :], two(norm_tmp[:, s % 2, :]),
                                      h_hi[:, KG * s:KG * s + KG, :].bitcast(F32), ALU.subtract)\
                        .then_inc(h_lo_ready, 1)

                for s in range(UPT):
                    dve.wait_ge(n_turned, UPT * r + s + 1)
                    if s >= 2:
                        dve.wait_ge(h_lo_ready, 2 * UPT * r + s - 1)
                    for kk in range(KG):
                        k = KG * s + kk
                        ins = dve.tensor_scalar(norm_tmp[:, s % 2, kk * SEQ:(kk + 1) * SEQ],
                                                banks[SCORES + s % 4][:, kk * SEQ:(kk + 1) * SEQ],
                                                gain[:, k:k + 1], shift[:, k:k + 1] if r else 1.0,
                                                ALU.mult, ALU.add if r else ALU.mult)
                    ins.then_inc(n_scaled, 1)
                    if s:
                        low(s - 1)
                low(UPT - 1)

            def low_h(src, done):
                for s in range(UPT):
                    dve.wait_ge(h_hi_ready, done + s + 1)
                    dve.tensor_tensor(h_lo[:, KG * s:KG * s + KG, :], src[:, KG * s:KG * s + KG, :],
                                      h_hi[:, KG * s:KG * s + KG, :].bitcast(F32), ALU.subtract)\
                        .then_inc(h_lo_ready, 1)

            def read_mods(n, gain_vec):
                dve.wait_ge(mod_cols, n + 1)
                dve.scalar_tensor_tensor(pre_gain[:, :], banks[OUTS][:, 0:KT], 1.0, vecs[:, gain_vec:gain_vec + KT],
                                         ALU.add, ALU.mult).then_inc(mod_ready, 1)
                dve.tensor_copy(pre_shift[:, :], banks[OUTS][:, KT:2 * KT]).then_inc(mod_ready, 1)

            def gate_gain(n):
                dve.wait_ge(gain_loaded[n + 1], 16)
                for q in range(4):
                    dve.wait_ge(mod_rows, 4 * n + q + 1)
                    part = post_gain[:, q * CH:(q + 1) * CH]
                    dve.tensor_tensor(part, banks[SCORES + q][:, :], part, ALU.mult).then_inc(gain_ready, 1)

            def chunk_result(t, turn, chunk):
                if t == 0:
                    dve.wait_ge(front_done, chunk + 1)
                else:
                    dve.wait_ge(mm_done, unit_of(turn, UPT))

            def scale_y(p, t, n, col, y):
                dve.wait_ge(y_squared, n)
                dve.tensor_tensor(y[:, t, bass.ds(col * CH, CH)], pair[p][t][:, :], post_gain[:, bass.ds(col * CH, CH)],
                                  ALU.mult).then_inc(evicted[p][t], 1)

            dve.sem_inc(s1_masked, 2)
            dve.sem_inc(o1_kept, 1)
            dve.sem_inc(y_tok_ready, T)
            dve.sem_inc(o2_kept, 1)
            dve.wait_ge(cond_sig, 1)
            dve.tensor_tensor(cond[:, :], cond[:, :], vecs[:, V_C:V_C + KT], ALU.mult).then_inc(cond_ready, 1)
            norm(0, y1, vecs[:, V_PRE:V_PRE + KT], None)
            for s in range(AHEAD):
                split(TURN_KV, s)
            dve.wait_ge(cond_ready, 1)
            for n in range(2):
                dve.wait_ge(acc_init[n], 16)
            for s in range(UPT):
                split(TURN_KV, s + AHEAD)
                if s < 2:
                    dve.wait_ge(ada_loaded[s], 16)
                    part = acc_a[:, s * (D // 2):(s + 1) * (D // 2)]
                    dve.scalar_tensor_tensor(part, ada_raw[:, s, :], cond[:, 0:1], part, ALU.mult, ALU.add)\
                        .then_inc(ada_done, 1)
                else:
                    ada(0, s, acc_a, s // 2)
            dve.wait_ge(sink_loaded, 16)
            dve.tensor_scalar(sink_sc[:, :], sink[:, :], 1.0 / SCALE_A, None, ALU.mult).then_inc(sink_scaled, 1)
            dve.wait_ge(consts_loaded, 16)
            dve.wait_ge(sink_scaled, 1)

            def set_heads(i):
                dve.tensor_copy(slope_cur[:, :], consts[:, bass.ds(i * GROUP_A + C_SLOPE, GROUP_A)])
                dve.tensor_copy(sink_cur[:, :], sink_sc[:, bass.ds(i * GROUP_A, GROUP_A)]).then_inc(heads_cur, 1)

            def attn1_scores(i, j):
                h = i * GROUP_A + j
                dve.wait_ge(bias_ready, h + 1)
                dve.wait_ge(s1_ready, h + 1)
                if j == 0:
                    dve.wait_ge(heads_cur, i + 1)
                dve.sem_inc(s1_seen, 1)
                for t, (c0, c1) in enumerate(((0, P), (P, MASK_W))):
                    ins = dve.tensor_tensor_reduce(s1[:, j % 2, c0:c1], banks[SCORES + j % 2][:, c0:c1],
                                                   bias1[:, j % 2, c0:c1], 1.0, LOWEST, ALU.add, ALU.max,
                                                   m1[:, j % 2, t:t + 1])
                ins.then_inc(s1_masked, 1)
                dve.wait_ge(s1_masked, h + 3)
                dve.tensor_scalar(neg_cur[:, j, :], m1[:, j % 2, :], sink_cur[:, j:j + 1], -SCALE_A, ALU.max, ALU.mult)\
                    .then_inc(neg1_ready, 1)

            def attn1_turned(i, j):
                dve.wait_ge(p1_turned, i * GROUP_A + j + 1)
                dve.tensor_copy(p1_t[:, :], banks[TURNED][:, 0:MASK_W]).then_inc(p1_t_ready, 1)

            def attn1_out(i, b):
                dve.wait_ge(o1_ready, i * 2 + b + 1)
                dve.tensor_copy(o[:, :, bass.ds(i * CH + b * (CH // 2), CH // 2)], two(banks[OUTS][:, :]))\
                    .then_inc(o1_kept, 1)

            def attn1(i, k):
                if k == 6:
                    attn1_out(i, 0)
                if k < GROUP_A:
                    attn1_scores(i, k)
                if 1 <= k <= GROUP_A:
                    attn1_turned(i, k - 1)
                if k == GROUP_A + 1:
                    attn1_out(i, 1)

            def keep_stats(i):
                dve.wait_ge(p1_ready, i * GROUP_A + GROUP_A)
                dve.tensor_copy(neg_m1[:, :, bass.ds(i * GROUP_A, GROUP_A)], neg_cur[:, :, :].rearrange("p j t -> p t j"))
                dve.tensor_copy(l1[:, :, bass.ds(i * GROUP_A, GROUP_A)], l_cur[:, :, :].rearrange("p j t -> p t j"))\
                    .then_inc(stats_kept, 1)

            set_heads(0)
            for s in range(UPT):
                split(TURN_Q, s + AHEAD)
                ada(8, s, acc_a, 4 + s // 2)
            with dve.Fori(0, D // CH - 1) as i:
                for s in range(UPT):
                    split(i + TURN_Q + 1, s + AHEAD)
                    if s:
                        attn1(i, s - 1)
                for k in range(UPT - 1, GROUP_A + 2):
                    attn1(i, k)
                keep_stats(i)
                set_heads(i + 1)
            last = D // CH - 1
            for s in range(UPT):
                split(TURN_Z, s + AHEAD)
                if s:
                    attn1(last, s - 1)
                if s < UPT - 1:
                    ada(16, s, acc_a, 8 + s // 2)
            for k in range(UPT - 1, GROUP_A + 2):
                attn1(last, k)
            ada(16, UPT - 1, acc_a, 8 + (UPT - 1) // 2)
            keep_stats(last)
            dve.wait_ge(stats_kept, D // CH)
            dve.tensor_tensor(sink_e[:, :, :], neg_m1[:, :, :], sink[:, :].unsqueeze(1).to_broadcast([P, T, HEADS_A]),
                              ALU.add).then_inc(l1_step, 1)
            dve.wait_ge(sink_exp, 1)
            dve.tensor_tensor(l1[:, :, :], l1[:, :, :], sink_e[:, :, :], ALU.add).then_inc(l1_step, 1)
            dve.wait_ge(l1_step, 2)
            dve.reciprocal(l1[:, :, :], l1[:, :, :]).then_inc(l1_step, 1)
            dve.wait_ge(l1_step, 3)

            def gate_o(c):
                for t in range(T):
                    dve.wait_ge(z_sig, c * T + t + 1)
                    dve.tensor_tensor(z_silu[:, t, :], pair[PAIR_A][t][:, :], z_silu[:, t, :], ALU.mult)\
                        .then_inc(evicted[PAIR_A][t], 1)
                    part = o[:, t, bass.ds(c * CH, CH)].rearrange("p (j d) -> p j d", d=DH_A)
                    inv = l1[:, t, bass.ds(c * GROUP_A, GROUP_A)].unsqueeze(2).to_broadcast([P, GROUP_A, DH_A])
                    dve.tensor_tensor(part, part, inv, ALU.mult).then_inc(o_step, 1)
                for t in range(T):
                    dve.wait_ge(o_step, c * T + t + 1)
                    dve.wait_ge(evicted[PAIR_A][t], c + 2)
                    dve.tensor_tensor(z_silu[:, t, :], o[:, t, bass.ds(c * CH, CH)], z_silu[:, t, :], ALU.mult)\
                        .then_inc(o_gated, 1)

            dve.wait_ge(o1_kept, 2 * (D // CH) + 1)
            gate_o(0)
            with dve.Fori(1, D // CH) as c:
                for s in range(UPT):
                    split(c + TURN_Z, s + AHEAD)
                    ada(c * 8 + 16, s, acc_b, c * 4 - 4 + s // 2)
                gate_o(c)
            low_h(o_gated_t, H_OUT)

            dve.wait_ge(gain_loaded[0], 16)
            with dve.Fori(0, 2) as it:
                for b in range(2):
                    for s in range(UPT):
                        split(it * 2 + TURN_OUT + b, s + AHEAD)
                        if s % 2:
                            n = 4 * b + s // 2
                            ada(it * 8 + 48, n, (acc_a, acc_b)[b], it * 2 + 12 + n // 2 % 2)
                    for t in range(T):
                        scale_y(b, t, it * 4 + 2 * b + t + 2, it * 2 + b, y1)
            for p in range(2):
                for t in range(T):
                    dve.wait_ge(evicted[p][t], 7 - p)
            read_mods(0, V_MIX)
            norm(1, y1, pre_gain, pre_shift)

            def rope(src, dst, p, t, use, n, heads, half, cos0, sin0, copies=1):
                cols = heads * 2 * half
                cos = consts[:, cos0 + t * half:cos0 + (t + 1) * half]
                sin = consts[:, sin0 + t * half:sin0 + (t + 1) * half]
                xin = src.rearrange("p (h r d) -> p h r d", h=heads, r=2)
                ra = rope_a[:, 0:cols].rearrange("p (h r d) -> p h r d", h=heads, r=2)
                rb = rope_b[:, 0:cols].rearrange("p (h r d) -> p h r d", h=heads, r=2)

                def wide(tab):
                    return tab.unsqueeze(1).to_broadcast([P, heads, half])

                if not (isinstance(n, int) and n + t == 0):
                    dve.wait_ge(rot_ready, n * T + t)
                for r in range(2):
                    dve.tensor_tensor(ra[:, :, r, :], xin[:, :, r, :], wide(cos), ALU.mult)
                for r in range(2):
                    ins = dve.tensor_tensor(rb[:, :, r, :], xin[:, :, 1 - r, :], wide(sin), ALU.mult)
                ins.then_inc(evicted[p][t], 1)
                dve.wait_ge(evicted[p][t], use + 1)
                rows = dst.rearrange("p (h r d) -> p h r d", h=heads * copies, r=2)
                for c in range(copies):
                    for r in range(2):
                        ins = dve.tensor_tensor(rows[:, c * heads:(c + 1) * heads, r, :], ra[:, :, r, :], rb[:, :, r, :],
                                                (ALU.subtract, ALU.add)[r])
                ins.then_inc(rot_ready, 1)

            def index_add(h):
                dve.wait_ge(i_relu, h + 1)
                if h:
                    dve.wait_ge(i_added, h)
                for t, (c0, c1) in enumerate(((0, P), (P, MASK_W))):
                    base = (score if h else causal)[:, c0:c1]
                    ins = dve.scalar_tensor_tensor(score[:, c0:c1], s2[:, h % 2, c0:c1], w_idx[:, t, h:h + 1], base,
                                                   ALU.mult, ALU.add)
                ins.then_inc(i_added, 1)

            def top_round(r):
                if r:
                    dve.wait_ge(top_step, 2 * r)
                for t, (c0, c1) in enumerate(((0, P), (P, MASK_W))):
                    ins = dve.max(top8[:, t, :], score[:, c0:c1])
                ins.then_inc(top_step, 1)
                dve.wait_ge(top_step, 2 * r + 1)
                for t, (c0, c1) in enumerate(((0, P), (P, MASK_W))):
                    ins = dve.match_replace(score[:, c0:c1], top8[:, t, :], score[:, c0:c1], PICKED)
                ins.then_inc(top_step, 1)

            INDEX_AT = {1: (0, 1, 2), 2: (3, 4, 5), 3: (6, 7), 5: (8, 9, 10), 6: (11, 12, 13), 7: (14, 15)}

            for s in range(UPT):
                split(TURN_KI, s + AHEAD)
            for t in range(T):
                chunk_result(t, TURN_KI, TURN_KI)
                ki = pair[PAIR_A][t]
                dve.tensor_scalar(w_idx[:, t, :], ki[:, IDX_DIM:KI_COLS], IDX_SCALE, None, ALU.mult)\
                    .then_inc(w_idx_ready, 1)
                rope(ki[:, 0:IDX_DIM], rot[:, t, 0:2 * IDX_DIM], PAIR_A, t, 7, 0, 1, IDX_DIM // 2, C_COSI, C_SINI, 2)
            for c in range(2):
                for s in range(UPT):
                    split(TURN_QI + c, s + AHEAD)
                dve.wait_ge(i_turned, T * c + T)
                for t in range(T):
                    chunk_result(t, TURN_QI + c, TURN_QI + c)
                    rope(pair[1 - c][t][:, :], rot[:, t, :], 1 - c, t, 6 + 2 * c, 1 + c, CH // IDX_DIM,
                         IDX_DIM // 2, C_COSI, C_SINI)
            dve.wait_ge(w_idx_ready, T)

            def rope_chunk(p, turn, use, n):
                for t in range(T):
                    chunk_result(t, turn, turn)
                    rope(pair[p][t][:, :], rot[:, t, :], p, t, use, n, 4, DH_2 // 2, C_COS, C_SIN)

            def attn2(g, k):
                h = g * 4 + k
                if 1 <= k <= 4:
                    b = (k - 1) % 2
                    dve.wait_ge(p2_ready, h)
                    dve.reciprocal(l2_inv[:, :], l2[:, b, :]).then_inc(l2_ready, 1)
                    dve.wait_ge(l2_ready, h)
                    dve.tensor_scalar(s2[:, b, 0:P], s2[:, b, 0:P], l2_inv[:, 0:1], None, ALU.mult)
                    dve.tensor_scalar(s2[:, b, P:MASK_W], s2[:, b, P:MASK_W], l2_inv[:, 1:2], None, ALU.mult)\
                        .then_inc(p2_normed, 1)
                if k < 4:
                    dve.wait_ge(s2_ready, h + 1)
                    if k == 0:
                        dve.wait_ge(mask_set, g + 1)
                    dve.sem_inc(s2_seen, 1)
                    for t, (c0, c1) in enumerate(((0, P), (P, MASK_W))):
                        ins = dve.tensor_tensor_reduce(s2[:, k % 2, c0:c1], banks[SCORES + k % 2][:, c0:c1],
                                                       mask_cur[:, c0:c1], 1.0, LOWEST, ALU.add, ALU.max,
                                                       m2[:, k % 2, t:t + 1])
                    ins.then_inc(s2_masked, 1)
                    dve.wait_ge(s2_masked, h + 1)
                    dve.tensor_scalar(m2[:, k % 2, :], m2[:, k % 2, :], -SCALE_2, None, ALU.mult).then_inc(neg2_ready, 1)
                if k >= 2:
                    dve.wait_ge(o2_hi, h - 1)
                    dve.tensor_tensor(o_lo[:, bass.ds(h - 2, 1), :], banks[OUTS][:, 0:SEQ].unsqueeze(1),
                                      o_hi[:, bass.ds(h - 2, 1), :].bitcast(F32), ALU.subtract).then_inc(o2_kept, 1)

            def group_rest(g, with_top=False):
                if with_top:
                    dve.wait_ge(i_turned, 3 * T)
                else:
                    dve.wait_ge(qk_turned, g * 2 * T)
                rope_chunk(PAIR_B, g * 3 + TURN_GRP, g * 2 + 7, g * 2 + 3)
                for s in range(UPT):
                    split(g * 3 + TURN_GRP + 1, s + AHEAD)
                    if with_top and s % 2 == 0:
                        top_round(s // 2)
                    if s % 2:
                        ada(g * 8 + 64, s // 2, acc_a, g * 4 + s // 4)
                dve.wait_ge(qk_turned, g * 2 * T + T)
                rope_chunk(PAIR_A, g * 3 + TURN_GRP + 1, g + 9, g * 2 + 4)
                for s in range(UPT):
                    split(g * 3 + TURN_GRP + 2, s + AHEAD)
                    if with_top and s % 2 == 0:
                        top_round(4 + s // 2)
                    if s % 2:
                        ada(g * 8 + 64, 4 + s // 2, acc_a, g * 4 + 2 + s // 4)

            def attn2_turn(g, turn):
                for s in range(UPT):
                    split(turn, s + AHEAD)
                    if s == 0:
                        dve.tensor_copy(mask_cur[:, :], masks[:, bass.ds(dve.snap(g >> 1, min_val=0, max_val=1), 1), :]
                                        if not isinstance(g, int) else masks[:, g // 2, :]).then_inc(mask_set, 1)
                    if 1 <= s <= 6:
                        attn2(g, s - 1)

            for s in range(UPT):
                split(TURN_GRP, s + AHEAD)
                for h in INDEX_AT.get(s, ()):
                    index_add(h)
            dve.wait_ge(acc_init[2], 16)
            dve.wait_ge(i_added, IDX_HEADS)
            dve.tensor_copy(masks[:, 0, :], causal).then_inc(mask_ready, 1)
            group_rest(0, with_top=True)
            dve.wait_ge(top_step, TOPK // 4)
            dve.tensor_scalar(score[:, :], score[:, :], PICKED_BELOW, MASKED, ALU.is_gt, ALU.mult).then_inc(mask_ready, 1)
            dve.wait_ge(mask_ready, 2)
            dve.tensor_tensor(masks[:, 1, :], score[:, :], causal, ALU.add).then_inc(mask_ready, 1)
            dve.wait_ge(mask_ready, 3)
            with dve.Fori(1, 4) as g:
                attn2_turn(g - 1, g * 3 + TURN_GRP)
                group_rest(g)

            gate_gain(0)
            attn2_turn(3, TURN_GATE)
            for n in (3, 4):
                dve.wait_ge(acc_init[n], 16)

            def ada16(c, s):
                n = s % 8
                ada(c * 16 + 96 + (s - n), n, (acc_a, acc_b)[s // 8], c * 4 + n // 2)

            for s in range(UPT):
                split(TURN_GATE + 1, s + AHEAD)
                ada16(0, 2 * s)
                ada16(0, 2 * s + 1)

            def gate_y(c):
                for t in range(T):
                    dve.wait_ge(y_turned, c * T + t + 1)
                    dve.wait_ge(evicted[PAIR_A][t], c * 2 + 14)
                    dve.wait_ge(front_done, c * 4 + CHUNK_YAB + 1)
                    if t:
                        dve.wait_ge(mm_done, c * 3 * UPT + TURN_YAB * UPT + UPT // 2)
                    dve.tensor_tensor(y_tok[:, t, :], pair[PAIR_A][t][:, :], gate_a[:, t, :], ALU.mult)\
                        .then_inc(evicted[PAIR_A][t], 1)
                for t in range(T):
                    chunk_result(t, c * 3 + TURN_YAB, c * 4 + CHUNK_YAB + 1)
                    dve.wait_ge(evicted[PAIR_B][t], c * 2 + 16)
                    dve.tensor_tensor(gate_b[:, t, :], pair[PAIR_B][t][:, :], gate_b[:, t, :], ALU.mult)\
                        .then_inc(evicted[PAIR_B][t], 1)
                for t in range(T):
                    dve.wait_ge(evicted[PAIR_A][t], c * 2 + 15)
                    dve.wait_ge(evicted[PAIR_B][t], c * 2 + 17)
                    dve.tensor_tensor(y_tok[:, t, :], y_tok[:, t, :], gate_b[:, t, :], ALU.add).then_inc(y_tok_ready, 1)

            with dve.Fori(0, D // CH - 1) as c:
                for s in range(UPT):
                    split(c * 3 + TURN_YAB, s + AHEAD)
                gate_y(c)
                for part in range(2):
                    for s in range(UPT):
                        split(c * 3 + TURN_YAB + 1 + part, s + AHEAD)
                        ada16(c + 1, part * 8 + s)
            for s in range(UPT):
                split(TURN_YAB + 9, s + AHEAD)
            gate_y(D // CH - 1)
            low_h(y_t, H_WO)

            dve.wait_ge(gain_ready, 4)
            with dve.Fori(0, 2) as it:
                for b in range(2):
                    for s in range(UPT):
                        split(it * 2 + TURN_WO + b, s + AHEAD)
                    for t in range(T):
                        scale_y(b, t, it * 4 + 2 * b + t + 10, it * 2 + b, y2)
            for p in range(2):
                for t in range(T):
                    dve.wait_ge(evicted[p][t], 23 + 2 * p)
            read_mods(1, V_FFN)
            norm(2, y2, pre_gain, pre_shift)

            def square(p, use):
                for t in range(T):
                    dve.wait_ge(evicted[p][t], use + 1)
                    dve.tensor_tensor(f_tok[:, t, :], f_tok[:, t, :], f_tok[:, t, :], ALU.mult).then_inc(f_sq, 1)

            def keep_f(c):
                dve.wait_ge(f_turned, c * T + 2 + T)
                dve.tensor_copy(f_t[:, bass.ds(c * 4, 4), P:SEQ], two(banks[OUTS][:, :], 4)).then_inc(f_t_ready[1], 1)

            dve.wait_ge(acc_init[5], 16)
            for s in range(UPT):
                split(TURN_FF1, s + AHEAD)
            square(PAIR_A, 23)

            with dve.Fori(0, 7) as it:
                for b in range(2):
                    for s in range(UPT):
                        split(it * 2 + 1 + b + TURN_FF1, s + AHEAD)
                        if s == 4:
                            keep_f(it * 2 + b)
                        if s in (1, 6):
                            n = 2 * b + s // 6
                            ada(it * 4 + 160, n, acc_a, it * 2 + b)
                    square(1 - b, it + 25 - b)
            for s in range(UPT):
                split(TURN_FF1 + 15, s + AHEAD)
                if s == 4:
                    keep_f(14)
                if s in (1, 3, 5, 7):
                    ada(188, s // 2, acc_a, 14 + s // 4)
            square(PAIR_B, 32)
            keep_f(15)
            gate_gain(1)

            def low_f(c, b):
                dve.wait_ge(f_hi_ready, c + 1)
                dve.tensor_tensor(h_lo[:, 4 * b:4 * b + 4, :], f_t[:, bass.ds(c * 4, 4), :],
                                  h_hi[:, 4 * b:4 * b + 4, :].bitcast(F32), ALU.subtract).then_inc(f_lo_ready, 1)

            low_f(0, 0)

            def ff2_turn(c, b, last=False):
                for s in range(UPT):
                    if not last or s + AHEAD < UPT:
                        split(c + TURN_FF2, s + AHEAD)
                    if s == 4 and not last:
                        low_f(c + 1, 1 - b)

            with dve.Fori(0, 7) as it:
                for b in range(2):
                    ff2_turn(it * 2 + b, b)
            ff2_turn(14, 0)
            ff2_turn(15, 1, last=True)
            dve.wait_ge(gain_ready, 8)
            for t in range(T):
                for c in range(D // CH):
                    dve.wait_ge(y_squared, 18 + t * 4 + c)
                    dve.tensor_tensor(y2[:, t, c * CH:(c + 1) * CH], banks[t * 4 + c][:, :],
                                      post_gain[:, c * CH:(c + 1) * CH], ALU.mult).then_inc(y_scaled, 1)
            dve.wait_ge(y_scaled, T * (D // CH))
            dve.tensor_reduce(y_var[:, :], y_sq[:, :, :], AX.X, ALU.add).then_inc(y_stat, 1)
            dve.wait_ge(y_stat, 5)
            dve.tensor_scalar(y_var[:, :], y_var[:, :], 1.0 / D, EPS, ALU.mult, ALU.add).then_inc(y_stat, 1)
            dve.wait_ge(y_root, 5)
            dve.reciprocal(y_rstd[:, :], y_rstd[:, :]).then_inc(y_root, 1)
            add_residual(3, y2)

        @block.tensor
        def _(pe):
            def three(out_ap, hi, lo, rhs_hi, rhs_lo, start, stop):
                pe.matmul(out_ap, hi, rhs_hi, start=start, stop=False)
                pe.matmul(out_ap, hi, rhs_lo, start=False, stop=False)
                return pe.matmul(out_ap, lo, rhs_hi, start=False, stop=stop)

            def unit(turn, s, hi, lo, k0, p, use, first, last, cols=CH):
                pe.wait_ge(lo_ready, unit_of(turn, s) + 1)
                for t in range(T):
                    if first and not (isinstance(use, int) and use == 0):
                        pe.wait_ge(evicted[p][t], use)
                    for kk in range(KG):
                        w = slice(kk * CH, kk * CH + cols)
                        mm = three(pair[p][t][:, 0:cols], hi[:, k0 + kk, t * P:(t + 1) * P],
                                   lo[:, k0 + kk, t * P:(t + 1) * P], w_hi[:, s % SLOTS, w], w_lo[:, s % SLOTS, w],
                                   first and kk == 0, last and kk == KG - 1)
                    if last and t == 0:
                        mm.then_inc(front_done, 1)
                mm.then_inc(mm_done, 1)

            def chunk_unit(turn, s, p, use, h=None, cols=CH):
                if h is not None:
                    pe.wait_ge(h_lo_ready, h + s + 1)
                unit(turn, s, h_hi, h_lo, KG * s, p, use, s == 0, s == UPT - 1, cols)

            def turn_rows(src, t, n, dst, ready):
                for b in range(n):
                    ins = pe.transpose(dst[:, b * P:(b + 1) * P], src[:, t, b * P:(b + 1) * P], ident)
                ins.then_inc(ready, 1)

            def norm(r, y):
                for t in range(T):
                    pe.wait_ge(x_norm[t], r + 1)
                for s in range(UPT):
                    if s >= 4:
                        pe.wait_ge(n_scaled, UPT * r + s - 3)
                    if r and s == 3:
                        pe.wait_ge(mod_ready, 2 * r)
                    for kk in range(KG):
                        for t in range(T):
                            k = KG * s + kk
                            ins = pe.transpose(banks[SCORES + s % 4][:, kk * SEQ + t * P:kk * SEQ + (t + 1) * P],
                                               y[:, t, k * P:(k + 1) * P], ident)
                    ins.then_inc(n_turned, 1)

            def columns(units):
                pe.wait_ge(ada_done, units)
                for a, acc in enumerate((acc_a, acc_b)):
                    for k in range(KT):
                        ins = pe.matmul(banks[OUTS][:, a * KT + k:a * KT + k + 1], acc[:, k * P:(k + 1) * P],
                                        ones[:, 0:1], start=True, stop=True)
                ins.then_inc(mod_cols, 1)

            def rows(units):
                pe.wait_ge(ada_done, units)
                for q in range(4):
                    pe.matmul(banks[SCORES + q][:, :], ones, acc_a[:, q * CH:(q + 1) * CH], start=True, stop=True)\
                        .then_inc(mod_rows, 1)

            for credit in (og_turned, y_turned, f_turned):
                pe.sem_inc(credit, T)
            pe.wait_ge(consts_loaded, 16)
            norm(0, y1)
            for s in range(UPT):
                chunk_unit(TURN_KV, s, PAIR_A, 0, H_NORM0)
            for s in range(UPT):
                chunk_unit(TURN_Q, s, PAIR_B, 0)
                if s == 2:
                    for t in range(T):
                        pe.wait_ge(kv_tok, t + 1)
                        turn_rows(q1_tok, t, KV_A, banks[TURNED + t], k1_turned)

            def turn_q1(i):
                pe.wait_ge(o1_kept, i * 2 + 1)
                for t in range(T):
                    pe.wait_ge(evicted[PAIR_B][t], i + 1)
                    turn_rows(q1_tok, t, 4, banks[TURNED + t], q1_turned)

            def attn1(i, k):
                if k < GROUP_A:
                    if k == 0:
                        pe.wait_ge(q1_t_ready, i * T + T)
                        pe.wait_ge(kv_cur_ready, i * 2 + 2)
                    lane = slice((k % 2) * DH_A, (k % 2 + 1) * DH_A)
                    q = q1_t[lane, k // 2, :]
                    pe.matmul(banks[SCORES + k % 2][:, 0:P], q[:, 0:P], k1_cur[lane, 0:P], start=True, stop=True)
                    pe.matmul(banks[SCORES + k % 2][:, P:MASK_W], q[:, P:SEQ], k1_cur[lane, :], start=True, stop=True)\
                        .then_inc(s1_ready, 1)
                if k >= 2:
                    j = k - 2
                    pe.wait_ge(p1_t_ready, i * GROUP_A + j + 1)
                    if j % 4 == 0:
                        pe.wait_ge(o1_kept, i * 2 + j // 4 + 1)
                    out0 = banks[OUTS][:, (j % 4) * DH_A:(j % 4 + 1) * DH_A]
                    out1 = banks[OUTS][:, CH // 2 + (j % 4) * DH_A:CH // 2 + (j % 4 + 1) * DH_A]
                    pe.matmul(out0, p1_t[:, 0:P], v1_cur[:, 0, :], start=True, stop=True)
                    pe.matmul(out1, p1_t[:, P:SEQ], v1_cur[:, 0, :], start=True, stop=False)
                    ins = pe.matmul(out1, p1_t[:, SEQ:MASK_W], v1_cur[:, 1, :], start=False, stop=True)
                    if j % 4 == 3:
                        ins.then_inc(o1_ready, 1)
                if 1 <= k <= GROUP_A:
                    pe.wait_ge(p1_ready, i * GROUP_A + k)
                    for b in range(3):
                        ins = pe.transpose(banks[TURNED][:, b * P:(b + 1) * P],
                                           s1[:, (k - 1) % 2, b * P:(b + 1) * P], ident)
                    ins.then_inc(p1_turned, 1)

            def q1_turn(i, turn, p, use, chunk=None):
                for s in range(UPT):
                    chunk_unit(turn, s, p, use)
                    if s == 0:
                        turn_q1(i)
                    else:
                        attn1(i, s - 1)
                for k in range(UPT - 1, GROUP_A + 2):
                    attn1(i, k)

            pe.wait_ge(k1_ready, T)
            with pe.Fori(0, D // CH - 1) as i:
                q1_turn(i, i + TURN_Q + 1, PAIR_B, i + 1)
            q1_turn(D // CH - 1, TURN_Z, PAIR_A, 1)

            def turn_og(c):
                for t in range(T):
                    pe.wait_ge(o_gated, c * T + t + 1)
                    turn_rows(z_silu, t, 4, banks[TURNED + t], og_turned)

            with pe.Fori(1, D // CH) as c:
                for s in range(UPT):
                    chunk_unit(c + TURN_Z, s, PAIR_A, c + 1)
                    if s == 3:
                        turn_og(c - 1)
            turn_og(D // CH - 1)
            with pe.Fori(0, 2) as it:
                for b in range(2):
                    for s in range(UPT):
                        chunk_unit(it * 2 + TURN_OUT + b, s, b, it + 5 - b, H_OUT)
            columns(64)
            norm(1, y1)

            INDEX_AT = {1: (0, 1, 2), 2: (3, 4, 5), 3: (6, 7), 5: (8, 9, 10), 6: (11, 12, 13), 7: (14, 15)}
            ki_t = v2[:, 0:1, 0:SEQ]

            def turn_index(n, blocks):
                for t in range(T):
                    pe.wait_ge(rot_ready, n * T + t + 1)
                    turn_rows(rot, t, blocks, banks[TURNED + t], i_turned)

            def index_scores(h):
                if h >= 2:
                    pe.wait_ge(i_relu, h - 1)
                if h % 8 == 0:
                    pe.wait_ge(i_t_ready, 2 * T + h // 8 * T)
                lane = slice((h % 2) * IDX_DIM, (h % 2 + 1) * IDX_DIM)
                q = (q2_t, k2_t)[h // 8][lane, h // 2 % 4, :]
                keys = ki_t[lane, 0, :]
                pe.matmul(banks[SCORES + h % 2][:, 0:P], q[:, 0:P], keys[:, 0:P], start=True, stop=True)
                pe.matmul(banks[SCORES + h % 2][:, P:MASK_W], q[:, P:SEQ], keys, start=True, stop=True)\
                    .then_inc(i_scores, 1)

            for s in range(UPT):
                chunk_unit(TURN_KI, s, PAIR_A, 7, H_NORM1, KI_COLS)
            for s in range(UPT):
                chunk_unit(TURN_QI, s, PAIR_B, 6)
                if s == 4:
                    turn_index(0, 1)
            for s in range(UPT):
                chunk_unit(TURN_QI + 1, s, PAIR_A, 8)
                if s == 0:
                    pe.wait_ge(i_t_ready, T)
                if s == 4:
                    turn_index(1, 4)

            def turn_qk(n, p, use):
                for t in range(T):
                    pe.wait_ge(rot_ready, (n + 3) * T + t + 1)
                    turn_rows(rot, t, 4, banks[TURNED + t], qk_turned)

            def attn2(g, k):
                h = g * 4 + k
                if k < 4:
                    if k == 0:
                        pe.wait_ge(qk_ready, (g + 1) * 2 * T)
                        for t in range(T):
                            pe.wait_ge(evicted[PAIR_B][t], g * 2 + 9)
                    bank = banks[SCORES + k % 2]
                    pe.matmul(bank[:, 0:P], q2_t[:, k, 0:P], k2_t[:, k, 0:P], start=True, stop=True)
                    pe.matmul(bank[:, P:MASK_W], q2_t[:, k, P:SEQ], k2_t[:, k, :], start=True, stop=True)\
                        .then_inc(s2_ready, 1)
                if k >= 2:
                    pe.wait_ge(p2_t_ready, h - 1)
                    pe.wait_ge(o2_kept, h - 1)
                    head = slice((k - 2) * DH_2, (k - 1) * DH_2)
                    pe.matmul(banks[OUTS][:, 0:SEQ], v2[:, 0, head], p2_t[:, 0:SEQ], start=True, stop=False)
                    pe.matmul(banks[OUTS][:, P:SEQ], v2[:, 1, head], p2_t[:, SEQ:MASK_W], start=False, stop=True)\
                        .then_inc(o2_ready, 1)
                if 1 <= k <= 4:
                    pe.wait_ge(p2_normed, h)
                    for b in range(3):
                        ins = pe.transpose(banks[TURNED][:, b * P:(b + 1) * P], s2[:, (k - 1) % 2, b * P:(b + 1) * P],
                                           ident)
                    ins.then_inc(p2_turned, 1)

            def group_rest(g):
                for s in range(UPT):
                    chunk_unit(g * 3 + TURN_GRP + 1, s, PAIR_A, g + 9)
                    if s == 3:
                        pe.wait_ge(o2_kept, g * 4 + 1)
                        turn_qk(g * 2, PAIR_B, None)
                for s in range(UPT):
                    chunk_unit(g * 3 + TURN_GRP + 2, s, PAIR_B, g * 2 + 8)
                    if s == 3:
                        turn_qk(g * 2 + 1, PAIR_A, None)

            def attn2_turn(g, turn, p, use):
                for s in range(UPT):
                    chunk_unit(turn, s, p, use)
                    if 1 <= s <= 6:
                        attn2(g, s - 1)

            for s in range(UPT):
                chunk_unit(TURN_GRP, s, PAIR_B, 7)
                if s == 3:
                    turn_index(2, 4)
                for h in INDEX_AT.get(s, ()):
                    index_scores(h)
            pe.wait_ge(i_relu, IDX_HEADS)
            group_rest(0)
            with pe.Fori(1, 4) as g:
                attn2_turn(g - 1, g * 3 + TURN_GRP, PAIR_B, g * 2 + 7)
                group_rest(g)

            pe.wait_ge(qk_ready, 8 * T)
            rows(96)
            pe.wait_ge(gain_ready, 4)
            attn2_turn(3, TURN_GATE, PAIR_A, 13)
            for s in range(UPT):
                chunk_unit(TURN_GATE + 1, s, PAIR_B, 15)

            def out_units(c):
                for s in range(UPT):
                    p = s // (UPT // 2)
                    at = s % (UPT // 2)
                    unit(c * 3 + TURN_YAB, s, o_hi, o_lo, KG * s, p, c * 2 + 14 + 2 * p, at == 0, at == UPT // 2 - 1)

            def turn_y(c):
                for t in range(T):
                    pe.wait_ge(y_tok_ready, c * T + T + t + 1)
                    turn_rows(y_tok, t, 4, banks[TURNED + t], y_turned)

            pe.wait_ge(o2_kept, 2 * HEADS_2 + 1)
            with pe.Fori(0, D // CH - 1) as c:
                out_units(c)
                for s in range(UPT):
                    chunk_unit(c * 3 + TURN_YAB + 1, s, PAIR_A, c * 2 + 15)
                    if s == 3:
                        turn_y(c)
                for s in range(UPT):
                    chunk_unit(c * 3 + TURN_YAB + 2, s, PAIR_B, c * 2 + 17)
            out_units(D // CH - 1)
            turn_y(D // CH - 1)
            with pe.Fori(0, 2) as it:
                for b in range(2):
                    for s in range(UPT):
                        chunk_unit(it * 2 + TURN_WO + b, s, b, it + 21 + 2 * b, H_WO)
            columns(160)
            norm(2, y2)

            def turn_f(c):
                for t in range(T):
                    pe.wait_ge(f_sq, c * T + t + 1)
                    turn_rows(f_tok, t, 4, banks[TURNED + t], f_turned)

            def ff1_turn(c, p, use):
                for s in range(UPT):
                    chunk_unit(c + TURN_FF1, s, p, use)
                    if s == 3:
                        turn_f(c - 1)

            for s in range(UPT):
                chunk_unit(TURN_FF1, s, PAIR_A, 23, H_NORM2)
            with pe.Fori(0, 7) as it:
                for b in range(2):
                    ff1_turn(it * 2 + 1 + b, 1 - b, it + 25 - b)
            ff1_turn(15, PAIR_B, 32)
            turn_f(15)
            for t in range(T):
                pe.wait_ge(f_t_ready[t], D_FF // CH)
            rows(192)
            pe.wait_ge(gain_ready, 8)
            for p, uses in ((PAIR_A, 31), (PAIR_B, 33)):
                for t in range(T):
                    pe.wait_ge(evicted[p][t], uses)

            def ff2_turn(c, b, start=False, stop=False):
                pe.wait_ge(f_lo_ready, c + 1)
                for s in range(UPT):
                    pe.wait_ge(lo_ready, unit_of(c + TURN_FF2, s) + 1)
                    k = 4 * b + s // 2
                    for t in range(T):
                        for cc in range(KG):
                            w = slice(cc * CH, (cc + 1) * CH)
                            mm = three(banks[t * 4 + s % 2 * KG + cc][:, :], h_hi[:, k, t * P:(t + 1) * P],
                                       h_lo[:, k, t * P:(t + 1) * P], w_hi[:, s % SLOTS, w], w_lo[:, s % SLOTS, w],
                                       start and s < 2, stop and s >= UPT - 2)
                    mm.then_inc(mm_done, 1)

            ff2_turn(0, 0, start=True)
            ff2_turn(1, 1)
            with pe.Fori(1, 7) as it:
                for b in range(2):
                    ff2_turn(it * 2 + b, b)
            ff2_turn(14, 0)
            ff2_turn(15, 1, stop=True)


_OUT = (1, SEQ, D)


def kernel(x, g_pre, g_post, w_in_a, w_out_a, sinks_a, w_in_b, w_out_b, w_in_c, b_f_c, w_out_c, c_2,
           w_ada_2, b_ada_2, g_pre_mix_2, g_post_mix_2, w_in_2, w_moba_out_2, w_dsa_out_2, w_o_2,
           g_pre_ffn_2, g_post_ffn_2, w_ff1_2, w_ff2_2):
    import concourse.bacc as bacc
    from concourse.bass_utils import run_bass_kernel_spmd

    def columns(v):
        return np.asarray(v).reshape(KT, P).T

    arrays = {
        "x": np.asarray(x)[0],
        "w_in_a": np.asarray(w_in_a)[0],
        "w_out_a": np.asarray(w_out_a)[0],
        "w_ada": np.asarray(w_ada_2)[0],
        "w_in_2": np.asarray(w_in_2)[0],
        "w_moba": np.asarray(w_moba_out_2)[0],
        "w_dsa": np.asarray(w_dsa_out_2)[0],
        "w_o": np.asarray(w_o_2)[0],
        "w_ff1": np.asarray(w_ff1_2)[0],
        "w_ff2": np.asarray(w_ff2_2)[0],
        "b_ada": np.asarray(b_ada_2),
        "g_post": np.asarray(g_post)[0],
        "g_post_mix": np.asarray(g_post_mix_2)[0],
        "g_post_ffn": np.asarray(g_post_ffn_2)[0],
        "sinks": np.asarray(sinks_a)[0],
        "vecs": np.concatenate([columns(v) for v in (g_pre, g_pre_mix_2, g_pre_ffn_2, c_2)], axis=1),
        "consts": shape_constants(),
    }
    arrays = {n: np.ascontiguousarray(a) for n, a in arrays.items()}
    nc = bacc.Bacc("TRN2", target_bir_lowering=False, num_devices=1)
    args = [nc.dram_tensor("in_" + n, a.shape, F32, kind="ExternalInput").ap() for n, a in arrays.items()]
    out = nc.dram_tensor("out", (SEQ, D), F32, kind="ExternalOutput").ap()
    two_block_kernel(nc, *args, out)
    got = run_bass_kernel_spmd(nc, [{"in_" + n: a for n, a in arrays.items()}], core_ids=[0]).results[0]["out"]
    return got.reshape(_OUT)
```

```python
from contextlib import ExitStack

import numpy as np

import concourse.bass as bass
from concourse import mybir

F32 = mybir.dt.float32
F32R = mybir.dt.float32r
ALU = mybir.AluOpType
ACT = mybir.ActivationFunctionType
AX = mybir.AxisListType

P = 128
D = 2048
SEQ = 256
T = SEQ // P
KT = D // P
CH = 512
KG = 2
UNIT = KG * CH
SLOTS = 4
UPT = KT // KG
AHEAD = 3
EPS = 1e-6

HEADS_A = 32
DH_A = 64
KV_A = 4
GROUP_A = HEADS_A // KV_A
KV_COLS = KV_A * DH_A
WINDOW = 128
MASK_W = P + SEQ

HEADS_2 = 8
DH_2 = 128
IDX_HEADS = 16
IDX_DIM = 64
TOPK = min(256, SEQ // 4)
D_FF = 4 * D
W2 = HEADS_2 * DH_2
COL_QI = 6 * W2
COL_KI = COL_QI + IDX_HEADS * IDX_DIM
KI_COLS = IDX_DIM + IDX_HEADS
COL_GA = COL_KI + KI_COLS
COL_GB = COL_GA + D
SCALE_A = DH_A ** -0.5
SCALE_2 = DH_2 ** -0.5
IDX_SCALE = (IDX_DIM ** -0.5) * (IDX_HEADS ** -0.5)

MASKED = -1e30
FAR = 1e34
LOWEST = -3.4e38
PICKED = -3.0e38
PICKED_BELOW = -2.0e38

TURN_KV, TURN_Q, TURN_ZQ, TURN_Z_LAST, TURN_OUT = 0, 1, 2, 8, 9
TURN_QI, TURN_KI, TURN_QI_2, TURN_GRP, TURN_GATE, TURN_YAB, TURN_YAB_LAST = 13, 14, 15, 16, 28, 30, 39
TURN_WO, TURN_FF1, TURN_FF2, TURNS = 40, 44, 60, 76
CHUNK_GATE, CHUNK_YAB, CHUNK_WO, CHUNK_FF1 = 28, 30, 44, 48
CHUNKS = D // CH

STEPS = (2, 3, 4, 5, 6, 7, 8, 9, 10, 11)
SLOT_SUMS, SLOT_GATE, SLOT_TURN = 10, 12, 14
STEPS_LAST = (2, 3, 4, 5, 6, 7, 8, 9, 10, 10)
SUMS_LAST, GATE_LAST, TURN_LAST = 10, 10, 12
INDEX_AT = {2: (0, 1, 2), 3: (3, 4, 5), 4: (6, 7), 5: (8, 9, 10), 6: (11, 12, 13), 7: (14, 15)}

C_ID = 0
C_ONE = C_ID + P
C_DIST = C_ONE + P
C_CAUSAL = C_DIST + MASK_W
C_SLOPE = C_CAUSAL + MASK_W
C_COS = C_SLOPE + HEADS_A
C_SIN = C_COS + T * DH_2 // 2
C_COSI = C_SIN + T * DH_2 // 2
C_SINI = C_COSI + T * IDX_DIM // 2
CONSTS = C_SINI + T * IDX_DIM // 2

V_PRE, V_MIX, V_FFN, V_C = 0, KT, 2 * KT, 3 * KT
VECS = 4 * KT

SH1, SC1, GT1, SH2, SC2, GT2 = range(6)


def shape_constants():
    out = np.zeros((P, CONSTS), np.float32)
    out[:, C_ID:C_ID + P] = np.eye(P)
    q = np.arange(P)[:, None]
    query = np.concatenate([np.broadcast_to(q, (P, P)), np.broadcast_to(q + P, (P, SEQ))], axis=1)
    key = np.concatenate([np.arange(P), np.arange(SEQ)])[None, :]
    dist = query - key
    seen = (dist >= 0) & (dist < WINDOW)
    out[:, C_DIST:C_DIST + MASK_W] = np.where(seen, -dist / SCALE_A, -FAR)
    out[:, C_CAUSAL:C_CAUSAL + MASK_W] = np.where(dist >= 0, 0.0, MASKED)
    slopes = 2.0 ** (-8.0 * np.arange(1, HEADS_A + 1, dtype=np.float32) / HEADS_A)
    out[:, C_SLOPE:C_SLOPE + HEADS_A] = slopes.astype(np.float32)[None]
    for half, c_cos, c_sin in ((DH_2 // 2, C_COS, C_SIN), (IDX_DIM // 2, C_COSI, C_SINI)):
        power = -np.arange(half, dtype=np.float32) / np.float32(half)
        freq = np.power(10000.0, power.astype(np.float64)).astype(np.float32)
        angle = (np.arange(SEQ, dtype=np.float32)[:, None] * freq[None]).astype(np.float32)
        for c, table in ((c_cos, np.cos(angle)), (c_sin, np.sin(angle))):
            out[:, c:c + T * half] = table.astype(np.float32).reshape(T, P, half).transpose(1, 0, 2).reshape(P, -1)
    out[:, C_ONE:C_ONE + P] = 1.0
    return out


def two_block_kernel(nc, x_in, w_in_a, w_out_a, w_ada, w_in_2, w_moba, w_dsa, w_o, w_ff1, w_ff2,
                     b_ada, g_post, g_post_mix, g_post_ffn, sinks, vecs_in, consts_in, out):
    ctx = ExitStack()
    with ctx:
        def sb(name, shape, dt=F32, on=ctx):
            return on.enter_context(nc.sbuf_tensor(name, shape, dt))

        def sem(name):
            return ctx.enter_context(nc.semaphore(name))

        raw = sb("raw", [P, SLOTS, UNIT])
        w_hi = sb("w_hi", [P, SLOTS, UNIT], F32R)
        w_lo = sb("w_lo", [P, SLOTS, UNIT], F32R)
        x = sb("x", [P, T, D])
        h_hi = sb("h_hi", [P, KT, SEQ], F32R)
        h_lo = sb("h_lo", [P, KT, SEQ], F32R)
        post_gain = sb("post_gain", [P, D])
        acc_a = sb("acc_a", [P, D])
        acc_b = sb("acc_b", [P, D])
        ada_raw = sb("ada_raw", [P, 2, D // 2])
        consts = sb("consts", [P, CONSTS])
        vecs = sb("vecs", [P, VECS])
        cond = sb("cond", [P, KT])
        pre_gain = sb("pre_gain", [P, KT])
        pre_shift = sb("pre_shift", [P, KT])
        y_sq = sb("y_sq", [P, T, D // CH])
        y_var = sb("y_var", [P, T])
        y_rstd = sb("y_rstd", [P, T])
        x_sq_part = sb("x_sq_part", [P, T, CHUNKS])
        x_sq = sb("x_sq", [P, T])
        x_rstd = sb("x_rstd", [P, T])
        root_one = sb("root_one", [P, 1])
        rstd_diag = sb("rstd_diag", [P, T, P])
        rstd_row = sb("rstd_row", [P, SEQ])

        with ExitStack() as a:
            o_gated_t = sb("o_gated_t", [P, KT, SEQ], on=a)
            o = sb("o", [P, T, CH], on=a)
            v1 = sb("v1", [P, T, KV_COLS], on=a)
            k1_t = sb("k1_t", [P, KV_A, SEQ], on=a)
            k1_cur = sb("k1_cur", [P, SEQ], on=a)
            v1_cur = sb("v1_cur", [P, T, DH_A], on=a)
            q1_tok = sb("q1_tok", [P, T, CH], on=a)
            q1_t = sb("q1_t", [P, GROUP_A // 2, SEQ], on=a)
            bias1 = sb("bias1", [P, 2, MASK_W], on=a)
            s1 = sb("s1", [P, 2, MASK_W], on=a)
            p1_t = sb("p1_t", [P, MASK_W], on=a)
            z_silu = sb("z_silu", [P, T, CH], on=a)
            slope_cur = sb("slope_cur", [P, GROUP_A], on=a)
            sink_cur = sb("sink_cur", [P, GROUP_A], on=a)
            sink = sb("sink", [P, HEADS_A], on=a)
            sink_sc = sb("sink_sc", [P, HEADS_A], on=a)
            sink_raw_cur = sb("sink_raw_cur", [P, GROUP_A], on=a)
            m1 = sb("m1", [P, 2, T], on=a)
            sink_e = sb("sink_e", [P, GROUP_A, T], on=a)
            neg_cur = sb("neg_cur", [P, GROUP_A, T], on=a)
            l_cur = sb("l_cur", [P, GROUP_A, T], on=a)
        with ExitStack() as a:
            sb("pad_o_gated_t", [P, KT, SEQ], on=a)
            y1 = sb("y1", [P, T, D], on=a)
            sq1 = sb("sq1", [P, CH], on=a)
        with ExitStack() as a:
            o_hi = sb("o_hi", [P, 2 * HEADS_2, SEQ], F32R, on=a)
            o_lo = sb("o_lo", [P, 2 * HEADS_2, SEQ], F32R, on=a)
            with ExitStack() as a2:
                rope_a = sb("rope_a", [P, CH], on=a2)
                rope_b = sb("rope_b", [P, CH], on=a2)
                rot = sb("rot", [P, T, CH], on=a2)
                rot_key = sb("rot_key", [P, T, 2 * IDX_DIM], on=a2)
                q2_t = sb("q2_t", [P, 4, SEQ], on=a2)
                k2_t = sb("k2_t", [P, 4, SEQ], on=a2)
                v2 = sb("v2", [P, T, CH], on=a2)
                s2 = sb("s2", [P, 2, MASK_W], on=a2)
                p2_t = sb("p2_t", [P, MASK_W], on=a2)
                mask_cur = sb("mask_cur", [P, MASK_W], on=a2)
                masks = sb("masks", [P, 2, MASK_W], on=a2)
                score = sb("score", [P, MASK_W], on=a2)
                w_idx = sb("w_idx", [P, T, IDX_HEADS], on=a2)
                top8 = sb("top8", [P, T, 8], on=a2)
                m2 = sb("m2", [P, 2, T], on=a2)
                l2 = sb("l2", [P, 2, T], on=a2)
                l2_inv = sb("l2_inv", [P, T], on=a2)
            with ExitStack() as a2:
                y_t = sb("y_t", [P, KT, SEQ], on=a2)
                gate_a = sb("gate_a", [P, T, CH], on=a2)
                gate_b = sb("gate_b", [P, T, CH], on=a2)
                y_tok = sb("y_tok", [P, T, CH], on=a2)
        with ExitStack() as a:
            y2 = sb("y2", [P, T, D], on=a)
            sq2 = sb("sq2", [P, CH], on=a)
        with ExitStack() as a:
            f_t = sb("f_t", [P, D_FF // P, SEQ], on=a)
        f_tok = acc_b[:, 0:T * CH].rearrange("p (t n) -> p t n", t=T)
        norm_tmp = post_gain[:, 0:2 * KG * SEQ].rearrange("p (b n) -> p b n", b=2)

        ident = consts[:, C_ID:C_ID + P]
        dist8 = consts[:, C_DIST:C_DIST + MASK_W]
        causal = consts[:, C_CAUSAL:C_CAUSAL + MASK_W]
        ones = consts[:, C_ONE:C_ONE + P]

        banks = [ctx.enter_context(nc.psum_tensor(f"bank{n}", [P, CH], F32)) for n in range(8)]
        PAIR_A, PAIR_B = 0, 1
        pair = [banks[0:2], banks[2:4]]
        SCORES, TURNED, OUTS = 4, 6, 7

        raw_loaded = [sem(f"raw_loaded{s}") for s in range(SLOTS)]
        hi_ready = sem("hi_ready")
        lo_ready = sem("lo_ready")
        mm_done = sem("mm_done")
        front_done = sem("front_done")
        evicted = [[sem(f"evicted_{'ab'[p]}{t}") for t in range(T)] for p in range(2)]
        x_loaded = [sem(f"x_loaded{c}") for c in range(CHUNKS)]
        ident_loaded = sem("ident_loaded")
        consts_loaded = sem("consts_loaded")
        vecs_loaded = sem("vecs_loaded")
        sink_loaded = sem("sink_loaded")
        gain_loaded = [sem(f"gain_loaded{n}") for n in range(3)]
        acc_zero = sem("acc_zero")
        acc_init = [sem(f"acc_init{n}") for n in range(6)]
        ada_loaded = [sem("ada_loaded0"), sem("ada_loaded1")]
        ada_done = sem("ada_done")
        cond_sig = sem("cond_sig")
        cond_ready = sem("cond_ready")
        mod_cols = sem("mod_cols")
        scale_rows_ready = sem("scale_rows_ready")
        scale_picked = sem("scale_picked")
        mod_ready = sem("mod_ready")
        mod_rows = sem("mod_rows")
        gain_ready = sem("gain_ready")
        y_squared = sem("y_squared")
        y_last = sem("y_last")
        y_scaled = sem("y_scaled")
        y_stat = sem("y_stat")
        y_root = sem("y_root")
        x_new = sem("x_new")
        x_squared = sem("x_squared")
        x_stat = sem("x_stat")
        x_root = sem("x_root")
        rstd_spread = sem("rstd_spread")
        rstd_row_ready = sem("rstd_row_ready")
        n_turned = sem("n_turned")
        n_scaled = sem("n_scaled")
        h_hi_ready = sem("h_hi_ready")
        h_lo_ready = sem("h_lo_ready")
        kv_tok = sem("kv_tok")
        k1_turned = sem("k1_turned")
        k1_ready = sem("k1_ready")
        q1_ready = sem("q1_ready")
        q1_turned = sem("q1_turned")
        q1_t_ready = sem("q1_t_ready")
        kv_cur_ready = sem("kv_cur_ready")
        heads_cur = sem("heads_cur")
        sink_scaled = sem("sink_scaled")
        bias_ready = sem("bias_ready")
        s1_ready = sem("s1_ready")
        s1_seen = sem("s1_seen")
        s1_masked = sem("s1_masked")
        neg1_ready = sem("neg1_ready")
        p1_ready = sem("p1_ready")
        p1_turned = sem("p1_turned")
        p1_t_ready = sem("p1_t_ready")
        o1_ready = sem("o1_ready")
        o1_kept = sem("o1_kept")
        sink_exp = sem("sink_exp")
        l1_step = sem("l1_step")
        z_sig = sem("z_sig")
        z_ready = sem("z_ready")
        o_step = sem("o_step")
        o_gated = sem("o_gated")
        og_turned = sem("og_turned")
        og_ready = sem("og_ready")
        rot_ready = sem("rot_ready")
        w_idx_ready = sem("w_idx_ready")
        i_turned = sem("i_turned")
        i_t_ready = sem("i_t_ready")
        i_scores = sem("i_scores")
        i_relu = sem("i_relu")
        i_added = sem("i_added")
        top_step = sem("top_step")
        mask_ready = sem("mask_ready")
        qk_turned = sem("qk_turned")
        qk_ready = sem("qk_ready")
        mask_set = sem("mask_set")
        s2_ready = sem("s2_ready")
        s2_seen = sem("s2_seen")
        s2_masked = sem("s2_masked")
        neg2_ready = sem("neg2_ready")
        p2_ready = sem("p2_ready")
        l2_ready = sem("l2_ready")
        p2_normed = sem("p2_normed")
        p2_turned = sem("p2_turned")
        p2_t_ready = sem("p2_t_ready")
        o2_ready = sem("o2_ready")
        o2_hi = sem("o2_hi")
        o2_kept = sem("o2_kept")
        gate_ready = [sem("gate_a_ready"), sem("gate_b_ready")]
        y_part = sem("y_part")
        y_tok_ready = sem("y_tok_ready")
        y_turned = sem("y_turned")
        y_t_ready = sem("y_t_ready")
        f_sq = sem("f_sq")
        f_turned = sem("f_turned")
        f_t_ready = [sem(f"f_t_ready{t}") for t in range(T)]
        f_hi_ready = sem("f_hi_ready")
        f_lo_ready = sem("f_lo_ready")
        stored = sem("stored")

        H_NORM0, H_OUT, H_NORM1, H_WO, H_NORM2 = range(0, 5 * UPT, UPT)

        MOD_UNITS = (None, 64, 160)
        SHIFT_FIRST = 9
        SCALE_SLOTS = (1, 2, 3, 4)

        def shift_bank(r):
            return pair[(PAIR_B, PAIR_A)[r - 1]][1]

        X_STATS = (0, 3, 7)

        LAST_BANKS = [(t, half * KG + c) for half in range(2) for t in range(T) for c in range(KG)]

        w_a = w_in_a.rearrange("(k p) n -> p k n", p=P)
        w_oa = w_out_a.rearrange("(k p) n -> p k n", p=P)
        w_2 = w_in_2.rearrange("(k p) n -> p k n", p=P)
        w_m = w_moba.rearrange("(k p) n -> p k n", p=P)
        w_d = w_dsa.rearrange("(k p) n -> p k n", p=P)
        w_oo = w_o.rearrange("(k p) n -> p k n", p=P)
        w_f1 = w_ff1.rearrange("(k p) n -> p k n", p=P)
        w_f2 = w_ff2.rearrange("(k p) n -> p k n", p=P)
        w_ad = w_ada.rearrange("(k p) n -> p k n", p=P)

        def two(ap, k=2):
            return ap.rearrange("p (k n) -> p k n", k=k)

        def unit_of(turn, s):
            return turn * UPT + s

        def used(buf, turn, s):
            if isinstance(turn, int) and TURN_KI <= turn <= TURN_QI_2 and s % 2 == 0:
                return two(buf[:, s % SLOTS, :])[:, :, 0:KI_COLS]
            return buf[:, s % SLOTS, :]

        block = ctx.enter_context(nc.Block())

        @block.sync
        def _(sp):
            def load(turn, s, src, first=False):
                if not first:
                    sp.wait_ge(lo_ready, unit_of(turn, s) - SLOTS + 1)
                dst = two(raw[:, s % SLOTS, :], src.shape[1])[:, :, 0:src.shape[2]]
                sp.dma_start(dst, src).then_inc(raw_loaded[s % SLOTS], 16)

            def load_chunk(turn, w, col):
                for s in range(UPT):
                    load(turn, s, w[:, KG * s:KG * s + KG, bass.ds(col, CH)])

            def load_pair(turn, col):
                for s in range(UPT):
                    w, k = (w_m, s) if s < UPT // 2 else (w_d, s - UPT // 2)
                    load(turn, s, w[:, KG * k:KG * k + KG, bass.ds(col, CH)])

            x_tiles = x_in.rearrange("(t p) n -> p t n", p=P)

            def load_x(c):
                sp.dma_start(x[:, :, c * CH:(c + 1) * CH], x_tiles[:, :, c * CH:(c + 1) * CH])\
                    .then_inc(x_loaded[c], 16)

            for s in range(UPT):
                if s in (0, 1, 3, 4):
                    load_x((0, 1, 3, 4).index(s))
                if s == SLOTS:
                    sp.dma_start(consts[:, C_DIST:CONSTS], consts_in[:, C_DIST:CONSTS]).then_inc(consts_loaded, 16)
                load(TURN_KV, s, w_a[:, KG * s:KG * s + KG, D:D + CH], s < SLOTS)
            load_chunk(TURN_Q, w_a, 0)
            with sp.Fori(0, CHUNKS - 1) as i:
                load_chunk(i * 2 + TURN_ZQ, w_a, i * CH + D + 2 * KV_COLS)
                load_chunk(i * 2 + TURN_ZQ + 1, w_a, i * CH + CH)
            load_chunk(TURN_Z_LAST, w_a, 2 * D + 2 * KV_COLS - CH)
            with sp.Fori(0, CHUNKS) as i:
                load_chunk(i + TURN_OUT, w_oa, i * CH)
            load_chunk(TURN_QI, w_2, COL_QI)
            for s in range(2 * UPT):
                k = KG * (s // 2)
                col, cols = (COL_QI + CH, CH) if s % 2 else (COL_KI, KI_COLS)
                load(TURN_KI, s, w_2[:, k:k + KG, col:col + cols])
            for half in range(2):
                with sp.Fori(0, 2) as b:
                    for part in range(3):
                        load_chunk((b + 2 * half) * 3 + TURN_GRP + part, w_2,
                                   b * CH + (half * 3 + part) * W2)
            load_chunk(TURN_GATE, w_2, COL_GA)
            load_chunk(TURN_GATE + 1, w_2, COL_GB)
            with sp.Fori(0, D // CH - 1) as c:
                load_pair(c * 3 + TURN_YAB, c * CH)
                load_chunk(c * 3 + TURN_YAB + 1, w_2, c * CH + COL_GA + CH)
                load_chunk(c * 3 + TURN_YAB + 2, w_2, c * CH + COL_GB + CH)
            load_pair(TURN_YAB_LAST, D - CH)
            with sp.Fori(0, D // CH) as i:
                load_chunk(i + TURN_WO, w_oo, i * CH)
            with sp.Fori(0, D_FF // CH) as i:
                load_chunk(i + TURN_FF1, w_f1, i * CH)
            with sp.Fori(0, TURNS - TURN_FF2) as i:
                for s in range(UPT):
                    load(i + TURN_FF2, s, w_f2[:, bass.ds(i * 4 + s // 2, 1), (s % 2) * UNIT:(s % 2 + 1) * UNIT])
            out_tiles = out.rearrange("(t p) n -> p t n", p=P)
            for c in range(CHUNKS):
                for t in range(T):
                    sp.wait_ge(x_new, (2 * CHUNKS + c) * T + t + 1)
                    sp.dma_start(out_tiles[:, t, c * CH:(c + 1) * CH], x[:, t, c * CH:(c + 1) * CH]).then_inc(stored, 16)
            sp.wait_ge(stored, 16 * T * CHUNKS)

        @block.gpsimd
        def _(pool):
            def init_acc(acc, part, n):
                pool.memset(acc[:, :], 0.0).then_inc(acc_zero, 1)
                pool.wait_ge(acc_zero, n + 1)
                pool.dma_start(acc[0:1, :], b_ada[:, part * D:(part + 1) * D]).then_inc(acc_init[n], 16)

            def load_ada(m, slot, part, k, half, first=False):
                if not first:
                    pool.wait_ge(ada_done, m - 1)
                col = part * D + half * (D // 2)
                pool.dma_start(two(ada_raw[:, slot, :], 1), w_ad[:, bass.ds(k, 1), col:col + D // 2])\
                    .then_inc(ada_loaded[slot], 16)

            def load_tiles(m, part, k, tiles=4, first=False):
                for n in range(2 * tiles):
                    load_ada(m + n, n % 2, part, k + n // 2, n % 2, first and n < 2)

            def bias(i, j):
                pool.wait_ge(s1_masked, i * GROUP_A + j + 1)
                pool.tensor_tensor(bias1[:, j % 2, :], dist8, slope_cur[:, j:j + 1].to_broadcast([P, MASK_W]), ALU.mult)\
                    .then_inc(bias_ready, 1)

            def load_gain(n, g):
                pool.dma_start(post_gain[:, :], g.partition_broadcast(P)).then_inc(gain_loaded[n], 16)

            def ada_and_bias(i, m, part, k, units, slots, steps):
                for n in slots:
                    at = n % UPT - UPT + units
                    if 0 <= at and n - slots[0] < UPT:
                        load_ada(m + at, at % 2, part, k + at // 2, at % 2)
                    for j in range(GROUP_A):
                        if steps[j] == n + 1:
                            bias(i, j)

            pool.dma_start(sink[:, :], sinks.partition_broadcast(P)).then_inc(sink_loaded, 16)
            init_acc(acc_a, SC1, 0)
            init_acc(acc_b, SH1, 1)
            pool.wait_ge(x_loaded[CHUNKS - 1], 16)
            load_tiles(0, SC1, 0, first=True)
            pool.wait_ge(consts_loaded, 16)
            with pool.Fori(0, CHUNKS - 1) as i:
                pool.wait_ge(heads_cur, i + 1)
                ada_and_bias(i, i * 12 + 8, SH1, i * 2, 4, range(UPT), STEPS)
                ada_and_bias(i, i * 12 + 12, SC1, i * 4 + 4, 8, range(UPT, 2 * UPT), STEPS)
            pool.wait_ge(heads_cur, CHUNKS)
            ada_and_bias(CHUNKS - 1, 44, SH1, 6, 4, range(2 * UPT), STEPS_LAST)
            pool.wait_ge(h_lo_ready, H_NORM0 + UPT)
            load_gain(0, g_post)
            load_tiles(48, SH1, 8, 8)
            pool.wait_ge(mod_ready, 2)
            init_acc(acc_a, GT1, 2)
            init_acc(acc_b, SH2, 3)
            pool.wait_ge(h_lo_ready, H_NORM1 + UPT)
            load_gain(1, g_post_mix)
            with pool.Fori(0, 4) as g:
                load_tiles(g * 8 + 64, GT1, g * 4)
            load_tiles(96, SH2, 0)
            pool.wait_ge(gain_ready, 4)
            init_acc(acc_a, SC2, 4)
            with pool.Fori(0, CHUNKS - 1) as c:
                load_tiles(c * 12 + 104, SC2, c * 2, 2)
                load_tiles(c * 12 + 108, SH2, c * 4 + 4, 4)
            load_tiles(140, SC2, 6, 10)
            pool.wait_ge(mod_ready, 4)
            init_acc(acc_a, GT2, 5)
            pool.wait_ge(h_lo_ready, H_NORM2 + UPT)
            load_gain(2, g_post_ffn)
            with pool.Fori(0, 8) as it:
                load_tiles(it * 4 + 160, GT2, it * 2, 2)

        @block.scalar
        def _(act):
            def split(turn, s, first=False):
                turn, s = turn + s // UPT, s % UPT
                act.wait_ge(raw_loaded[s % SLOTS], (turn * (UPT // SLOTS) + s // SLOTS + 1) * 16)
                if not first:
                    act.wait_ge(mm_done, unit_of(turn, s) - SLOTS + 1)
                act.activation(used(w_hi, turn, s), used(raw, turn, s), ACT.Copy).then_inc(hi_ready, 1)

            def norm_stats(r, junk):
                for c in range(CHUNKS):
                    for t in range(T):
                        if r:
                            act.wait_ge(x_new, ((r - 1) * CHUNKS + c) * T + t + 1)
                        elif t == 0:
                            act.wait_ge(x_loaded[c], 16)
                        act.activation(junk[:, t, c * CH:(c + 1) * CH], x[:, t, c * CH:(c + 1) * CH], ACT.Square,
                                       accum_out=x_sq_part[:, t, c:c + 1]).then_inc(x_squared, 1)
                act.wait_ge(x_stat, X_STATS[r] + 2)
                act.activation(x_rstd[:, :], x_sq[:, :], ACT.Sqrt).then_inc(x_root, 1)

            def norm_row(r):
                act.wait_ge(rstd_spread, r)
                act.activation(rstd_row[:, :], pair[PAIR_B][0][:, 0:SEQ], ACT.Copy).then_inc(rstd_row_ready, 1)

            def norm_hi(r, s):
                act.wait_ge(n_scaled, UPT * r + s + 1)
                if r and s == 0:
                    act.wait_ge(mod_ready, 2 * r)
                for kk in range(KG):
                    k = KG * s + kk
                    src = norm_tmp[:, s % 2, kk * SEQ:(kk + 1) * SEQ]
                    if r:
                        ins = act.activation(h_hi[:, k, :], src, ACT.Identity, bias=pre_shift[:, k:k + 1])
                    else:
                        ins = act.activation(h_hi[:, k, :], src, ACT.Copy)
                ins.then_inc(h_hi_ready, 1)

            def norm_turn(r, turn, first=False):
                for s in range(2):
                    norm_hi(r, s)
                    if first:
                        split(turn, s, first)
                if first:
                    split(turn, 2, first)
                for s in range(UPT):
                    split(turn, s + AHEAD, first and s + AHEAD < SLOTS)
                    if s + 2 < UPT:
                        norm_hi(r, s + 2)

            def load_sqrt():
                act.activation(root_one[:, :], ones[:, 0:1], ACT.Sqrt)

            def y_roots(r):
                act.wait_ge(y_stat, 2 * r)
                act.activation(y_rstd[:, :], y_var[:, :], ACT.Sqrt).then_inc(y_root, 1)

            def round_h(src, s):
                act.activation(h_hi[:, KG * s:KG * s + KG, :], src[:, KG * s:KG * s + KG, :], ACT.Copy)\
                    .then_inc(h_hi_ready, 1)

            def chunk_result(t, turn, chunk):
                if t == 0:
                    act.wait_ge(front_done, chunk + 1)
                else:
                    act.wait_ge(mm_done, unit_of(turn, UPT))

            def square_y(p, t, turn, chunk, n, col, scratch):
                chunk_result(t, turn, chunk)
                act.wait_ge(y_squared, n)
                act.activation(scratch[:, :], pair[p][t][:, :], ACT.Square, accum_out=y_sq[:, t, col:col + 1])\
                    .then_inc(y_squared, 1)

            act.dma_start(consts[:, 0:C_DIST], consts_in[:, 0:C_DIST]).then_inc(ident_loaded, 16)
            act.dma_start(vecs[:, :], vecs_in).then_inc(vecs_loaded, 16)
            act.sem_inc(y_squared, 1)
            act.sem_inc(og_ready, T)
            act.wait_ge(vecs_loaded, 16)
            act.activation(cond[:, :], vecs[:, V_C:V_C + KT], ACT.Sigmoid).then_inc(cond_sig, 1)

            norm_turn(0, TURN_KV, first=True)
            norm_stats(0, y1)
            act.wait_ge(x_stat, 3)
            for t in range(T):
                chunk_result(t, TURN_KV, 0)
                kv = pair[PAIR_A][t][:, :]
                act.activation(q1_tok[:, t, :].rearrange("p (h r d) -> p h r d", h=KV_A, r=2),
                               kv[:, 0:KV_COLS].rearrange("p (h d) -> p h d", h=KV_A).unsqueeze(2)
                               .to_broadcast([P, KV_A, 2, DH_A]), ACT.Copy, scale=x_rstd[:, t:t + 1]).then_inc(kv_tok, 1)
                act.activation(v1[:, t, :], kv[:, KV_COLS:2 * KV_COLS], ACT.Copy, scale=x_rstd[:, t:t + 1])\
                    .then_inc(evicted[PAIR_A][t], 1)

            def keep_q1(turn):
                for t in range(T):
                    chunk_result(t, turn, turn)
                    act.activation(q1_tok[:, t, :], pair[PAIR_B][t][:, :], ACT.Copy, scale=x_rstd[:, t:t + 1])\
                        .then_inc(evicted[PAIR_B][t], 1)

            def turn_q1(i):
                act.wait_ge(k1_ready, T)
                for t in range(T):
                    act.wait_ge(evicted[PAIR_A][t], 1)
                    act.wait_ge(q1_turned, i * T + t + 1)
                    act.activation(q1_t[:, :, t * P:t * P + P], two(banks[TURNED + t][:, :], 4), ACT.Copy)\
                        .then_inc(q1_t_ready, 1)
                act.activation(k1_cur[:, :], k1_t[:, bass.ds(i, 1), :], ACT.Copy).then_inc(kv_cur_ready, 1)
                act.activation(v1_cur[:, :, :], v1[:, :, bass.ds(i * DH_A, DH_A)], ACT.Copy).then_inc(kv_cur_ready, 1)

            def attn1_out(i, b):
                act.wait_ge(o1_ready, i * 2 + b + 1)
                act.activation(o[:, :, b * (CH // 2):(b + 1) * (CH // 2)], two(banks[OUTS][:, :]), ACT.Copy)\
                    .then_inc(o1_kept, 1)

            def attn1(i, k):
                if k < GROUP_A:
                    act.wait_ge(neg1_ready, i * GROUP_A + k + 1)
                    act.activation(s1[:, k % 2, 0:P], s1[:, k % 2, 0:P], ACT.Exp, bias=neg_cur[:, k, 0:1], scale=SCALE_A,
                                   accum_out=l_cur[:, k, 0:1])
                    act.activation(s1[:, k % 2, P:MASK_W], s1[:, k % 2, P:MASK_W], ACT.Exp, bias=neg_cur[:, k, 1:2],
                                   scale=SCALE_A, accum_out=l_cur[:, k, 1:2]).then_inc(p1_ready, 1)
                if 1 <= k <= GROUP_A:
                    act.wait_ge(p1_turned, i * GROUP_A + k)
                    act.activation(p1_t[:, :], banks[TURNED][:, 0:MASK_W], ACT.Copy).then_inc(p1_t_ready, 1)
                if k == 5:
                    attn1_out(i, 0)

            def sink_share(i):
                act.wait_ge(l1_step, i * 3 + 1)
                act.activation(sink_e[:, :, :], sink_e[:, :, :], ACT.Exp).then_inc(sink_exp, 1)

            def z_sigmoid(c, turn):
                for t in range(T):
                    chunk_result(t, turn, turn)
                    act.wait_ge(og_turned, c * T + t + 1)
                    act.activation(z_silu[:, t, :], pair[PAIR_A][t][:, :], ACT.Sigmoid, scale=x_rstd[:, t:t + 1])\
                        .then_inc(z_sig, 1)

            def attn1_slot(i, n, steps, sums, gate, turn):
                if n == 1:
                    turn_q1(i)
                for k, at in enumerate(steps):
                    if at == n:
                        attn1(i, k)
                if n == sums:
                    sink_share(i)
                    z_sigmoid(i, i * 2 + TURN_ZQ)
                if n == gate:
                    attn1_out(i, 1)
                if n == turn + 1:
                    keep_og(i)

            def keep_og(c):
                for t in range(T):
                    act.wait_ge(og_turned, c * T + T + t + 1)
                    act.activation(o_gated_t[:, bass.ds(c * 4, 4), t * P:t * P + P], two(banks[TURNED + t][:, :], 4),
                                   ACT.Copy).then_inc(og_ready, 1)

            for s in range(UPT):
                split(TURN_Q, s + AHEAD)
                if s == 3:
                    for t in range(T):
                        act.wait_ge(k1_turned, t + 1)
                        act.activation(k1_t[:, :, t * P:t * P + P], two(banks[TURNED + t][:, :], KV_A), ACT.Copy)\
                            .then_inc(k1_ready, 1)
            keep_q1(TURN_Q)
            with act.Fori(0, CHUNKS - 1) as i:
                for s in range(UPT):
                    split(i * 2 + TURN_ZQ, s + AHEAD)
                    attn1_slot(i, s, STEPS, SLOT_SUMS, SLOT_GATE, SLOT_TURN)
                for s in range(UPT):
                    split(i * 2 + TURN_ZQ + 1, s + AHEAD)
                    attn1_slot(i, UPT + s, STEPS, SLOT_SUMS, SLOT_GATE, SLOT_TURN)
                keep_q1(i * 2 + TURN_ZQ + 1)
            last = CHUNKS - 1
            for s in range(UPT):
                split(TURN_Z_LAST, s + AHEAD)
                attn1_slot(last, s, STEPS_LAST, SUMS_LAST, GATE_LAST, UPT * 2)
                if s == 2:
                    act.wait_ge(og_ready, T * CHUNKS)
                if s >= 2:
                    act.wait_ge(mm_done, TURN_Z_LAST * UPT + s - 1)
                    round_h(o_gated_t, s - 2)

            for s in range(UPT):
                split(TURN_OUT, s + AHEAD)
                attn1_slot(last, UPT + s, STEPS_LAST, SUMS_LAST, GATE_LAST, UPT * 2)
                if UPT + s == TURN_LAST:
                    keep_og(last)
                    act.wait_ge(og_ready, T * (CHUNKS + 1))
                    for k in (6, 7):
                        round_h(o_gated_t, k)
            for n in range(CHUNKS):
                if n:
                    for s in range(UPT):
                        split(TURN_OUT + n, s + AHEAD)
                if n == 2:
                    load_sqrt()
                for t in range(T):
                    square_y((n + 1) % 2, t, TURN_OUT + n, TURN_OUT + n, n * T + t + 1, n, sq1)
            y_roots(1)
            norm_stats(1, y1)
            norm_row(1)

            def keep_turned(count, dst, heads=4):
                for t in range(T):
                    act.wait_ge(i_turned, count + t + 1)
                    act.activation(dst[:, :, t * P:t * P + P], two(banks[TURNED + t][:, 0:heads * P], heads), ACT.Copy)\
                        .then_inc(i_t_ready, 1)

            def index_relu(h):
                act.wait_ge(i_scores, h + 1)
                if h >= 2:
                    act.wait_ge(i_added, h - 1)
                act.activation(s2[:, h % 2, :], banks[SCORES + h % 2][:, 0:MASK_W], ACT.Relu).then_inc(i_relu, 1)

            ki_t = v2[:, 0:1, 0:SEQ]
            norm_turn(1, TURN_QI)
            for s in range(2 * UPT):
                split(TURN_KI, s + AHEAD)
                if s == 8:
                    keep_turned(0, q2_t)

            def keep_qk(n, dst):
                for t in range(T):
                    act.wait_ge(qk_turned, n * T + t + 1)
                    act.activation(dst[:, :, t * P:t * P + P], two(banks[TURNED + t][:, :], 4), ACT.Copy)\
                        .then_inc(qk_ready, 1)

            def attn2(g, k):
                if 1 <= k <= 4:
                    act.wait_ge(p2_turned, g * 4 + k)
                    act.activation(p2_t[:, :], banks[TURNED][:, 0:MASK_W], ACT.Copy).then_inc(p2_t_ready, 1)
                if k < 4:
                    act.wait_ge(neg2_ready, g * 4 + k + 1)
                    act.activation(s2[:, k % 2, 0:P], s2[:, k % 2, 0:P], ACT.Exp, bias=m2[:, k % 2, 0:1], scale=SCALE_2,
                                   accum_out=l2[:, k % 2, 0:1])
                    act.activation(s2[:, k % 2, P:MASK_W], s2[:, k % 2, P:MASK_W], ACT.Exp, bias=m2[:, k % 2, 1:2],
                                   scale=SCALE_2, accum_out=l2[:, k % 2, 1:2]).then_inc(p2_ready, 1)
                if k >= 2:
                    act.wait_ge(o2_ready, g * 4 + k - 1)
                    act.activation(o_hi[:, bass.ds(g * 4 + k - 2, 1), :], banks[OUTS][:, 0:SEQ].unsqueeze(1), ACT.Copy)\
                        .then_inc(o2_hi, 1)

            def group_rest(g):
                for s in range(UPT):
                    split(g * 3 + TURN_GRP + 1, s + AHEAD)
                    if s == 4:
                        keep_qk(g * 2, q2_t)
                for s in range(UPT):
                    split(g * 3 + TURN_GRP + 2, s + AHEAD)
                    if s == 4:
                        keep_qk(g * 2 + 1, k2_t)
                for t in range(T):
                    chunk_result(t, g * 3 + TURN_GRP + 2, g * 3 + TURN_GRP + 2)
                    act.activation(v2[:, t, :], pair[PAIR_B][t][:, :], ACT.Copy).then_inc(evicted[PAIR_B][t], 1)

            def attn2_turn(g, turn):
                for s in range(UPT):
                    split(turn, s + AHEAD)
                    if 1 <= s <= 6:
                        attn2(g, s - 1)

            for s in range(UPT):
                split(TURN_GRP, s + AHEAD)
                if s == 1:
                    keep_turned(T, ki_t, 1)
                if s == 4:
                    keep_turned(2 * T, k2_t)
                for h in INDEX_AT.get(s, ()):
                    index_relu(h)
            group_rest(0)
            with act.Fori(1, 4) as g:
                attn2_turn(g - 1, g * 3 + TURN_GRP)
                group_rest(g)

            def keep_gate(n, c, turn, chunk):
                dst = (gate_a, gate_b)[n]
                for t in range(T):
                    chunk_result(t, turn, chunk)
                    act.wait_ge(y_tok_ready, c * T + t + 1)
                    act.activation(dst[:, t, :], pair[n][t][:, :], ACT.Sigmoid).then_inc(evicted[n][t], 1)

            def keep_y(c):
                for t in range(T):
                    act.wait_ge(y_turned, c * T + T + t + 1)
                    act.activation(y_t[:, bass.ds(c * 4, 4), t * P:t * P + P], two(banks[TURNED + t][:, :], 4), ACT.Copy)\
                        .then_inc(y_t_ready, 1)

            attn2_turn(3, TURN_GATE)
            act.wait_ge(o2_kept, 2 * HEADS_2 + 1)
            keep_gate(0, 0, TURN_GATE, CHUNK_GATE)
            for s in range(UPT):
                split(TURN_GATE + 1, s + AHEAD)
            keep_gate(1, 0, TURN_GATE + 1, CHUNK_GATE + 1)
            with act.Fori(0, D // CH - 1) as c:
                for s in range(UPT):
                    split(c * 3 + TURN_YAB, s + AHEAD)
                for s in range(UPT):
                    split(c * 3 + TURN_YAB + 1, s + AHEAD)
                    if s == 6:
                        keep_y(c)
                keep_gate(0, c + 1, c * 3 + TURN_YAB + 1, c * 4 + CHUNK_YAB + 2)
                for s in range(UPT):
                    split(c * 3 + TURN_YAB + 2, s + AHEAD)
                keep_gate(1, c + 1, c * 3 + TURN_YAB + 2, c * 4 + CHUNK_YAB + 3)
            act.wait_ge(mm_done, TURN_YAB_LAST * UPT)
            act.wait_ge(y_t_ready, T * (CHUNKS - 1))
            for s in range(UPT):
                split(TURN_YAB_LAST, s + AHEAD)
                if s < 6:
                    round_h(y_t, s)
            for n in range(CHUNKS):
                for s in range(UPT):
                    split(TURN_WO + n, s + AHEAD)
                    if n == 0 and s == 2:
                        keep_y(CHUNKS - 1)
                        act.wait_ge(y_t_ready, T * CHUNKS)
                        for k in (6, 7):
                            round_h(y_t, k)
                if n == 2:
                    load_sqrt()
                for t in range(T):
                    square_y(n % 2, t, TURN_WO + n, CHUNK_WO + n, (CHUNKS + n) * T + t + 1, n, sq2)
            y_roots(2)
            norm_stats(2, y2)
            norm_row(2)

            def relu(p, c, turn):
                for t in range(T):
                    chunk_result(t, turn, c + CHUNK_FF1)
                    act.wait_ge(f_turned, c * T + t + 1)
                    act.activation(f_tok[:, t, :], pair[p][t][:, :], ACT.Relu).then_inc(evicted[p][t], 1)

            def keep_f(c):
                act.wait_ge(f_turned, c * T + 1 + T)
                act.activation(f_t[:, bass.ds(c * 4, 4), 0:P], two(banks[TURNED][:, :], 4), ACT.Copy)\
                    .then_inc(f_t_ready[0], 1)

            def ff1_turn(c):
                for s in range(UPT):
                    split(c + TURN_FF1, s + AHEAD)
                    if s == 4:
                        keep_f(c - 1)

            norm_turn(2, TURN_FF1)
            relu(PAIR_A, 0, TURN_FF1)
            with act.Fori(0, 7) as it:
                for b in range(2):
                    ff1_turn(it * 2 + 1 + b)
                    relu(1 - b, it * 2 + 1 + b, it * 2 + 1 + b + TURN_FF1)
            def round_f(c, b):
                act.activation(h_hi[:, 4 * b:4 * b + 4, :], f_t[:, bass.ds(c * 4, 4), :], ACT.Copy)\
                    .then_inc(f_hi_ready, 1)

            for s in range(UPT):
                split(TURN_FF2 - 1, s + AHEAD)
                if s == 3:
                    for t in range(T):
                        act.wait_ge(f_t_ready[t], 1)
                    act.wait_ge(mm_done, (TURN_FF2 - 1) * UPT + 4 // KG)
                    round_f(0, 0)
                if s == 4:
                    keep_f(14)
            relu(PAIR_B, 15, TURN_FF1 + 15)

            def ff2_turn(c, b, last=False):
                for s in range(UPT):
                    if not last or s + AHEAD < UPT:
                        split(c + TURN_FF2, s + AHEAD)
                    if s == 4 and not last:
                        act.wait_ge(mm_done, (c + TURN_FF2) * UPT)
                        round_f(c + 1, 1 - b)

            split(TURN_FF2, AHEAD)
            keep_f(15)
            for t in range(T):
                act.wait_ge(f_t_ready[t], D_FF // CH)
            for s in range(1, UPT):
                split(TURN_FF2, s + AHEAD)
                if s == 4:
                    round_f(1, 1)
            ff2_turn(1, 1)
            with act.Fori(1, 7) as it:
                for b in range(2):
                    ff2_turn(it * 2 + b, b)
            ff2_turn(14, 0)
            ff2_turn(15, 1, last=True)
            for n, (t, c) in enumerate(LAST_BANKS):
                act.wait_ge(y_last, n // KG + 1)
                act.wait_ge(y_squared, 4 * CHUNKS + n + 1)
                act.activation(f_tok[:, 0, :], banks[t * CHUNKS + c][:, :], ACT.Square, accum_out=y_sq[:, t, c:c + 1])\
                    .then_inc(y_squared, 1)
            y_roots(3)

        @block.vector
        def _(dve):
            def split(turn, s):
                turn, s = turn + s // UPT, s % UPT
                dve.wait_ge(hi_ready, unit_of(turn, s) + 1)
                dve.tensor_tensor(used(w_lo, turn, s), used(raw, turn, s), used(w_hi, turn, s).bitcast(F32),
                                  ALU.subtract).then_inc(lo_ready, 1)

            def add_ada(m, slot, acc, k, half, loads):
                dve.wait_ge(ada_loaded[slot], loads)
                if not isinstance(m, int) or m > 1:
                    dve.wait_ge(ada_done, m - 1)
                part = acc[:, half * (D // 2):(half + 1) * (D // 2)]
                dve.scalar_tensor_tensor(part, ada_raw[:, slot, :], cond[:, bass.ds(k, 1)], part, ALU.mult, ALU.add)\
                    .then_inc(ada_done, 1)

            def ada(m, n, acc, k):
                add_ada(m + n, n % 2, acc, k, n % 2, (m + n - n % 2) * 8 + 16)

            def y_stats(r):
                dve.wait_ge(y_squared, T * CHUNKS * r + 1)
                dve.tensor_reduce(y_var[:, :], y_sq[:, :, :], AX.X, ALU.add).then_inc(y_stat, 1)
                dve.wait_ge(y_stat, 2 * r - 1)
                dve.tensor_scalar(y_var[:, :], y_var[:, :], 1.0 / D, EPS, ALU.mult, ALU.add).then_inc(y_stat, 1)

            def add_residual(r, y):
                dve.wait_ge(y_root, 2 * r - 1)
                dve.reciprocal(y_rstd[:, :], y_rstd[:, :]).then_inc(y_root, 1)
                dve.wait_ge(y_root, 2 * r)
                for c in range(CHUNKS):
                    for t in range(T):
                        piece = x[:, t, c * CH:(c + 1) * CH]
                        dve.scalar_tensor_tensor(piece, y[:, t, c * CH:(c + 1) * CH], y_rstd[:, t:t + 1], piece,
                                                 ALU.mult, ALU.add).then_inc(x_new, 1)

            def norm_stats(r):
                dve.wait_ge(x_squared, T * CHUNKS * (r + 1))
                dve.tensor_reduce(x_sq[:, :], x_sq_part[:, :, :], AX.X, ALU.add).then_inc(x_stat, 1)
                dve.wait_ge(x_stat, X_STATS[r] + 1)
                dve.tensor_scalar(x_sq[:, :], x_sq[:, :], 1.0 / D, EPS, ALU.mult, ALU.add).then_inc(x_stat, 1)
                dve.wait_ge(x_root, r + 1)
                dve.reciprocal(x_rstd[:, :], x_rstd[:, :]).then_inc(x_stat, 1)
                if r == 0:
                    return
                dve.wait_ge(x_stat, X_STATS[r] + 3)
                for t in range(T):
                    ins = dve.tensor_scalar(rstd_diag[:, t, :], ident, x_rstd[:, t:t + 1], None, ALU.mult)
                ins.then_inc(x_stat, 1)

            def norm_scale(r, s, gain):
                dve.wait_ge(n_turned, UPT * r + s + 1)
                if r and s == 0:
                    dve.wait_ge(rstd_row_ready, r)
                if s >= 2:
                    dve.wait_ge(h_lo_ready, 2 * UPT * r + s - 1)
                for kk in range(KG):
                    k = KG * s + kk
                    cols = slice(kk * SEQ, (kk + 1) * SEQ)
                    src = banks[SCORES + s % 4][:, cols]
                    if r:
                        ins = dve.scalar_tensor_tensor(norm_tmp[:, s % 2, cols], src, gain[:, k:k + 1], rstd_row[:, :],
                                                       ALU.mult, ALU.mult)
                    else:
                        ins = dve.tensor_scalar(norm_tmp[:, s % 2, cols], src, gain[:, k:k + 1], None, ALU.mult)
                ins.then_inc(n_scaled, 1)

            def norm_lo(r, s):
                dve.wait_ge(h_hi_ready, 2 * UPT * r + s + 1)
                for kk in range(KG):
                    k = KG * s + kk
                    src = norm_tmp[:, s % 2, kk * SEQ:(kk + 1) * SEQ]
                    hi = h_hi[:, k, :].bitcast(F32)
                    if r:
                        ins = dve.scalar_tensor_tensor(h_lo[:, k, :], src, pre_shift[:, k:k + 1], hi, ALU.add,
                                                       ALU.subtract)
                    else:
                        ins = dve.tensor_tensor(h_lo[:, k, :], src, hi, ALU.subtract)
                ins.then_inc(h_lo_ready, 1)

            def norm_first(r, gain):
                norm_scale(r, 0, gain)
                norm_scale(r, 1, gain)
                norm_lo(r, 0)
                norm_scale(r, 2, gain)
                norm_lo(r, 1)

            def norm_turn(r, turn, gain):
                for s in range(UPT):
                    split(turn, s + AHEAD)
                    if s + 3 < UPT:
                        norm_scale(r, s + 3, gain)
                    if s + 2 < UPT:
                        norm_lo(r, s + 2)

            def low_h(src, s, done):
                dve.wait_ge(h_hi_ready, done + s + 1)
                dve.tensor_tensor(h_lo[:, KG * s:KG * s + KG, :], src[:, KG * s:KG * s + KG, :],
                                  h_hi[:, KG * s:KG * s + KG, :].bitcast(F32), ALU.subtract).then_inc(h_lo_ready, 1)

            def pick_scale(r, q):
                dve.wait_ge(scale_rows_ready, (r - 1) * 4 + q + 1)
                if q:
                    dve.wait_ge(scale_picked, (r - 1) * 8 + 2 * q)
                own = two(ada_raw[:, 0, 0:CH], CH // P)
                dve.tensor_tensor(own, two(banks[SCORES + q][:, :], CH // P),
                                  ident.unsqueeze(1).to_broadcast([P, CH // P, P]), ALU.mult).then_inc(scale_picked, 1)
                dve.wait_ge(scale_picked, (r - 1) * 8 + 2 * q + 1)
                dve.tensor_reduce(pre_gain[:, q * CH // P:(q + 1) * CH // P], own, AX.X, ALU.add)\
                    .then_inc(scale_picked, 1)

            def read_scale(r):
                dve.wait_ge(scale_picked, r * 8)
                gain = (V_MIX, V_FFN)[r - 1]
                dve.scalar_tensor_tensor(pre_gain[:, :], pre_gain[:, :], 1.0, vecs[:, gain:gain + KT], ALU.add,
                                         ALU.mult).then_inc(mod_ready, 1)

            def read_shift(r):
                dve.wait_ge(mod_cols, r)
                dve.tensor_copy(pre_shift[:, :], shift_bank(r)[:, 0:KT]).then_inc(mod_ready, 1)

            def gate_gain(n, q, bank):
                dve.wait_ge(gain_loaded[n + 1], 16)
                dve.wait_ge(mod_rows, 4 * n + q + 1)
                part = post_gain[:, q * CH:(q + 1) * CH]
                dve.tensor_tensor(part, banks[bank][:, :], part, ALU.mult).then_inc(gain_ready, 1)

            def chunk_result(t, turn, chunk):
                if t == 0:
                    dve.wait_ge(front_done, chunk + 1)
                else:
                    dve.wait_ge(mm_done, unit_of(turn, UPT))

            def scale_y(p, t, n, col, y):
                dve.wait_ge(y_squared, n)
                dve.tensor_tensor(y[:, t, col * CH:(col + 1) * CH], pair[p][t][:, :],
                                  post_gain[:, col * CH:(col + 1) * CH], ALU.mult).then_inc(evicted[p][t], 1)

            dve.sem_inc(s1_masked, 2)
            dve.sem_inc(o1_kept, 1)
            dve.sem_inc(y_tok_ready, T)
            dve.sem_inc(o2_kept, 1)
            dve.wait_ge(cond_sig, 1)
            dve.tensor_tensor(cond[:, :], cond[:, :], vecs[:, V_C:V_C + KT], ALU.mult).then_inc(cond_ready, 1)
            dve.wait_ge(ident_loaded, 16)
            for s in range(AHEAD):
                norm_scale(0, s, vecs[:, V_PRE:V_PRE + KT])
                if s < 2:
                    norm_lo(0, s)
                split(TURN_KV, s)
            norm_turn(0, TURN_KV, vecs[:, V_PRE:V_PRE + KT])
            norm_stats(0)
            dve.wait_ge(x_stat, 3)
            dve.wait_ge(cond_ready, 1)
            for n in range(2):
                dve.wait_ge(acc_init[n], 16)
            dve.wait_ge(sink_loaded, 16)
            dve.tensor_scalar(sink_sc[:, :], sink[:, :], 1.0 / SCALE_A, None, ALU.mult).then_inc(sink_scaled, 1)
            dve.wait_ge(consts_loaded, 16)
            dve.wait_ge(sink_scaled, 1)

            def set_heads(i):
                dve.tensor_copy(slope_cur[:, :], consts[:, bass.ds(i * GROUP_A + C_SLOPE, GROUP_A)])
                dve.tensor_copy(sink_raw_cur[:, :], sink[:, bass.ds(i * GROUP_A, GROUP_A)])
                dve.tensor_copy(sink_cur[:, :], sink_sc[:, bass.ds(i * GROUP_A, GROUP_A)]).then_inc(heads_cur, 1)

            def attn1_scores(i, j):
                h = i * GROUP_A + j
                dve.wait_ge(bias_ready, h + 1)
                dve.wait_ge(s1_ready, h + 1)
                if j == 0:
                    dve.wait_ge(heads_cur, i + 1)
                dve.sem_inc(s1_seen, 1)
                for t, (c0, c1) in enumerate(((0, P), (P, MASK_W))):
                    ins = dve.tensor_tensor_reduce(s1[:, j % 2, c0:c1], banks[SCORES + j % 2][:, c0:c1],
                                                   bias1[:, j % 2, c0:c1], 1.0, LOWEST, ALU.add, ALU.max,
                                                   m1[:, j % 2, t:t + 1])
                ins.then_inc(s1_masked, 1)
                dve.wait_ge(s1_masked, h + 3)
                dve.tensor_scalar(neg_cur[:, j, :], m1[:, j % 2, :], sink_cur[:, j:j + 1], -SCALE_A, ALU.max, ALU.mult)\
                    .then_inc(neg1_ready, 1)

            def sums1(i):
                dve.wait_ge(p1_ready, i * GROUP_A + GROUP_A)
                dve.tensor_tensor(sink_e[:, :, :], neg_cur[:, :, :],
                                  sink_raw_cur[:, :].unsqueeze(2).to_broadcast([P, GROUP_A, T]), ALU.add)\
                    .then_inc(l1_step, 1)

            def gate_z(i):
                for t in range(T):
                    dve.wait_ge(z_sig, i * T + t + 1)
                    dve.scalar_tensor_tensor(z_silu[:, t, :], pair[PAIR_A][t][:, :], x_rstd[:, t:t + 1], z_silu[:, t, :],
                                             ALU.mult, ALU.mult).then_inc(evicted[PAIR_A][t], 1)

            def gate_o(i):
                dve.wait_ge(sink_exp, i + 1)
                dve.tensor_tensor(l_cur[:, :, :], l_cur[:, :, :], sink_e[:, :, :], ALU.add).then_inc(l1_step, 1)
                dve.wait_ge(l1_step, i * 3 + 2)
                dve.reciprocal(l_cur[:, :, :], l_cur[:, :, :]).then_inc(l1_step, 1)
                dve.wait_ge(o1_kept, i * 2 + 3)
                dve.wait_ge(l1_step, i * 3 + 3)
                for t in range(T):
                    part = o[:, t, :].rearrange("p (j d) -> p j d", d=DH_A)
                    inv = l_cur[:, :, t:t + 1].to_broadcast([P, GROUP_A, DH_A])
                    dve.tensor_tensor(part, part, inv, ALU.mult).then_inc(o_step, 1)
                gate_z(i)
                for t in range(T):
                    dve.wait_ge(o_step, i * T + t + 1)
                    dve.wait_ge(evicted[PAIR_A][t], i + 2)
                    dve.tensor_tensor(z_silu[:, t, :], o[:, t, :], z_silu[:, t, :], ALU.mult).then_inc(o_gated, 1)

            def attn1_slot(i, n, steps, sums, gate):
                for k, at in enumerate(steps[0:GROUP_A]):
                    if at == n:
                        attn1_scores(i, k)
                if n == sums:
                    sums1(i)
                if n == gate:
                    gate_o(i)

            set_heads(0)
            for s in range(UPT):
                split(TURN_Q, s + AHEAD)
                ada(0, s, acc_a, s // 2)
            with dve.Fori(0, CHUNKS - 1) as i:
                for s in range(UPT):
                    split(i * 2 + TURN_ZQ, s + AHEAD)
                    attn1_slot(i, s, STEPS, SLOT_SUMS, SLOT_GATE)
                    if s >= 4:
                        ada(i * 12 + 8, s - 4, acc_b, i * 2 + (s - 4) // 2)
                for s in range(UPT):
                    split(i * 2 + TURN_ZQ + 1, s + AHEAD)
                    attn1_slot(i, UPT + s, STEPS, SLOT_SUMS, SLOT_GATE)
                    if UPT + s == SLOT_GATE:
                        set_heads(i + 1)
                    ada(i * 12 + 12, s, acc_a, i * 4 + 4 + s // 2)
            last = CHUNKS - 1
            for s in range(UPT):
                split(TURN_Z_LAST, s + AHEAD)
                attn1_slot(last, s, STEPS_LAST, SUMS_LAST, GATE_LAST)
                if s >= 2:
                    low_h(o_gated_t, s - 2, H_OUT)
                if s >= 4:
                    ada(44, s - 4, acc_b, 6 + (s - 4) // 2)

            for n in range(CHUNKS):
                for s in range(UPT):
                    split(TURN_OUT + n, s + AHEAD)
                    if n == 0:
                        attn1_slot(last, UPT + s, STEPS_LAST, SUMS_LAST, GATE_LAST)
                        if UPT + s == TURN_LAST:
                            for k in (6, 7):
                                low_h(o_gated_t, k, H_OUT)
                    elif n < 3:
                        ada(40 + 8 * n, s, acc_b, 4 + 4 * n + s // 2)
                    elif s - 1 in SCALE_SLOTS:
                        pick_scale(1, SCALE_SLOTS.index(s - 1))
                    elif s == UPT - 1:
                        read_scale(1)
                if n == 0:
                    dve.wait_ge(gain_loaded[0], 16)
                for t in range(T):
                    scale_y((n + 1) % 2, t, n * T + t + 2, n, y1)
            for t in range(T):
                dve.wait_ge(evicted[PAIR_A][t], 7)
                dve.wait_ge(evicted[PAIR_B][t], 6)
            y_stats(1)
            add_residual(1, y1)
            norm_stats(1)
            read_shift(1)
            norm_first(1, pre_gain)

            def rope(src, dst, p, t, use, n, heads, half, cos0, sin0, copies=1):
                cols = heads * 2 * half
                cos = consts[:, cos0 + t * half:cos0 + (t + 1) * half]
                sin = consts[:, sin0 + t * half:sin0 + (t + 1) * half]
                xin = src.rearrange("p (h r d) -> p h r d", h=heads, r=2)
                ra = rope_a[:, 0:cols].rearrange("p (h r d) -> p h r d", h=heads, r=2)
                rb = rope_b[:, 0:cols].rearrange("p (h r d) -> p h r d", h=heads, r=2)

                def wide(tab):
                    return tab.unsqueeze(1).to_broadcast([P, heads, half])

                if not (isinstance(n, int) and n + t == 0):
                    dve.wait_ge(rot_ready, n * T + t)
                for r in range(2):
                    dve.tensor_tensor(ra[:, :, r, :], xin[:, :, r, :], wide(cos), ALU.mult)
                for r in range(2):
                    ins = dve.tensor_tensor(rb[:, :, r, :], xin[:, :, 1 - r, :], wide(sin), ALU.mult)
                ins.then_inc(evicted[p][t], 1)
                dve.wait_ge(evicted[p][t], use + 1)
                rows = dst.rearrange("p (h r d) -> p h r d", h=heads * copies, r=2)
                for c in range(copies):
                    for r in range(2):
                        ins = dve.tensor_tensor(rows[:, c * heads:(c + 1) * heads, r, :], ra[:, :, r, :], rb[:, :, r, :],
                                                (ALU.subtract, ALU.add)[r])
                ins.then_inc(rot_ready, 1)

            def index_add(h):
                dve.wait_ge(i_relu, h + 1)
                if h:
                    dve.wait_ge(i_added, h)
                for t, (c0, c1) in enumerate(((0, P), (P, MASK_W))):
                    base = (score if h else causal)[:, c0:c1]
                    ins = dve.scalar_tensor_tensor(score[:, c0:c1], s2[:, h % 2, c0:c1], w_idx[:, t, h:h + 1], base,
                                                   ALU.mult, ALU.add)
                ins.then_inc(i_added, 1)

            def top_round(r):
                if r:
                    dve.wait_ge(top_step, 2 * r)
                for t, (c0, c1) in enumerate(((0, P), (P, MASK_W))):
                    ins = dve.max(top8[:, t, :], score[:, c0:c1])
                ins.then_inc(top_step, 1)
                dve.wait_ge(top_step, 2 * r + 1)
                for t, (c0, c1) in enumerate(((0, P), (P, MASK_W))):
                    ins = dve.match_replace(score[:, c0:c1], top8[:, t, :], score[:, c0:c1], PICKED)
                ins.then_inc(top_step, 1)

            norm_turn(1, TURN_QI, pre_gain)
            def rope_index(turn, t):
                n = 0 if turn == TURN_QI else 2
                chunk_result(t, turn, turn)
                rope(pair[PAIR_A][t][:, :], rot[:, t, :], PAIR_A, t, 7 + n // 2, n, CH // IDX_DIM, IDX_DIM // 2, C_COSI,
                     C_SINI)

            for t in range(T):
                rope_index(TURN_QI, t)
                if t == 0:
                    split(TURN_KI, AHEAD)
            for s in range(1, 2 * UPT):
                split(TURN_KI, s + AHEAD)
            for t in range(T):
                chunk_result(t, TURN_QI_2, TURN_KI)
                ki = pair[PAIR_B][t]
                dve.tensor_scalar(w_idx[:, t, :], ki[:, IDX_DIM:KI_COLS], IDX_SCALE, None, ALU.mult)\
                    .then_inc(w_idx_ready, 1)
                rope(ki[:, 0:IDX_DIM], rot_key[:, t, :], PAIR_B, t, 6, 1, 1, IDX_DIM // 2, C_COSI, C_SINI, 2)
            dve.wait_ge(i_turned, T)
            for t in range(T):
                rope_index(TURN_QI_2, t)
            dve.wait_ge(w_idx_ready, T)

            def rope_chunk(p, turn, use, n):
                for t in range(T):
                    chunk_result(t, turn, turn)
                    rope(pair[p][t][:, :], rot[:, t, :], p, t, use, n, 4, DH_2 // 2, C_COS, C_SIN)

            def attn2_norm(g, k):
                h = g * 4 + k
                if 1 <= k <= 4:
                    b = (k - 1) % 2
                    dve.wait_ge(p2_ready, h)
                    dve.reciprocal(l2_inv[:, :], l2[:, b, :]).then_inc(l2_ready, 1)
                    dve.wait_ge(l2_ready, h)
                    dve.tensor_scalar(s2[:, b, 0:P], s2[:, b, 0:P], l2_inv[:, 0:1], None, ALU.mult)
                    dve.tensor_scalar(s2[:, b, P:MASK_W], s2[:, b, P:MASK_W], l2_inv[:, 1:2], None, ALU.mult)\
                        .then_inc(p2_normed, 1)

            def attn2(g, k):
                h = g * 4 + k
                if k < 4:
                    dve.wait_ge(s2_ready, h + 1)
                    if k == 0:
                        dve.wait_ge(mask_set, g + 1)
                    dve.sem_inc(s2_seen, 1)
                    for t, (c0, c1) in enumerate(((0, P), (P, MASK_W))):
                        ins = dve.tensor_tensor_reduce(s2[:, k % 2, c0:c1], banks[SCORES + k % 2][:, c0:c1],
                                                       mask_cur[:, c0:c1], 1.0, LOWEST, ALU.add, ALU.max,
                                                       m2[:, k % 2, t:t + 1])
                    ins.then_inc(s2_masked, 1)
                    dve.wait_ge(s2_masked, h + 1)
                    dve.tensor_scalar(m2[:, k % 2, :], m2[:, k % 2, :], -SCALE_2, None, ALU.mult).then_inc(neg2_ready, 1)
                if k >= 2:
                    dve.wait_ge(o2_hi, h - 1)
                    dve.tensor_tensor(o_lo[:, bass.ds(h - 2, 1), :], banks[OUTS][:, 0:SEQ].unsqueeze(1),
                                      o_hi[:, bass.ds(h - 2, 1), :].bitcast(F32), ALU.subtract).then_inc(o2_kept, 1)

            def group_rest(g, with_top=False):
                if with_top:
                    dve.wait_ge(i_turned, 3 * T)
                else:
                    dve.wait_ge(qk_turned, g * 2 * T)
                rope_chunk(PAIR_B, g * 3 + TURN_GRP, g * 2 + 7, g * 2 + 3)
                for s in range(UPT):
                    split(g * 3 + TURN_GRP + 1, s + AHEAD)
                    if with_top and s % 2 == 0:
                        top_round(s // 2)
                    if s % 2:
                        ada(g * 8 + 64, s // 2, acc_a, g * 4 + s // 4)
                dve.wait_ge(qk_turned, g * 2 * T + T)
                rope_chunk(PAIR_A, g * 3 + TURN_GRP + 1, g + 9, g * 2 + 4)
                for s in range(UPT):
                    split(g * 3 + TURN_GRP + 2, s + AHEAD)
                    if with_top and s % 2 == 0:
                        top_round(4 + s // 2)
                    if s % 2:
                        ada(g * 8 + 64, 4 + s // 2, acc_a, g * 4 + 2 + s // 4)

            def attn2_turn(g, turn):
                for s in range(UPT):
                    if 1 <= s <= 6:
                        attn2_norm(g, s - 1)
                    split(turn, s + AHEAD)
                    if s == 0:
                        dve.tensor_copy(mask_cur[:, :], masks[:, bass.ds(dve.snap(g >> 1, min_val=0, max_val=1), 1), :]
                                        if not isinstance(g, int) else masks[:, g // 2, :]).then_inc(mask_set, 1)
                    if 1 <= s <= 6:
                        attn2(g, s - 1)

            for s in range(UPT):
                split(TURN_GRP, s + AHEAD)
                for h in INDEX_AT.get(s, ()):
                    index_add(h)
            dve.wait_ge(acc_init[2], 16)
            dve.wait_ge(i_added, IDX_HEADS)
            dve.tensor_copy(masks[:, 0, :], causal).then_inc(mask_ready, 1)
            group_rest(0, with_top=True)
            dve.wait_ge(top_step, TOPK // 4)
            dve.tensor_scalar(score[:, :], score[:, :], PICKED_BELOW, MASKED, ALU.is_gt, ALU.mult).then_inc(mask_ready, 1)
            dve.wait_ge(mask_ready, 2)
            dve.tensor_tensor(masks[:, 1, :], score[:, :], causal, ALU.add).then_inc(mask_ready, 1)
            dve.wait_ge(mask_ready, 3)
            with dve.Fori(1, 4) as g:
                attn2_turn(g - 1, g * 3 + TURN_GRP)
                group_rest(g)

            attn2_turn(3, TURN_GATE)
            dve.wait_ge(acc_init[3], 16)
            for s in range(UPT):
                split(TURN_GATE + 1, s + AHEAD)
                if 1 <= s <= 4:
                    gate_gain(0, s - 1, SCORES + s - 1)
                ada(96, s, acc_b, s // 2)
            dve.wait_ge(acc_init[4], 16)

            def gate_ya(c):
                for t in range(T):
                    dve.wait_ge(y_turned, c * T + t + 1)
                    dve.wait_ge(evicted[PAIR_A][t], c * 2 + 14)
                    dve.wait_ge(front_done, c * 4 + CHUNK_YAB + 1)
                    if t:
                        dve.wait_ge(mm_done, c * 3 * UPT + TURN_YAB * UPT + UPT // 2)
                    dve.tensor_tensor(y_tok[:, t, :], pair[PAIR_A][t][:, :], gate_a[:, t, :], ALU.mult)\
                        .then_inc(evicted[PAIR_A][t], 1)

            def gate_y(c):
                for t in range(T):
                    chunk_result(t, c * 3 + TURN_YAB, c * 4 + CHUNK_YAB + 1)
                    dve.wait_ge(evicted[PAIR_B][t], c * 2 + 16)
                    dve.tensor_tensor(gate_b[:, t, :], pair[PAIR_B][t][:, :], gate_b[:, t, :], ALU.mult)\
                        .then_inc(evicted[PAIR_B][t], 1)
                for t in range(T):
                    dve.wait_ge(evicted[PAIR_A][t], c * 2 + 15)
                    dve.wait_ge(evicted[PAIR_B][t], c * 2 + 17)
                    dve.tensor_tensor(y_tok[:, t, :], y_tok[:, t, :], gate_b[:, t, :], ALU.add).then_inc(y_tok_ready, 1)

            with dve.Fori(0, CHUNKS - 1) as c:
                for s in range(UPT):
                    split(c * 3 + TURN_YAB, s + AHEAD)
                    if s % 2:
                        ada(c * 12 + 104, s // 2, acc_a, c * 2 + s // 4)
                    if s == 6:
                        gate_ya(c)
                gate_y(c)
                for part in range(2):
                    for s in range(UPT):
                        split(c * 3 + TURN_YAB + 1 + part, s + AHEAD)
                        if s % 2:
                            ada(c * 12 + 108 + part * 4, s // 2, acc_b, c * 4 + 4 + part * 2 + s // 4)
            for s in range(UPT):
                split(TURN_YAB_LAST, s + AHEAD)
                if s < 6:
                    low_h(y_t, s, H_WO)
                if s % 2:
                    ada(140, s // 2, acc_a, 6 + s // 4)
                if s == 6:
                    gate_ya(CHUNKS - 1)
            gate_y(CHUNKS - 1)

            dve.wait_ge(gain_ready, 4)
            for n in range(CHUNKS):
                for s in range(UPT):
                    split(TURN_WO + n, s + AHEAD)
                    if n == 0 and s == 2:
                        for k in (6, 7):
                            low_h(y_t, k, H_WO)
                    if n < 2:
                        ada(144 + 8 * n, s, acc_a, 8 + 4 * n + s // 2)
                    if n == CHUNKS - 1:
                        if s - 1 in SCALE_SLOTS:
                            pick_scale(2, SCALE_SLOTS.index(s - 1))
                        elif s == UPT - 1:
                            read_scale(2)
                for t in range(T):
                    scale_y(n % 2, t, (CHUNKS + n) * T + t + 2, n, y2)
            for t in range(T):
                dve.wait_ge(evicted[PAIR_A][t], 23)
                dve.wait_ge(evicted[PAIR_B][t], 25)
            y_stats(2)
            add_residual(2, y2)
            norm_stats(2)
            read_shift(2)
            norm_first(2, pre_gain)

            def square(p, use):
                for t in range(T):
                    dve.wait_ge(evicted[p][t], use + 1)
                    dve.tensor_tensor(f_tok[:, t, :], f_tok[:, t, :], f_tok[:, t, :], ALU.mult).then_inc(f_sq, 1)

            def keep_f(c):
                dve.wait_ge(f_turned, c * T + 2 + T)
                dve.tensor_copy(f_t[:, bass.ds(c * 4, 4), P:SEQ], two(banks[OUTS][:, :], 4)).then_inc(f_t_ready[1], 1)

            norm_turn(2, TURN_FF1, pre_gain)
            square(PAIR_A, 23)
            dve.wait_ge(acc_init[5], 16)

            with dve.Fori(0, 7) as it:
                for b in range(2):
                    for s in range(UPT):
                        split(it * 2 + 1 + b + TURN_FF1, s + AHEAD)
                        if s == 4:
                            keep_f(it * 2 + b)
                        if s in (1, 6):
                            n = 2 * b + s // 6
                            ada(it * 4 + 160, n, acc_a, it * 2 + b)
                    square(1 - b, it + 25 - b)
            def low_f(c, b):
                dve.wait_ge(f_hi_ready, c + 1)
                dve.tensor_tensor(h_lo[:, 4 * b:4 * b + 4, :], f_t[:, bass.ds(c * 4, 4), :],
                                  h_hi[:, 4 * b:4 * b + 4, :].bitcast(F32), ALU.subtract).then_inc(f_lo_ready, 1)

            for s in range(UPT):
                split(TURN_FF2 - 1, s + AHEAD)
                if s < 4:
                    ada(188, s, acc_a, 14 + s // 2)
                if s == 3:
                    dve.wait_ge(f_t_ready[1], 1)
                    low_f(0, 0)
                if s == 4:
                    keep_f(14)
                if s >= 6:
                    for q in (0, 1):
                        gate_gain(1, 2 * (s - 6) + q, SCORES + q)
            square(PAIR_B, 32)

            def ff2_turn(c, b, last=False):
                for s in range(UPT):
                    if not last or s + AHEAD < UPT:
                        split(c + TURN_FF2, s + AHEAD)
                    if s == 4 and not last:
                        low_f(c + 1, 1 - b)

            split(TURN_FF2, AHEAD)
            keep_f(15)
            dve.wait_ge(f_t_ready[1], D_FF // CH)
            for s in range(1, UPT):
                split(TURN_FF2, s + AHEAD)
                if s == 4:
                    low_f(1, 1)
            ff2_turn(1, 1)
            with dve.Fori(1, 7) as it:
                for b in range(2):
                    ff2_turn(it * 2 + b, b)
            ff2_turn(14, 0)
            ff2_turn(15, 1, last=True)
            dve.wait_ge(gain_ready, 8)
            for n, (t, c) in enumerate(LAST_BANKS):
                if n == len(LAST_BANKS) - 1:
                    y_stats(3)
                dve.wait_ge(y_squared, 2 * T * CHUNKS + n + 2)
                dve.tensor_tensor(y2[:, t, c * CH:(c + 1) * CH], banks[t * CHUNKS + c][:, :],
                                  post_gain[:, c * CH:(c + 1) * CH], ALU.mult).then_inc(y_scaled, 1)
            dve.wait_ge(y_scaled, T * CHUNKS)
            add_residual(3, y2)

        @block.tensor
        def _(pe):
            def three(out_ap, hi, lo, rhs_hi, rhs_lo, start, stop):
                pe.matmul(out_ap, hi, rhs_hi, start=start, stop=False)
                pe.matmul(out_ap, hi, rhs_lo, start=False, stop=False)
                return pe.matmul(out_ap, lo, rhs_hi, start=False, stop=stop)

            def unit(turn, s, hi, lo, k0, p, use, first, last, cols=CH):
                pe.wait_ge(lo_ready, unit_of(turn, s) + 1)
                for t in range(T):
                    if first and not (isinstance(use, int) and use == 0):
                        pe.wait_ge(evicted[p][t], use)
                    for kk in range(KG):
                        w = slice(kk * CH, kk * CH + cols)
                        mm = three(pair[p][t][:, 0:cols], hi[:, k0 + kk, t * P:(t + 1) * P],
                                   lo[:, k0 + kk, t * P:(t + 1) * P], w_hi[:, s % SLOTS, w], w_lo[:, s % SLOTS, w],
                                   first and kk == 0, last and kk == KG - 1)
                    if last and t == 0:
                        mm.then_inc(front_done, 1)
                mm.then_inc(mm_done, 1)

            def chunk_unit(turn, s, p, use, h=None, cols=CH):
                if h is not None:
                    pe.wait_ge(h_lo_ready, h + s + 1)
                unit(turn, s, h_hi, h_lo, KG * s, p, use, s == 0, s == UPT - 1, cols)

            def turn_rows(src, t, n, dst, ready):
                for b in range(n):
                    ins = pe.transpose(dst[:, b * P:(b + 1) * P], src[:, t, b * P:(b + 1) * P], ident)
                ins.then_inc(ready, 1)

            def norm_turned(r, s):
                if r:
                    pe.wait_ge(x_new, ((r - 1) * CHUNKS + KG * s * P // CH + 1) * T)
                else:
                    pe.wait_ge(x_loaded[KG * s * P // CH], 16)
                if s >= 4:
                    pe.wait_ge(n_scaled, UPT * r + s - 3)
                for kk in range(KG):
                    for t in range(T):
                        k = KG * s + kk
                        ins = pe.transpose(banks[SCORES + s % 4][:, kk * SEQ + t * P:kk * SEQ + (t + 1) * P],
                                           x[:, t, k * P:(k + 1) * P], ident)
                ins.then_inc(n_turned, 1)

            def norm_turn(r, turn, p, use, h):
                if r:
                    shift_columns(r, 0, SHIFT_FIRST)
                ahead = 4 if r else 3
                for s in range(ahead):
                    norm_turned(r, s)
                if r:
                    shift_columns(r, SHIFT_FIRST, KT)
                    pe.wait_ge(x_stat, X_STATS[r] + 4)
                    for t in range(T):
                        ins = pe.matmul(pair[PAIR_B][0][:, t * P:(t + 1) * P], ones, rstd_diag[:, t, :],
                                        start=True, stop=True)
                    ins.then_inc(rstd_spread, 1)
                for s in range(UPT):
                    chunk_unit(turn, s, p, use, h)
                    if s + ahead < UPT:
                        norm_turned(r, s + ahead)

            def shift_columns(r, k0, k1):
                pe.wait_ge(ada_done, MOD_UNITS[r])
                for k in range(k0, k1):
                    ins = pe.matmul(shift_bank(r)[:, k:k + 1], acc_b[:, k * P:(k + 1) * P], ones[:, 0:1],
                                    start=True, stop=True)
                if k1 == KT:
                    ins.then_inc(mod_cols, 1)

            def scale_rows(r, q):
                pe.wait_ge(ada_done, MOD_UNITS[r])
                pe.matmul(banks[SCORES + q][:, :], ones, acc_a[:, q * CH:(q + 1) * CH], start=True, stop=True)\
                    .then_inc(scale_rows_ready, 1)

            def rows(units, q, bank):
                pe.wait_ge(ada_done, units)
                pe.matmul(banks[bank][:, :], ones, acc_a[:, q * CH:(q + 1) * CH], start=True, stop=True)\
                    .then_inc(mod_rows, 1)

            for credit in (og_turned, y_turned, f_turned):
                pe.sem_inc(credit, T)
            pe.wait_ge(ident_loaded, 16)
            norm_turn(0, TURN_KV, PAIR_A, 0, H_NORM0)
            for s in range(UPT):
                chunk_unit(TURN_Q, s, PAIR_B, 0)
                if s == 2:
                    for t in range(T):
                        pe.wait_ge(kv_tok, t + 1)
                        turn_rows(q1_tok, t, KV_A, banks[TURNED + t], k1_turned)

            def turn_q1(i):
                pe.wait_ge(og_ready, i * T + T)
                for t in range(T):
                    pe.wait_ge(evicted[PAIR_B][t], i + 1)
                    turn_rows(q1_tok, t, 4, banks[TURNED + t], q1_turned)

            def attn1(i, k):
                if k < GROUP_A:
                    if k == 0:
                        pe.wait_ge(q1_t_ready, i * T + T)
                        pe.wait_ge(kv_cur_ready, i * 2 + 2)
                    lane = slice((k % 2) * DH_A, (k % 2 + 1) * DH_A)
                    q = q1_t[lane, k // 2, :]
                    pe.matmul(banks[SCORES + k % 2][:, 0:P], q[:, 0:P], k1_cur[lane, 0:P], start=True, stop=True)
                    pe.matmul(banks[SCORES + k % 2][:, P:MASK_W], q[:, P:SEQ], k1_cur[lane, :], start=True, stop=True)\
                        .then_inc(s1_ready, 1)
                if k >= 2:
                    j = k - 2
                    pe.wait_ge(p1_t_ready, i * GROUP_A + j + 1)
                    if j % 4 == 0:
                        pe.wait_ge(o1_kept, i * 2 + j // 4 + 1)
                    out0 = banks[OUTS][:, (j % 4) * DH_A:(j % 4 + 1) * DH_A]
                    out1 = banks[OUTS][:, CH // 2 + (j % 4) * DH_A:CH // 2 + (j % 4 + 1) * DH_A]
                    pe.matmul(out0, p1_t[:, 0:P], v1_cur[:, 0, :], start=True, stop=True)
                    pe.matmul(out1, p1_t[:, P:SEQ], v1_cur[:, 0, :], start=True, stop=False)
                    ins = pe.matmul(out1, p1_t[:, SEQ:MASK_W], v1_cur[:, 1, :], start=False, stop=True)
                    if j % 4 == 3:
                        ins.then_inc(o1_ready, 1)
                if 1 <= k <= GROUP_A:
                    pe.wait_ge(p1_ready, i * GROUP_A + k)
                    for b in range(3):
                        ins = pe.transpose(banks[TURNED][:, b * P:(b + 1) * P],
                                           s1[:, (k - 1) % 2, b * P:(b + 1) * P], ident)
                    ins.then_inc(p1_turned, 1)

            def turn_og(c):
                for t in range(T):
                    pe.wait_ge(o_gated, c * T + t + 1)
                    turn_rows(z_silu, t, 4, banks[TURNED + t], og_turned)

            def attn1_slot(i, n, steps, turn):
                if n == 1:
                    turn_q1(i)
                for k, at in enumerate(steps):
                    if at == n:
                        attn1(i, k)
                if n == turn:
                    turn_og(i)

            pe.wait_ge(k1_ready, T)
            with pe.Fori(0, CHUNKS - 1) as i:
                for s in range(UPT):
                    chunk_unit(i * 2 + TURN_ZQ, s, PAIR_A, i + 1)
                    attn1_slot(i, s, STEPS, SLOT_TURN)
                for s in range(UPT):
                    chunk_unit(i * 2 + TURN_ZQ + 1, s, PAIR_B, i + 1)
                    attn1_slot(i, UPT + s, STEPS, SLOT_TURN)
            last = CHUNKS - 1
            for s in range(UPT):
                chunk_unit(TURN_Z_LAST, s, PAIR_A, CHUNKS)
                attn1_slot(last, s, STEPS_LAST, TURN_LAST)
            for n in range(CHUNKS):
                for s in range(UPT):
                    chunk_unit(TURN_OUT + n, s, (n + 1) % 2, CHUNKS + (n + 1) // 2, H_OUT)
                    if n == 0:
                        attn1_slot(last, UPT + s, STEPS_LAST, TURN_LAST)
                    if n == CHUNKS - 1 and s in SCALE_SLOTS:
                        scale_rows(1, SCALE_SLOTS.index(s))

            ki_t = v2[:, 0:1, 0:SEQ]

            def turn_index(n, blocks):
                for t in range(T):
                    pe.wait_ge(rot_ready, n * T + t + 1)
                    turn_rows(rot_key if n == 1 else rot, t, blocks, banks[TURNED + t], i_turned)

            def index_scores(h):
                if h >= 2:
                    pe.wait_ge(i_relu, h - 1)
                if h % 8 == 0:
                    pe.wait_ge(i_t_ready, 2 * T + h // 8 * T)
                lane = slice((h % 2) * IDX_DIM, (h % 2 + 1) * IDX_DIM)
                q = (q2_t, k2_t)[h // 8][lane, h // 2 % 4, :]
                keys = ki_t[lane, 0, :]
                pe.matmul(banks[SCORES + h % 2][:, 0:P], q[:, 0:P], keys[:, 0:P], start=True, stop=True)
                pe.matmul(banks[SCORES + h % 2][:, P:MASK_W], q[:, P:SEQ], keys, start=True, stop=True)\
                    .then_inc(i_scores, 1)

            norm_turn(1, TURN_QI, PAIR_A, 7, H_NORM1)
            for s in range(2 * UPT):
                p, use, cols = (PAIR_A, 8, CH) if s % 2 else (PAIR_B, 6, KI_COLS)
                unit(TURN_KI, s, h_hi, h_lo, KG * (s // 2), p, use, s < 2, s >= 2 * UPT - 2, cols)
                if s == 6:
                    turn_index(0, 4)

            def turn_qk(n):
                for t in range(T):
                    pe.wait_ge(rot_ready, (n + 3) * T + t + 1)
                    turn_rows(rot, t, 4, banks[TURNED + t], qk_turned)

            def attn2(g, k):
                h = g * 4 + k
                if k < 4:
                    if k == 0:
                        pe.wait_ge(qk_ready, (g + 1) * 2 * T)
                        for t in range(T):
                            pe.wait_ge(evicted[PAIR_B][t], g * 2 + 9)
                    bank = banks[SCORES + k % 2]
                    pe.matmul(bank[:, 0:P], q2_t[:, k, 0:P], k2_t[:, k, 0:P], start=True, stop=True)
                    pe.matmul(bank[:, P:MASK_W], q2_t[:, k, P:SEQ], k2_t[:, k, :], start=True, stop=True)\
                        .then_inc(s2_ready, 1)
                if k >= 2:
                    pe.wait_ge(p2_t_ready, h - 1)
                    pe.wait_ge(o2_kept, h - 1)
                    head = slice((k - 2) * DH_2, (k - 1) * DH_2)
                    pe.matmul(banks[OUTS][:, 0:SEQ], v2[:, 0, head], p2_t[:, 0:SEQ], start=True, stop=False)
                    pe.matmul(banks[OUTS][:, P:SEQ], v2[:, 1, head], p2_t[:, SEQ:MASK_W], start=False, stop=True)\
                        .then_inc(o2_ready, 1)
                if 1 <= k <= 4:
                    pe.wait_ge(p2_normed, h)
                    for b in range(3):
                        ins = pe.transpose(banks[TURNED][:, b * P:(b + 1) * P], s2[:, (k - 1) % 2, b * P:(b + 1) * P],
                                           ident)
                    ins.then_inc(p2_turned, 1)

            def group_rest(g):
                for s in range(UPT):
                    chunk_unit(g * 3 + TURN_GRP + 1, s, PAIR_A, g + 9)
                    if s == 3:
                        pe.wait_ge(o2_kept, g * 4 + 1)
                        turn_qk(g * 2)
                for s in range(UPT):
                    chunk_unit(g * 3 + TURN_GRP + 2, s, PAIR_B, g * 2 + 8)
                    if s == 3:
                        turn_qk(g * 2 + 1)

            def attn2_turn(g, turn, p, use):
                for s in range(UPT):
                    chunk_unit(turn, s, p, use)
                    if 1 <= s <= 6:
                        attn2(g, s - 1)

            for s in range(UPT):
                chunk_unit(TURN_GRP, s, PAIR_B, 7)
                if s == 1:
                    pe.wait_ge(i_t_ready, T)
                    turn_index(1, 1)
                if s == 3:
                    turn_index(2, 4)
                for h in INDEX_AT.get(s, ()):
                    index_scores(h)
            pe.wait_ge(i_relu, IDX_HEADS)
            group_rest(0)
            with pe.Fori(1, 4) as g:
                attn2_turn(g - 1, g * 3 + TURN_GRP, PAIR_B, g * 2 + 7)
                group_rest(g)

            attn2_turn(3, TURN_GATE, PAIR_A, 13)
            pe.wait_ge(o2_kept, 2 * HEADS_2 + 1)
            for s in range(UPT):
                chunk_unit(TURN_GATE + 1, s, PAIR_B, 15)
                if s < 4:
                    rows(96, s, SCORES + s)

            def out_units(c):
                for s in range(UPT):
                    p = s // (UPT // 2)
                    at = s % (UPT // 2)
                    unit(c * 3 + TURN_YAB, s, o_hi, o_lo, KG * s, p, c * 2 + 14 + 2 * p, at == 0, at == UPT // 2 - 1)

            def turn_y(c):
                for t in range(T):
                    pe.wait_ge(y_tok_ready, c * T + T + t + 1)
                    turn_rows(y_tok, t, 4, banks[TURNED + t], y_turned)

            with pe.Fori(0, D // CH - 1) as c:
                out_units(c)
                for s in range(UPT):
                    chunk_unit(c * 3 + TURN_YAB + 1, s, PAIR_A, c * 2 + 15)
                    if s == 5:
                        turn_y(c)
                for s in range(UPT):
                    chunk_unit(c * 3 + TURN_YAB + 2, s, PAIR_B, c * 2 + 17)
            out_units(CHUNKS - 1)
            for n in range(CHUNKS):
                for s in range(UPT):
                    chunk_unit(TURN_WO + n, s, n % 2, 21 + n // 2 + 2 * (n % 2), H_WO)
                    if n == 0 and s == 1:
                        turn_y(CHUNKS - 1)
                    if n == CHUNKS - 1 and s in SCALE_SLOTS:
                        scale_rows(2, SCALE_SLOTS.index(s))

            def turn_f(c):
                for t in range(T):
                    pe.wait_ge(f_sq, c * T + t + 1)
                    turn_rows(f_tok, t, 4, banks[TURNED + t], f_turned)

            def ff1_turn(c, p, use):
                for s in range(UPT):
                    chunk_unit(c + TURN_FF1, s, p, use)
                    if s == 3:
                        turn_f(c - 1)

            norm_turn(2, TURN_FF1, PAIR_A, 23, H_NORM2)
            with pe.Fori(0, 7) as it:
                for b in range(2):
                    ff1_turn(it * 2 + 1 + b, 1 - b, it + 25 - b)
            for s in range(UPT):
                chunk_unit(TURN_FF2 - 1, s, PAIR_B, 32)
                if s == 3:
                    turn_f(14)
                if s in (4, 6):
                    if s == 6:
                        pe.wait_ge(gain_ready, 6)
                    for q in (0, 1):
                        rows(192, s - 4 + q, SCORES + q)

            def ff2_half(s, t, b, start=False, stop=False):
                k = 4 * b + s // 2
                for cc in range(KG):
                    w = slice(cc * CH, (cc + 1) * CH)
                    mm = three(banks[t * CHUNKS + s % 2 * KG + cc][:, :], h_hi[:, k, t * P:(t + 1) * P],
                               h_lo[:, k, t * P:(t + 1) * P], w_hi[:, s % SLOTS, w], w_lo[:, s % SLOTS, w],
                               start and s < 2, stop and s >= UPT - 2)
                return mm

            def ff2_turn(c, b, first_unit=0, stop=False):
                pe.wait_ge(f_lo_ready, c + 1)
                for s in range(first_unit, UPT):
                    pe.wait_ge(lo_ready, unit_of(c + TURN_FF2, s) + 1)
                    for t in range(T):
                        mm = ff2_half(s, t, b, stop=stop)
                        if stop and s >= UPT - 2 and t == 0:
                            mm.then_inc(y_last, 1)
                    if stop and s >= UPT - 2:
                        mm.then_inc(y_last, 1)
                    else:
                        mm.then_inc(mm_done, 1)

            pe.wait_ge(f_lo_ready, 1)
            for t in range(T):
                pe.wait_ge(evicted[PAIR_A][t], 31)
            pe.wait_ge(lo_ready, unit_of(TURN_FF2, 0) + 1)
            ff2_half(0, 0, 0, start=True)
            turn_f(15)
            pe.wait_ge(lo_ready, unit_of(TURN_FF2, 1) + 1)
            for t in range(T):
                pe.wait_ge(evicted[PAIR_B][t], 33)
            ff2_half(1, 0, 0, start=True)
            pe.wait_ge(gain_ready, 8)
            ff2_half(0, 1, 0, start=True).then_inc(mm_done, 1)
            for t in range(T):
                pe.wait_ge(f_t_ready[t], D_FF // CH)
            ff2_half(1, 1, 0, start=True).then_inc(mm_done, 1)
            ff2_turn(0, 0, 2)
            ff2_turn(1, 1)
            with pe.Fori(1, 7) as it:
                for b in range(2):
                    ff2_turn(it * 2 + b, b)
            ff2_turn(14, 0)
            ff2_turn(15, 1, stop=True)


_OUT = (1, SEQ, D)


def kernel(x, g_pre, g_post, w_in_a, w_out_a, sinks_a, w_in_b, w_out_b, w_in_c, b_f_c, w_out_c, c_2,
           w_ada_2, b_ada_2, g_pre_mix_2, g_post_mix_2, w_in_2, w_moba_out_2, w_dsa_out_2, w_o_2,
           g_pre_ffn_2, g_post_ffn_2, w_ff1_2, w_ff2_2):
    import concourse.bacc as bacc
    from concourse.bass_utils import run_bass_kernel_spmd

    def columns(v):
        return np.asarray(v).reshape(KT, P).T

    arrays = {
        "x": np.asarray(x)[0],
        "w_in_a": np.asarray(w_in_a)[0],
        "w_out_a": np.asarray(w_out_a)[0],
        "w_ada": np.asarray(w_ada_2)[0],
        "w_in_2": np.asarray(w_in_2)[0],
        "w_moba": np.asarray(w_moba_out_2)[0],
        "w_dsa": np.asarray(w_dsa_out_2)[0],
        "w_o": np.asarray(w_o_2)[0],
        "w_ff1": np.asarray(w_ff1_2)[0],
        "w_ff2": np.asarray(w_ff2_2)[0],
        "b_ada": np.asarray(b_ada_2),
        "g_post": np.asarray(g_post)[0],
        "g_post_mix": np.asarray(g_post_mix_2)[0],
        "g_post_ffn": np.asarray(g_post_ffn_2)[0],
        "sinks": np.asarray(sinks_a)[0],
        "vecs": np.concatenate([columns(v) for v in (g_pre, g_pre_mix_2, g_pre_ffn_2, c_2)], axis=1),
        "consts": shape_constants(),
    }
    arrays = {n: np.ascontiguousarray(a) for n, a in arrays.items()}
    nc = bacc.Bacc("TRN2", target_bir_lowering=False, num_devices=1)
    args = [nc.dram_tensor("in_" + n, a.shape, F32, kind="ExternalInput").ap() for n, a in arrays.items()]
    out = nc.dram_tensor("out", (SEQ, D), F32, kind="ExternalOutput").ap()
    two_block_kernel(nc, *args, out)
    got = run_bass_kernel_spmd(nc, [{"in_" + n: a for n, a in arrays.items()}], core_ids=[0]).results[0]["out"]
    return got.reshape(_OUT)
```

```python
from contextlib import ExitStack

import numpy as np

import concourse.bass as bass
from concourse import mybir

F32 = mybir.dt.float32
F32R = mybir.dt.float32r
ALU = mybir.AluOpType
ACT = mybir.ActivationFunctionType
AX = mybir.AxisListType

P = 128
D = 2048
SEQ = 256
T = SEQ // P
KT = D // P
CH = 512
KG = 2
UNIT = KG * CH
SLOTS = 4
UPT = KT // KG
AHEAD = 3
EPS = 1e-6

HEADS_A = 32
DH_A = 64
KV_A = 4
GROUP_A = HEADS_A // KV_A
KV_COLS = KV_A * DH_A
WINDOW = 128
MASK_W = P + SEQ

HEADS_2 = 8
DH_2 = 128
IDX_HEADS = 16
IDX_DIM = 64
TOPK = min(256, SEQ // 4)
D_FF = 4 * D
W2 = HEADS_2 * DH_2
COL_QI = 6 * W2
COL_KI = COL_QI + IDX_HEADS * IDX_DIM
KI_COLS = IDX_DIM + IDX_HEADS
COL_GA = COL_KI + KI_COLS
COL_GB = COL_GA + D
SCALE_A = DH_A ** -0.5
SCALE_2 = DH_2 ** -0.5
IDX_SCALE = (IDX_DIM ** -0.5) * (IDX_HEADS ** -0.5)

MASKED = -1e30
FAR = 1e34
LOWEST = -3.4e38
PICKED = -3.0e38
PICKED_BELOW = -2.0e38

TURN_KV, TURN_Q, TURN_ZQ, TURN_Z_LAST, TURN_OUT = 0, 1, 2, 8, 9
TURN_QI, TURN_KI, TURN_QI_2, TURN_GRP, TURN_GATE, TURN_YAB, TURN_YAB_LAST = 13, 14, 15, 16, 28, 30, 39
TURN_WO, TURN_FF1, TURN_FF2, TURNS = 40, 44, 60, 76
CHUNK_GATE, CHUNK_YAB, CHUNK_WO, CHUNK_FF1 = 28, 30, 44, 48
CHUNKS = D // CH

STEPS = (2, 3, 4, 5, 6, 7, 8, 9, 10, 11)
SLOT_SUMS, SLOT_GATE, SLOT_TURN = 10, 12, 14
STEPS_LAST = (2, 3, 4, 5, 6, 7, 8, 9, 10, 10)
SUMS_LAST, GATE_LAST, TURN_LAST = 10, 10, 12
INDEX_AT = {2: (0, 1, 2), 3: (3, 4, 5), 4: (6, 7), 5: (8, 9, 10), 6: (11, 12, 13), 7: (14, 15)}

C_ID = 0
C_ONE = C_ID + P
C_DIST = C_ONE + P
C_CAUSAL = C_DIST + MASK_W
C_SLOPE = C_CAUSAL + MASK_W
C_COS = C_SLOPE + HEADS_A
C_SIN = C_COS + T * DH_2 // 2
C_COSI = C_SIN + T * DH_2 // 2
C_SINI = C_COSI + T * IDX_DIM // 2
CONSTS = C_SINI + T * IDX_DIM // 2

V_PRE, V_MIX, V_FFN, V_C = 0, KT, 2 * KT, 3 * KT
VECS = 4 * KT

SH1, SC1, GT1, SH2, SC2, GT2 = range(6)


def shape_constants():
    out = np.zeros((P, CONSTS), np.float32)
    out[:, C_ID:C_ID + P] = np.eye(P)
    q = np.arange(P)[:, None]
    query = np.concatenate([np.broadcast_to(q, (P, P)), np.broadcast_to(q + P, (P, SEQ))], axis=1)
    key = np.concatenate([np.arange(P), np.arange(SEQ)])[None, :]
    dist = query - key
    seen = (dist >= 0) & (dist < WINDOW)
    out[:, C_DIST:C_DIST + MASK_W] = np.where(seen, -dist / SCALE_A, -FAR)
    out[:, C_CAUSAL:C_CAUSAL + MASK_W] = np.where(dist >= 0, 0.0, MASKED)
    slopes = 2.0 ** (-8.0 * np.arange(1, HEADS_A + 1, dtype=np.float32) / HEADS_A)
    out[:, C_SLOPE:C_SLOPE + HEADS_A] = slopes.astype(np.float32)[None]
    for half, c_cos, c_sin in ((DH_2 // 2, C_COS, C_SIN), (IDX_DIM // 2, C_COSI, C_SINI)):
        power = -np.arange(half, dtype=np.float32) / np.float32(half)
        freq = np.power(10000.0, power.astype(np.float64)).astype(np.float32)
        angle = (np.arange(SEQ, dtype=np.float32)[:, None] * freq[None]).astype(np.float32)
        for c, table in ((c_cos, np.cos(angle)), (c_sin, np.sin(angle))):
            out[:, c:c + T * half] = table.astype(np.float32).reshape(T, P, half).transpose(1, 0, 2).reshape(P, -1)
    out[:, C_ONE:C_ONE + P] = 1.0
    return out


def two_block_kernel(nc, x_in, w_in_a, w_out_a, w_ada, w_in_2, w_moba, w_dsa, w_o, w_ff1, w_ff2,
                     b_ada, g_post, g_post_mix, g_post_ffn, sinks, vecs_in, consts_in, out):
    ctx = ExitStack()
    with ctx:
        def sb(name, shape, dt=F32, on=ctx):
            return on.enter_context(nc.sbuf_tensor(name, shape, dt))

        def sem(name):
            return ctx.enter_context(nc.semaphore(name))

        raw = sb("raw", [P, SLOTS, UNIT])
        w_hi = sb("w_hi", [P, SLOTS, UNIT], F32R)
        w_lo = sb("w_lo", [P, SLOTS, UNIT], F32R)
        x = sb("x", [P, T, D])
        h_hi = sb("h_hi", [P, KT, SEQ], F32R)
        h_lo = sb("h_lo", [P, KT, SEQ], F32R)
        post_gain = sb("post_gain", [P, D])
        acc_a = sb("acc_a", [P, D])
        acc_b = sb("acc_b", [P, D])
        ada_raw = sb("ada_raw", [P, 2, D // 2])
        consts = sb("consts", [P, CONSTS])
        vecs = sb("vecs", [P, VECS])
        cond = sb("cond", [P, KT])
        pre_gain = sb("pre_gain", [P, KT])
        pre_shift = sb("pre_shift", [P, KT])
        y_sq = sb("y_sq", [P, T, D // CH])
        y_var = sb("y_var", [P, T])
        y_rstd = sb("y_rstd", [P, T])
        x_sq_part = sb("x_sq_part", [P, T, CHUNKS])
        x_sq = sb("x_sq", [P, T])
        x_rstd = sb("x_rstd", [P, T])
        root_one = sb("root_one", [P, 1])
        ones_r = sb("ones_r", [P, P], F32R)
        sum_hi = sb("sum_hi", [P, 2, CH], F32R)
        sum_lo = sb("sum_lo", [P, CH], F32R)
        rstd_diag = sb("rstd_diag", [P, T, P])
        rstd_row = sb("rstd_row", [P, SEQ])

        with ExitStack() as a:
            o_gated_t = sb("o_gated_t", [P, KT, SEQ], on=a)
            o = sb("o", [P, T, CH], on=a)
            v1 = sb("v1", [P, T, KV_COLS], on=a)
            k1_t = sb("k1_t", [P, KV_A, SEQ], on=a)
            k1_cur = sb("k1_cur", [P, SEQ], on=a)
            v1_cur = sb("v1_cur", [P, T, DH_A], on=a)
            q1_tok = sb("q1_tok", [P, T, CH], on=a)
            q1_t = sb("q1_t", [P, GROUP_A // 2, SEQ], on=a)
            bias1 = sb("bias1", [P, 2, MASK_W], on=a)
            s1 = sb("s1", [P, 2, MASK_W], on=a)
            p1_t = sb("p1_t", [P, MASK_W], on=a)
            z_silu = sb("z_silu", [P, T, CH], on=a)
            slope_cur = sb("slope_cur", [P, GROUP_A], on=a)
            sink_cur = sb("sink_cur", [P, GROUP_A], on=a)
            sink = sb("sink", [P, HEADS_A], on=a)
            sink_sc = sb("sink_sc", [P, HEADS_A], on=a)
            sink_raw_cur = sb("sink_raw_cur", [P, GROUP_A], on=a)
            m1 = sb("m1", [P, 2, T], on=a)
            sink_e = sb("sink_e", [P, GROUP_A, T], on=a)
            neg_cur = sb("neg_cur", [P, GROUP_A, T], on=a)
            l_cur = sb("l_cur", [P, GROUP_A, T], on=a)
        with ExitStack() as a:
            sb("pad_o_gated_t", [P, KT, SEQ], on=a)
            y1 = sb("y1", [P, T, D], on=a)
            sq1 = sb("sq1", [P, CH], on=a)
        with ExitStack() as a:
            o_hi = sb("o_hi", [P, 2 * HEADS_2, SEQ], F32R, on=a)
            o_lo = sb("o_lo", [P, 2 * HEADS_2, SEQ], F32R, on=a)
            with ExitStack() as a2:
                rope_a = sb("rope_a", [P, CH], on=a2)
                rope_b = sb("rope_b", [P, CH], on=a2)
                rot = sb("rot", [P, T, CH], on=a2)
                rot_key = sb("rot_key", [P, T, 2 * IDX_DIM], on=a2)
                q2_t = sb("q2_t", [P, 4, SEQ], on=a2)
                k2_t = sb("k2_t", [P, 4, SEQ], on=a2)
                v2 = sb("v2", [P, T, CH], on=a2)
                s2 = sb("s2", [P, 2, MASK_W], on=a2)
                p2_t = sb("p2_t", [P, MASK_W], on=a2)
                mask_cur = sb("mask_cur", [P, MASK_W], on=a2)
                masks = sb("masks", [P, 2, MASK_W], on=a2)
                score = sb("score", [P, MASK_W], on=a2)
                w_idx = sb("w_idx", [P, T, IDX_HEADS], on=a2)
                top8 = sb("top8", [P, T, 8], on=a2)
                m2 = sb("m2", [P, 2, T], on=a2)
                l2 = sb("l2", [P, 2, T], on=a2)
                l2_inv = sb("l2_inv", [P, T], on=a2)
            with ExitStack() as a2:
                y_t = sb("y_t", [P, KT, SEQ], on=a2)
                gate_a = sb("gate_a", [P, T, CH], on=a2)
                gate_b = sb("gate_b", [P, T, CH], on=a2)
                y_tok = sb("y_tok", [P, T, CH], on=a2)
        with ExitStack() as a:
            y2 = sb("y2", [P, T, D], on=a)
            sq2 = sb("sq2", [P, CH], on=a)
        with ExitStack() as a:
            f_t = sb("f_t", [P, D_FF // P, SEQ], on=a)
        f_tok = acc_b[:, 0:T * CH].rearrange("p (t n) -> p t n", t=T)
        norm_tmp = post_gain[:, 0:2 * KG * SEQ].rearrange("p (b n) -> p b n", b=2)

        ident = consts[:, C_ID:C_ID + P]
        dist8 = consts[:, C_DIST:C_DIST + MASK_W]
        causal = consts[:, C_CAUSAL:C_CAUSAL + MASK_W]
        ones = consts[:, C_ONE:C_ONE + P]

        banks = [ctx.enter_context(nc.psum_tensor(f"bank{n}", [P, CH], F32)) for n in range(8)]
        PAIR_A, PAIR_B = 0, 1
        pair = [banks[0:2], banks[2:4]]
        SCORES, TURNED, OUTS = 4, 6, 7

        raw_loaded = [sem(f"raw_loaded{s}") for s in range(SLOTS)]
        hi_ready = sem("hi_ready")
        lo_ready = sem("lo_ready")
        mm_done = sem("mm_done")
        front_done = sem("front_done")
        evicted = [[sem(f"evicted_{'ab'[p]}{t}") for t in range(T)] for p in range(2)]
        x_loaded = [sem(f"x_loaded{c}") for c in range(CHUNKS)]
        ident_loaded = sem("ident_loaded")
        consts_loaded = sem("consts_loaded")
        vecs_loaded = sem("vecs_loaded")
        sink_loaded = sem("sink_loaded")
        gain_loaded = [sem(f"gain_loaded{n}") for n in range(3)]
        acc_zero = sem("acc_zero")
        acc_init = [sem(f"acc_init{n}") for n in range(6)]
        ada_loaded = [sem("ada_loaded0"), sem("ada_loaded1")]
        ada_done = sem("ada_done")
        cond_sig = sem("cond_sig")
        cond_ready = sem("cond_ready")
        ones_ready = sem("ones_ready")
        sum_hi_ready = sem("sum_hi_ready")
        sum_lo_ready = sem("sum_lo_ready")
        mod_rows = sem("mod_rows")
        mod_picked = sem("mod_picked")
        mod_ready = sem("mod_ready")
        gain_ready = sem("gain_ready")
        y_squared = sem("y_squared")
        y_last = sem("y_last")
        y_scaled = sem("y_scaled")
        y_stat = sem("y_stat")
        y_root = sem("y_root")
        x_new = sem("x_new")
        x_squared = sem("x_squared")
        x_stat = sem("x_stat")
        x_root = sem("x_root")
        rstd_spread = sem("rstd_spread")
        rstd_row_ready = sem("rstd_row_ready")
        n_turned = sem("n_turned")
        n_scaled = sem("n_scaled")
        n_rounded = sem("n_rounded")
        h_hi_ready = sem("h_hi_ready")
        h_lo_ready = sem("h_lo_ready")
        kv_tok = sem("kv_tok")
        k1_turned = sem("k1_turned")
        k1_ready = sem("k1_ready")
        q1_turned = sem("q1_turned")
        q1_t_ready = sem("q1_t_ready")
        kv_cur_ready = sem("kv_cur_ready")
        heads_cur = sem("heads_cur")
        sink_scaled = sem("sink_scaled")
        bias_ready = sem("bias_ready")
        s1_ready = sem("s1_ready")
        s1_seen = sem("s1_seen")
        s1_masked = sem("s1_masked")
        neg1_ready = sem("neg1_ready")
        p1_ready = sem("p1_ready")
        p1_turned = sem("p1_turned")
        p1_t_ready = sem("p1_t_ready")
        o1_ready = sem("o1_ready")
        o1_kept = sem("o1_kept")
        sink_exp = sem("sink_exp")
        l1_step = sem("l1_step")
        z_sig = sem("z_sig")
        o_step = sem("o_step")
        o_gated = sem("o_gated")
        og_turned = sem("og_turned")
        og_ready = sem("og_ready")
        rot_ready = sem("rot_ready")
        w_idx_ready = sem("w_idx_ready")
        i_turned = sem("i_turned")
        i_t_ready = sem("i_t_ready")
        i_scores = sem("i_scores")
        i_relu = sem("i_relu")
        i_added = sem("i_added")
        top_step = sem("top_step")
        mask_ready = sem("mask_ready")
        qk_turned = sem("qk_turned")
        qk_ready = sem("qk_ready")
        mask_set = sem("mask_set")
        s2_ready = sem("s2_ready")
        s2_seen = sem("s2_seen")
        s2_masked = sem("s2_masked")
        neg2_ready = sem("neg2_ready")
        p2_ready = sem("p2_ready")
        l2_ready = sem("l2_ready")
        p2_normed = sem("p2_normed")
        p2_turned = sem("p2_turned")
        p2_t_ready = sem("p2_t_ready")
        o2_ready = sem("o2_ready")
        o2_hi = sem("o2_hi")
        o2_kept = sem("o2_kept")
        y_tok_ready = sem("y_tok_ready")
        y_turned = sem("y_turned")
        y_t_ready = sem("y_t_ready")
        f_sq = sem("f_sq")
        f_turned = sem("f_turned")
        f_t_ready = [sem(f"f_t_ready{t}") for t in range(T)]
        f_hi_ready = sem("f_hi_ready")
        f_lo_ready = sem("f_lo_ready")
        stored = sem("stored")

        H_NORM0, H_OUT, H_NORM1, H_WO, H_NORM2 = range(0, 5 * UPT, UPT)

        MOD_UNITS = (None, (44, 64), (140, 160))
        SUMS_MOD = (None, 0, 12)
        SUMS_GATE = (8, 20)
        GATE_UNITS = (96, 192)
        ADA_OUT = (range(4, 8), range(1, 8), range(0, 5))
        ADA_WO = (range(1, 7), range(1, 7), range(0, 4))
        ADA_OUT_UNITS = [(n, s) for n, slots in enumerate(ADA_OUT) for s in slots]
        ADA_WO_UNITS = [(n, s) for n, slots in enumerate(ADA_WO) for s in slots]
        TILE_FROM = UPT - SLOTS

        def of_scale(r, j):
            return (j < 4) == (r == 1)

        def mod_quarter(r, j):
            return (acc_a if of_scale(r, j) else acc_b)[:, j % 4 * CH:(j % 4 + 1) * CH]

        def gate_quarter(q):
            return acc_a[:, q * CH:(q + 1) * CH]

        X_STATS = (0, 3, 7)

        LAST_BANKS = [(t, half * KG + c) for t in range(T) for half in range(2) for c in range(KG)]

        w_a = w_in_a.rearrange("(k p) n -> p k n", p=P)
        w_oa = w_out_a.rearrange("(k p) n -> p k n", p=P)
        w_2 = w_in_2.rearrange("(k p) n -> p k n", p=P)
        w_m = w_moba.rearrange("(k p) n -> p k n", p=P)
        w_d = w_dsa.rearrange("(k p) n -> p k n", p=P)
        w_oo = w_o.rearrange("(k p) n -> p k n", p=P)
        w_f1 = w_ff1.rearrange("(k p) n -> p k n", p=P)
        w_f2 = w_ff2.rearrange("(k p) n -> p k n", p=P)
        w_ad = w_ada.rearrange("(k p) n -> p k n", p=P)

        def two(ap, k=2):
            return ap.rearrange("p (k n) -> p k n", k=k)

        def unit_of(turn, s):
            return turn * UPT + s

        def used(buf, turn, s):
            if isinstance(turn, int) and TURN_KI <= turn <= TURN_QI_2 and s % 2 == 0:
                return two(buf[:, s % SLOTS, :])[:, :, 0:KI_COLS]
            return buf[:, s % SLOTS, :]

        block = ctx.enter_context(nc.Block())

        @block.sync
        def _(sp):
            def load(turn, s, src, first=False):
                if not first:
                    sp.wait_ge(lo_ready, unit_of(turn, s) - SLOTS + 1)
                dst = two(raw[:, s % SLOTS, :], src.shape[1])[:, :, 0:src.shape[2]]
                sp.dma_start(dst, src).then_inc(raw_loaded[s % SLOTS], 16)

            def load_chunk(turn, w, col):
                for s in range(UPT):
                    load(turn, s, w[:, KG * s:KG * s + KG, bass.ds(col, CH)])

            def load_pair(turn, col):
                for s in range(UPT):
                    w, k = (w_m, s) if s < UPT // 2 else (w_d, s - UPT // 2)
                    load(turn, s, w[:, KG * k:KG * k + KG, bass.ds(col, CH)])

            x_tiles = x_in.rearrange("(t p) n -> p t n", p=P)

            def load_x(c):
                sp.dma_start(x[:, :, c * CH:(c + 1) * CH], x_tiles[:, :, c * CH:(c + 1) * CH])\
                    .then_inc(x_loaded[c], 16)

            for s in range(UPT):
                if s in (0, 1, 3, 4):
                    load_x((0, 1, 3, 4).index(s))
                if s == SLOTS:
                    sp.dma_start(consts[:, C_DIST:CONSTS], consts_in[:, C_DIST:CONSTS]).then_inc(consts_loaded, 16)
                load(TURN_KV, s, w_a[:, KG * s:KG * s + KG, D:D + CH], s < SLOTS)
            load_chunk(TURN_Q, w_a, 0)
            with sp.Fori(0, CHUNKS - 1) as i:
                load_chunk(i * 2 + TURN_ZQ, w_a, i * CH + D + 2 * KV_COLS)
                load_chunk(i * 2 + TURN_ZQ + 1, w_a, i * CH + CH)
            load_chunk(TURN_Z_LAST, w_a, 2 * D + 2 * KV_COLS - CH)
            with sp.Fori(0, CHUNKS) as i:
                load_chunk(i + TURN_OUT, w_oa, i * CH)
            load_chunk(TURN_QI, w_2, COL_QI)
            for s in range(2 * UPT):
                k = KG * (s // 2)
                col, cols = (COL_QI + CH, CH) if s % 2 else (COL_KI, KI_COLS)
                load(TURN_KI, s, w_2[:, k:k + KG, col:col + cols])
            for half in range(2):
                with sp.Fori(0, 2) as b:
                    for part in range(3):
                        load_chunk((b + 2 * half) * 3 + TURN_GRP + part, w_2,
                                   b * CH + (half * 3 + part) * W2)
            load_chunk(TURN_GATE, w_2, COL_GA)
            load_chunk(TURN_GATE + 1, w_2, COL_GB)
            with sp.Fori(0, D // CH - 1) as c:
                load_pair(c * 3 + TURN_YAB, c * CH)
                load_chunk(c * 3 + TURN_YAB + 1, w_2, c * CH + COL_GA + CH)
                load_chunk(c * 3 + TURN_YAB + 2, w_2, c * CH + COL_GB + CH)
            load_pair(TURN_YAB_LAST, D - CH)
            with sp.Fori(0, D // CH) as i:
                load_chunk(i + TURN_WO, w_oo, i * CH)
            with sp.Fori(0, D_FF // CH) as i:
                load_chunk(i + TURN_FF1, w_f1, i * CH)
            with sp.Fori(0, TURNS - TURN_FF2) as i:
                for s in range(UPT):
                    load(i + TURN_FF2, s, w_f2[:, bass.ds(i * 4 + s // 2, 1), (s % 2) * UNIT:(s % 2 + 1) * UNIT])
            out_tiles = out.rearrange("(t p) n -> p t n", p=P)
            for t in range(T):
                for c in range(CHUNKS):
                    sp.wait_ge(x_new, (2 * T + t) * CHUNKS + c + 1)
                    sp.dma_start(out_tiles[:, t, c * CH:(c + 1) * CH], x[:, t, c * CH:(c + 1) * CH]).then_inc(stored, 16)
            sp.wait_ge(stored, 16 * T * CHUNKS)

        @block.gpsimd
        def _(pool):
            def init_acc(acc, part, n):
                pool.memset(acc[:, :], 0.0).then_inc(acc_zero, 1)
                pool.wait_ge(acc_zero, n + 1)
                pool.dma_start(acc[0:1, :], b_ada[:, part * D:(part + 1) * D]).then_inc(acc_init[n], 16)

            def load_ada(m, slot, part, k, half, first=False):
                if not first:
                    pool.wait_ge(ada_done, m - 1)
                col = part * D + half * (D // 2)
                pool.dma_start(two(ada_raw[:, slot, :], 1), w_ad[:, bass.ds(k, 1), col:col + D // 2])\
                    .then_inc(ada_loaded[slot], 16)

            def load_tiles(m, part, k, tiles=4, first=False):
                for n in range(2 * tiles):
                    load_ada(m + n, n % 2, part, k + n // 2, n % 2, first and n < 2)

            def bias(i, j):
                pool.wait_ge(s1_masked, i * GROUP_A + j + 1)
                pool.tensor_tensor(bias1[:, j % 2, :], dist8, slope_cur[:, j:j + 1].to_broadcast([P, MASK_W]), ALU.mult)\
                    .then_inc(bias_ready, 1)

            def load_gain(n, g):
                pool.dma_start(post_gain[:, :], g.partition_broadcast(P)).then_inc(gain_loaded[n], 16)

            def ada_and_bias(i, m, part, k, units, slots, steps):
                for n in slots:
                    at = n % UPT - UPT + units
                    if 0 <= at and n - slots[0] < UPT:
                        load_ada(m + at, at % 2, part, k + at // 2, at % 2)
                    for j in range(GROUP_A):
                        if steps[j] == n + 1:
                            bias(i, j)

            def rest_of_sum(n, part):
                pool.wait_ge(sum_hi_ready, n + 1)
                if n:
                    pool.wait_ge(mod_rows, n)
                pool.tensor_tensor(sum_lo[:, :], part, sum_hi[:, n % 2, :].bitcast(F32), ALU.subtract)\
                    .then_inc(sum_lo_ready, 1)

            pool.dma_start(sink[:, :], sinks.partition_broadcast(P)).then_inc(sink_loaded, 16)
            init_acc(acc_a, SC1, 0)
            init_acc(acc_b, SH1, 1)
            pool.wait_ge(x_loaded[CHUNKS - 1], 16)
            load_tiles(0, SC1, 0, first=True)
            pool.wait_ge(consts_loaded, 16)
            with pool.Fori(0, CHUNKS - 1) as i:
                pool.wait_ge(heads_cur, i + 1)
                ada_and_bias(i, i * 12 + 8, SH1, i * 2, 4, range(UPT), STEPS)
                ada_and_bias(i, i * 12 + 12, SC1, i * 4 + 4, 8, range(UPT, 2 * UPT), STEPS)
            pool.wait_ge(heads_cur, CHUNKS)
            ada_and_bias(CHUNKS - 1, 44, SH1, 6, 4, range(2 * UPT), STEPS_LAST)
            pool.wait_ge(h_lo_ready, H_NORM0 + UPT)
            load_gain(0, g_post)
            for n in range(2 * UPT):
                if n == 2 * UPT - 1:
                    rest_of_sum(SUMS_MOD[1], mod_quarter(1, 0))
                load_ada(48 + n, n % 2, SH1, 8 + n // 2, n % 2)
            for j in range(1, 8):
                rest_of_sum(SUMS_MOD[1] + j, mod_quarter(1, j))
            pool.wait_ge(mod_ready, 1)
            init_acc(acc_a, GT1, 2)
            init_acc(acc_b, SH2, 3)
            pool.wait_ge(h_lo_ready, H_NORM1 + UPT)
            load_gain(1, g_post_mix)
            with pool.Fori(0, 4) as g:
                load_tiles(g * 8 + 64, GT1, g * 4)
            for n in range(UPT):
                load_ada(96 + n, n % 2, SH2, n // 2, n % 2)
                if 1 <= n <= 4:
                    rest_of_sum(SUMS_GATE[0] + n - 1, gate_quarter(n - 1))
            pool.wait_ge(gain_ready, 4)
            init_acc(acc_a, SC2, 4)
            with pool.Fori(0, CHUNKS - 1) as c:
                load_tiles(c * 12 + 104, SC2, c * 2, 2)
                load_tiles(c * 12 + 108, SH2, c * 4 + 4, 4)
            load_tiles(140, SC2, 6, 10)
            for j in range(8):
                rest_of_sum(SUMS_MOD[2] + j, mod_quarter(2, j))
            pool.wait_ge(mod_ready, 2)
            init_acc(acc_a, GT2, 5)
            pool.wait_ge(h_lo_ready, H_NORM2 + UPT)
            load_gain(2, g_post_ffn)
            with pool.Fori(0, 8) as it:
                load_tiles(it * 4 + 160, GT2, it * 2, 2)
            for q in range(4):
                rest_of_sum(SUMS_GATE[1] + q, gate_quarter(q))

        @block.scalar
        def _(act):
            def split(turn, s, first=False):
                turn, s = turn + s // UPT, s % UPT
                act.wait_ge(raw_loaded[s % SLOTS], (turn * (UPT // SLOTS) + s // SLOTS + 1) * 16)
                if not first:
                    act.wait_ge(mm_done, unit_of(turn, s) - SLOTS + 1)
                act.activation(used(w_hi, turn, s), used(raw, turn, s), ACT.Copy).then_inc(hi_ready, 1)

            def norm_squares(r, t, junk):
                for c in range(CHUNKS):
                    if r:
                        act.wait_ge(x_new, ((r - 1) * T + t) * CHUNKS + c + 1)
                    else:
                        act.wait_ge(x_loaded[c], 16)
                    act.activation(junk[:, t, c * CH:(c + 1) * CH], x[:, t, c * CH:(c + 1) * CH], ACT.Square,
                                   accum_out=x_sq_part[:, t, c:c + 1]).then_inc(x_squared, 1)

            def norm_root(r):
                act.wait_ge(x_stat, X_STATS[r] + 2)
                act.activation(x_rstd[:, :], x_sq[:, :], ACT.Sqrt).then_inc(x_root, 1)

            def norm_row(r):
                act.wait_ge(rstd_spread, r)
                act.activation(rstd_row[:, :], pair[PAIR_B][0][:, 0:SEQ], ACT.Copy).then_inc(rstd_row_ready, 1)

            def norm_hi(r, s):
                if r and s == 0:
                    act.wait_ge(mod_ready, r)
                for kk in range(KG):
                    k = KG * s + kk
                    act.wait_ge(n_scaled, KT * r + k + 1)
                    src = norm_tmp[:, s % 2, kk * SEQ:(kk + 1) * SEQ]
                    if r:
                        ins = act.activation(h_hi[:, k, :], src, ACT.Identity, bias=pre_shift[:, k:k + 1])
                    else:
                        ins = act.activation(h_hi[:, k, :], src, ACT.Copy)
                    ins.then_inc(n_rounded, 1)

            def norm_turn(r, turn, first=False):
                for s in range(2):
                    norm_hi(r, s)
                    if first:
                        split(turn, s, first)
                split(turn, 2, first)
                for s in range(UPT):
                    split(turn, s + AHEAD, first and s + AHEAD < SLOTS)
                    if s + 2 < UPT:
                        norm_hi(r, s + 2)

            def load_sqrt():
                act.activation(root_one[:, :], ones[:, 0:1], ACT.Sqrt)

            def round_sum(n, part, units):
                act.wait_ge(ada_done, units)
                if n >= 2:
                    act.wait_ge(mod_rows, n - 1)
                act.activation(sum_hi[:, n % 2, :], part, ACT.Copy).then_inc(sum_hi_ready, 1)

            def round_mod(r, j):
                round_sum(SUMS_MOD[r] + j, mod_quarter(r, j), MOD_UNITS[r][j // 4])

            def round_gate(n, q):
                round_sum(SUMS_GATE[n] + q, gate_quarter(q), GATE_UNITS[n])

            def y_roots(r, t):
                act.wait_ge(y_stat, 2 * ((r - 1) * T + t) + 2)
                act.activation(y_rstd[:, t:t + 1], y_var[:, t:t + 1], ACT.Sqrt).then_inc(y_root, 1)

            def residual_turn(r, turn, p, chunk, n, scratch, y):
                for s in range(TILE_FROM + 1):
                    split(turn, s + AHEAD)
                    if s < 3:
                        round_mod(r, s + 5)
                for t in range(T):
                    square_y(p, t, turn, chunk, n + t, CHUNKS - 1, scratch)
                    y_roots(r, t)
                    if t == 0:
                        split(turn, UPT)
                    norm_squares(r, t, y)
                norm_root(r)
                split(turn, UPT + 1)
                norm_row(r)

            def round_h(src, s):
                act.activation(h_hi[:, KG * s:KG * s + KG, :], src[:, KG * s:KG * s + KG, :], ACT.Copy)\
                    .then_inc(h_hi_ready, 1)

            def chunk_result(t, turn, chunk):
                if t == 0:
                    act.wait_ge(front_done, chunk + 1)
                else:
                    act.wait_ge(mm_done, unit_of(turn, UPT))

            def square_y(p, t, turn, chunk, n, col, scratch):
                chunk_result(t, turn, chunk)
                act.wait_ge(y_squared, n)
                act.activation(scratch[:, :], pair[p][t][:, :], ACT.Square, accum_out=y_sq[:, t, col:col + 1])\
                    .then_inc(y_squared, 1)

            act.dma_start(consts[:, 0:C_DIST], consts_in[:, 0:C_DIST]).then_inc(ident_loaded, 16)
            act.dma_start(vecs[:, :], vecs_in).then_inc(vecs_loaded, 16)
            act.sem_inc(y_squared, 1)
            act.sem_inc(og_ready, T)
            act.wait_ge(ident_loaded, 16)
            act.activation(ones_r[:, :], ones, ACT.Copy).then_inc(ones_ready, 1)
            act.wait_ge(vecs_loaded, 16)
            act.activation(cond[:, :], vecs[:, V_C:V_C + KT], ACT.Sigmoid).then_inc(cond_sig, 1)

            norm_turn(0, TURN_KV, first=True)
            for t in range(T):
                norm_squares(0, t, y1)
            norm_root(0)
            act.wait_ge(x_stat, 3)
            for t in range(T):
                chunk_result(t, TURN_KV, 0)
                kv = pair[PAIR_A][t][:, :]
                act.activation(q1_tok[:, t, :].rearrange("p (h r d) -> p h r d", h=KV_A, r=2),
                               kv[:, 0:KV_COLS].rearrange("p (h d) -> p h d", h=KV_A).unsqueeze(2)
                               .to_broadcast([P, KV_A, 2, DH_A]), ACT.Copy, scale=x_rstd[:, t:t + 1]).then_inc(kv_tok, 1)
                act.activation(v1[:, t, :], kv[:, KV_COLS:2 * KV_COLS], ACT.Copy, scale=x_rstd[:, t:t + 1])\
                    .then_inc(evicted[PAIR_A][t], 1)

            def keep_q1(turn):
                for t in range(T):
                    chunk_result(t, turn, turn)
                    act.activation(q1_tok[:, t, :], pair[PAIR_B][t][:, :], ACT.Copy, scale=x_rstd[:, t:t + 1])\
                        .then_inc(evicted[PAIR_B][t], 1)

            def turn_q1(i):
                act.wait_ge(k1_ready, T)
                for t in range(T):
                    act.wait_ge(evicted[PAIR_A][t], 1)
                    act.wait_ge(q1_turned, i * T + t + 1)
                    act.activation(q1_t[:, :, t * P:t * P + P], two(banks[TURNED + t][:, :], 4), ACT.Copy)\
                        .then_inc(q1_t_ready, 1)
                act.activation(k1_cur[:, :], k1_t[:, bass.ds(i, 1), :], ACT.Copy).then_inc(kv_cur_ready, 1)
                act.activation(v1_cur[:, :, :], v1[:, :, bass.ds(i * DH_A, DH_A)], ACT.Copy).then_inc(kv_cur_ready, 1)

            def attn1_out(i, b):
                act.wait_ge(o1_ready, i * 2 + b + 1)
                act.activation(o[:, :, b * (CH // 2):(b + 1) * (CH // 2)], two(banks[OUTS][:, :]), ACT.Copy)\
                    .then_inc(o1_kept, 1)

            def attn1(i, k):
                if k < GROUP_A:
                    act.wait_ge(neg1_ready, i * GROUP_A + k + 1)
                    act.activation(s1[:, k % 2, 0:P], s1[:, k % 2, 0:P], ACT.Exp, bias=neg_cur[:, k, 0:1], scale=SCALE_A,
                                   accum_out=l_cur[:, k, 0:1])
                    act.activation(s1[:, k % 2, P:MASK_W], s1[:, k % 2, P:MASK_W], ACT.Exp, bias=neg_cur[:, k, 1:2],
                                   scale=SCALE_A, accum_out=l_cur[:, k, 1:2]).then_inc(p1_ready, 1)
                if 1 <= k <= GROUP_A:
                    act.wait_ge(p1_turned, i * GROUP_A + k)
                    act.activation(p1_t[:, :], banks[TURNED][:, 0:MASK_W], ACT.Copy).then_inc(p1_t_ready, 1)
                if k == 5:
                    attn1_out(i, 0)

            def sink_share(i):
                act.wait_ge(l1_step, i * 3 + 1)
                act.activation(sink_e[:, :, :], sink_e[:, :, :], ACT.Exp).then_inc(sink_exp, 1)

            def z_sigmoid(c, turn):
                for t in range(T):
                    chunk_result(t, turn, turn)
                    act.wait_ge(og_turned, c * T + t + 1)
                    act.activation(z_silu[:, t, :], pair[PAIR_A][t][:, :], ACT.Sigmoid, scale=x_rstd[:, t:t + 1])\
                        .then_inc(z_sig, 1)

            def attn1_slot(i, n, steps, sums, gate, turn):
                if n == 1:
                    turn_q1(i)
                for k, at in enumerate(steps):
                    if at == n:
                        attn1(i, k)
                if n == sums:
                    sink_share(i)
                    z_sigmoid(i, i * 2 + TURN_ZQ)
                if n == gate:
                    attn1_out(i, 1)
                if n == turn + 1:
                    keep_og(i)

            def keep_og(c):
                for t in range(T):
                    act.wait_ge(og_turned, c * T + T + t + 1)
                    act.activation(o_gated_t[:, bass.ds(c * 4, 4), t * P:t * P + P], two(banks[TURNED + t][:, :], 4),
                                   ACT.Copy).then_inc(og_ready, 1)

            for s in range(UPT):
                split(TURN_Q, s + AHEAD)
                if s == 3:
                    for t in range(T):
                        act.wait_ge(k1_turned, t + 1)
                        act.activation(k1_t[:, :, t * P:t * P + P], two(banks[TURNED + t][:, :], KV_A), ACT.Copy)\
                            .then_inc(k1_ready, 1)
            keep_q1(TURN_Q)
            with act.Fori(0, CHUNKS - 1) as i:
                for s in range(UPT):
                    split(i * 2 + TURN_ZQ, s + AHEAD)
                    attn1_slot(i, s, STEPS, SLOT_SUMS, SLOT_GATE, SLOT_TURN)
                for s in range(UPT):
                    split(i * 2 + TURN_ZQ + 1, s + AHEAD)
                    attn1_slot(i, UPT + s, STEPS, SLOT_SUMS, SLOT_GATE, SLOT_TURN)
                keep_q1(i * 2 + TURN_ZQ + 1)
            last = CHUNKS - 1
            for s in range(UPT):
                split(TURN_Z_LAST, s + AHEAD)
                attn1_slot(last, s, STEPS_LAST, SUMS_LAST, GATE_LAST, UPT * 2)
                if s == 2:
                    act.wait_ge(og_ready, T * CHUNKS)
                if s >= 2:
                    act.wait_ge(mm_done, TURN_Z_LAST * UPT + s - 1)
                    round_h(o_gated_t, s - 2)

            for s in range(UPT):
                split(TURN_OUT, s + AHEAD)
                attn1_slot(last, UPT + s, STEPS_LAST, SUMS_LAST, GATE_LAST, UPT * 2)
                if UPT + s == TURN_LAST:
                    keep_og(last)
                    act.wait_ge(og_ready, T * (CHUNKS + 1))
                    for k in (6, 7):
                        round_h(o_gated_t, k)
            for n in range(CHUNKS - 1):
                if n:
                    for s in range(UPT):
                        split(TURN_OUT + n, s + AHEAD)
                        if n == 1 and s == 4:
                            load_sqrt()
                        if n == CHUNKS - 2 and s >= 3:
                            round_mod(1, s - 3)
                for t in range(T):
                    square_y((n + 1) % 2, t, TURN_OUT + n, TURN_OUT + n, n * T + t + 1, n, sq1)
            residual_turn(1, TURN_QI - 1, PAIR_A, TURN_QI - 1, (CHUNKS - 1) * T + 1, sq1, y1)

            def keep_turned(count, dst, heads=4):
                for t in range(T):
                    act.wait_ge(i_turned, count + t + 1)
                    act.activation(dst[:, :, t * P:t * P + P], two(banks[TURNED + t][:, 0:heads * P], heads), ACT.Copy)\
                        .then_inc(i_t_ready, 1)

            def index_relu(h):
                act.wait_ge(i_scores, h + 1)
                if h >= 2:
                    act.wait_ge(i_added, h - 1)
                act.activation(s2[:, h % 2, :], banks[SCORES + h % 2][:, 0:MASK_W], ACT.Relu).then_inc(i_relu, 1)

            ki_t = v2[:, 0:1, 0:SEQ]
            norm_turn(1, TURN_QI)
            for s in range(2 * UPT):
                split(TURN_KI, s + AHEAD)
                if s == 8:
                    keep_turned(0, q2_t)

            def keep_qk(n, dst):
                for t in range(T):
                    act.wait_ge(qk_turned, n * T + t + 1)
                    act.activation(dst[:, :, t * P:t * P + P], two(banks[TURNED + t][:, :], 4), ACT.Copy)\
                        .then_inc(qk_ready, 1)

            def attn2(g, k):
                if 1 <= k <= 4:
                    act.wait_ge(p2_turned, g * 4 + k)
                    act.activation(p2_t[:, :], banks[TURNED][:, 0:MASK_W], ACT.Copy).then_inc(p2_t_ready, 1)
                if k < 4:
                    act.wait_ge(neg2_ready, g * 4 + k + 1)
                    act.activation(s2[:, k % 2, 0:P], s2[:, k % 2, 0:P], ACT.Exp, bias=m2[:, k % 2, 0:1], scale=SCALE_2,
                                   accum_out=l2[:, k % 2, 0:1])
                    act.activation(s2[:, k % 2, P:MASK_W], s2[:, k % 2, P:MASK_W], ACT.Exp, bias=m2[:, k % 2, 1:2],
                                   scale=SCALE_2, accum_out=l2[:, k % 2, 1:2]).then_inc(p2_ready, 1)
                if k >= 2:
                    act.wait_ge(o2_ready, g * 4 + k - 1)
                    act.activation(o_hi[:, bass.ds(g * 4 + k - 2, 1), :], banks[OUTS][:, 0:SEQ].unsqueeze(1), ACT.Copy)\
                        .then_inc(o2_hi, 1)

            def group_rest(g):
                for s in range(UPT):
                    split(g * 3 + TURN_GRP + 1, s + AHEAD)
                    if s == 4:
                        keep_qk(g * 2, q2_t)
                for s in range(UPT):
                    split(g * 3 + TURN_GRP + 2, s + AHEAD)
                    if s == 4:
                        keep_qk(g * 2 + 1, k2_t)
                for t in range(T):
                    chunk_result(t, g * 3 + TURN_GRP + 2, g * 3 + TURN_GRP + 2)
                    act.activation(v2[:, t, :], pair[PAIR_B][t][:, :], ACT.Copy).then_inc(evicted[PAIR_B][t], 1)

            def attn2_turn(g, turn):
                for s in range(UPT):
                    split(turn, s + AHEAD)
                    if 1 <= s <= 6:
                        attn2(g, s - 1)

            for s in range(UPT):
                split(TURN_GRP, s + AHEAD)
                if s == 1:
                    keep_turned(T, ki_t, 1)
                if s == 4:
                    keep_turned(2 * T, k2_t)
                for h in INDEX_AT.get(s, ()):
                    index_relu(h)
            group_rest(0)
            with act.Fori(1, 4) as g:
                attn2_turn(g - 1, g * 3 + TURN_GRP)
                group_rest(g)

            def keep_gate(n, c, turn, chunk):
                dst = (gate_a, gate_b)[n]
                for t in range(T):
                    chunk_result(t, turn, chunk)
                    act.wait_ge(y_tok_ready, c * T + t + 1)
                    act.activation(dst[:, t, :], pair[n][t][:, :], ACT.Sigmoid).then_inc(evicted[n][t], 1)

            def keep_y(c):
                for t in range(T):
                    act.wait_ge(y_turned, c * T + T + t + 1)
                    act.activation(y_t[:, bass.ds(c * 4, 4), t * P:t * P + P], two(banks[TURNED + t][:, :], 4), ACT.Copy)\
                        .then_inc(y_t_ready, 1)

            attn2_turn(3, TURN_GATE)
            act.wait_ge(o2_kept, 2 * HEADS_2 + 1)
            keep_gate(0, 0, TURN_GATE, CHUNK_GATE)
            for s in range(UPT):
                split(TURN_GATE + 1, s + AHEAD)
                if s < 4:
                    round_gate(0, s)
            keep_gate(1, 0, TURN_GATE + 1, CHUNK_GATE + 1)
            with act.Fori(0, D // CH - 1) as c:
                for s in range(UPT):
                    split(c * 3 + TURN_YAB, s + AHEAD)
                for s in range(UPT):
                    split(c * 3 + TURN_YAB + 1, s + AHEAD)
                    if s == 6:
                        keep_y(c)
                keep_gate(0, c + 1, c * 3 + TURN_YAB + 1, c * 4 + CHUNK_YAB + 2)
                for s in range(UPT):
                    split(c * 3 + TURN_YAB + 2, s + AHEAD)
                keep_gate(1, c + 1, c * 3 + TURN_YAB + 2, c * 4 + CHUNK_YAB + 3)
            act.wait_ge(mm_done, TURN_YAB_LAST * UPT)
            act.wait_ge(y_t_ready, T * (CHUNKS - 1))
            for s in range(UPT):
                split(TURN_YAB_LAST, s + AHEAD)
                if s < 6:
                    round_h(y_t, s)
            for n in range(CHUNKS - 1):
                for s in range(UPT):
                    split(TURN_WO + n, s + AHEAD)
                    if n == 1 and s == 4:
                        load_sqrt()
                    if n == CHUNKS - 2 and s >= 3:
                        round_mod(2, s - 3)
                    if n == 0 and s == 2:
                        keep_y(CHUNKS - 1)
                        act.wait_ge(y_t_ready, T * CHUNKS)
                        for k in (6, 7):
                            round_h(y_t, k)
                for t in range(T):
                    square_y(n % 2, t, TURN_WO + n, CHUNK_WO + n, (CHUNKS + n) * T + t + 1, n, sq2)
            residual_turn(2, TURN_FF1 - 1, PAIR_B, CHUNK_FF1 - 1, (2 * CHUNKS - 1) * T + 1, sq2, y2)

            def relu(p, c, turn):
                for t in range(T):
                    chunk_result(t, turn, c + CHUNK_FF1)
                    act.wait_ge(f_turned, c * T + t + 1)
                    act.activation(f_tok[:, t, :], pair[p][t][:, :], ACT.Relu).then_inc(evicted[p][t], 1)

            def keep_f(c):
                act.wait_ge(f_turned, c * T + 1 + T)
                act.activation(f_t[:, bass.ds(c * 4, 4), 0:P], two(banks[TURNED][:, :], 4), ACT.Copy)\
                    .then_inc(f_t_ready[0], 1)

            def ff1_turn(c):
                for s in range(UPT):
                    split(c + TURN_FF1, s + AHEAD)
                    if s == 4:
                        keep_f(c - 1)

            norm_turn(2, TURN_FF1)
            relu(PAIR_A, 0, TURN_FF1)
            with act.Fori(0, 7) as it:
                for b in range(2):
                    ff1_turn(it * 2 + 1 + b)
                    relu(1 - b, it * 2 + 1 + b, it * 2 + 1 + b + TURN_FF1)
            def round_f(c, b):
                act.activation(h_hi[:, 4 * b:4 * b + 4, :], f_t[:, bass.ds(c * 4, 4), :], ACT.Copy)\
                    .then_inc(f_hi_ready, 1)

            for s in range(UPT):
                split(TURN_FF2 - 1, s + AHEAD)
                if s == 3:
                    for t in range(T):
                        act.wait_ge(f_t_ready[t], 1)
                    act.wait_ge(mm_done, (TURN_FF2 - 1) * UPT + 4 // KG)
                    round_f(0, 0)
                if s == 4:
                    keep_f(14)
                if s >= 4:
                    round_gate(1, s - 4)
            relu(PAIR_B, 15, TURN_FF1 + 15)

            def ff2_turn(c, b, last=False):
                for s in range(UPT):
                    if not last or s + AHEAD < UPT:
                        split(c + TURN_FF2, s + AHEAD)
                    if s == 4 and not last:
                        act.wait_ge(mm_done, (c + TURN_FF2) * UPT)
                        round_f(c + 1, 1 - b)

            split(TURN_FF2, AHEAD)
            keep_f(15)
            for t in range(T):
                act.wait_ge(f_t_ready[t], D_FF // CH)
            for s in range(1, UPT):
                split(TURN_FF2, s + AHEAD)
                if s == 4:
                    round_f(1, 1)
            ff2_turn(1, 1)
            with act.Fori(1, 7) as it:
                for b in range(2):
                    ff2_turn(it * 2 + b, b)
            ff2_turn(14, 0)
            ff2_turn(15, 1, last=True)
            for n, (t, c) in enumerate(LAST_BANKS):
                act.wait_ge(y_last, n // KG + 1)
                act.wait_ge(y_squared, 4 * CHUNKS + n + 1)
                act.activation(f_tok[:, 0, :], banks[t * CHUNKS + c][:, :], ACT.Square, accum_out=y_sq[:, t, c:c + 1])\
                    .then_inc(y_squared, 1)
                if n % CHUNKS == CHUNKS - 1:
                    y_roots(3, t)

        @block.vector
        def _(dve):
            def split(turn, s):
                turn, s = turn + s // UPT, s % UPT
                dve.wait_ge(hi_ready, unit_of(turn, s) + 1)
                dve.tensor_tensor(used(w_lo, turn, s), used(raw, turn, s), used(w_hi, turn, s).bitcast(F32),
                                  ALU.subtract).then_inc(lo_ready, 1)

            def add_ada(m, slot, acc, k, half, loads):
                dve.wait_ge(ada_loaded[slot], loads)
                if not isinstance(m, int) or m > 1:
                    dve.wait_ge(ada_done, m - 1)
                part = acc[:, half * (D // 2):(half + 1) * (D // 2)]
                dve.scalar_tensor_tensor(part, ada_raw[:, slot, :], cond[:, bass.ds(k, 1)], part, ALU.mult, ALU.add)\
                    .then_inc(ada_done, 1)

            def ada(m, n, acc, k):
                add_ada(m + n, n % 2, acc, k, n % 2, (m + n - n % 2) * 8 + 16)

            def y_stats(r, t, squares):
                n = 2 * ((r - 1) * T + t)
                dve.wait_ge(y_squared, squares)
                dve.tensor_reduce(y_var[:, t:t + 1], y_sq[:, t, :], AX.X, ALU.add).then_inc(y_stat, 1)
                dve.wait_ge(y_stat, n + 1)
                dve.tensor_scalar(y_var[:, t:t + 1], y_var[:, t:t + 1], 1.0 / D, EPS, ALU.mult, ALU.add)\
                    .then_inc(y_stat, 1)

            def add_residual(r, t, y):
                n = 2 * ((r - 1) * T + t)
                dve.wait_ge(y_root, n + 1)
                dve.reciprocal(y_rstd[:, t:t + 1], y_rstd[:, t:t + 1]).then_inc(y_root, 1)
                dve.wait_ge(y_root, n + 2)
                for c in range(CHUNKS):
                    piece = x[:, t, c * CH:(c + 1) * CH]
                    dve.scalar_tensor_tensor(piece, y[:, t, c * CH:(c + 1) * CH], y_rstd[:, t:t + 1], piece,
                                             ALU.mult, ALU.add).then_inc(x_new, 1)

            def residual_turn(r, turn, p, uses, y):
                for s in range(TILE_FROM + 1):
                    split(turn, s + AHEAD)
                    pick_mod(r, s + 3, y)
                read_scale(r)
                for t in range(T):
                    y_stats(r, t, (r * CHUNKS - 1) * T + t + 2)
                    scale_y(p, t, (r * CHUNKS - 1) * T + t + 2, CHUNKS - 1, y)
                    for q in (PAIR_A, PAIR_B):
                        dve.wait_ge(evicted[q][t], uses[q])
                    add_residual(r, t, y)
                    if t == 0:
                        split(turn, UPT)
                norm_stats(r)
                split(turn, UPT + 1)
                norm_first(r, pre_gain)
                split(turn, UPT + 2)

            def norm_stats(r):
                dve.wait_ge(x_squared, T * CHUNKS * (r + 1))
                dve.tensor_reduce(x_sq[:, :], x_sq_part[:, :, :], AX.X, ALU.add).then_inc(x_stat, 1)
                dve.wait_ge(x_stat, X_STATS[r] + 1)
                dve.tensor_scalar(x_sq[:, :], x_sq[:, :], 1.0 / D, EPS, ALU.mult, ALU.add).then_inc(x_stat, 1)
                dve.wait_ge(x_root, r + 1)
                dve.reciprocal(x_rstd[:, :], x_rstd[:, :]).then_inc(x_stat, 1)
                if r == 0:
                    return
                dve.wait_ge(x_stat, X_STATS[r] + 3)
                for t in range(T):
                    ins = dve.tensor_scalar(rstd_diag[:, t, :], ident, x_rstd[:, t:t + 1], None, ALU.mult)
                ins.then_inc(x_stat, 1)

            def norm_scale(r, s, gain):
                dve.wait_ge(n_turned, UPT * r + s + 1)
                if r and s == 0:
                    dve.wait_ge(rstd_row_ready, r)
                if s >= 2:
                    dve.wait_ge(h_lo_ready, 2 * UPT * r + s - 1)
                for kk in range(KG):
                    k = KG * s + kk
                    cols = slice(kk * SEQ, (kk + 1) * SEQ)
                    src = banks[SCORES + s % 4][:, cols]
                    if r:
                        ins = dve.scalar_tensor_tensor(norm_tmp[:, s % 2, cols], src, gain[:, k:k + 1], rstd_row[:, :],
                                                       ALU.mult, ALU.mult)
                    else:
                        ins = dve.tensor_scalar(norm_tmp[:, s % 2, cols], src, gain[:, k:k + 1], None, ALU.mult)
                    ins.then_inc(n_scaled, 1)

            def norm_lo(r, s):
                for kk in range(KG):
                    k = KG * s + kk
                    dve.wait_ge(n_rounded, KT * r + k + 1)
                    src = norm_tmp[:, s % 2, kk * SEQ:(kk + 1) * SEQ]
                    hi = h_hi[:, k, :].bitcast(F32)
                    if r:
                        ins = dve.scalar_tensor_tensor(h_lo[:, k, :], src, pre_shift[:, k:k + 1], hi, ALU.add,
                                                       ALU.subtract)
                    else:
                        ins = dve.tensor_tensor(h_lo[:, k, :], src, hi, ALU.subtract)
                ins.then_inc(h_lo_ready, 1)

            def norm_first(r, gain):
                norm_scale(r, 0, gain)
                norm_lo(r, 0)
                norm_scale(r, 1, gain)
                norm_lo(r, 1)
                norm_scale(r, 2, gain)

            def norm_turn(r, turn, gain):
                for s in range(UPT):
                    split(turn, s + AHEAD)
                    if s + 3 < UPT:
                        norm_scale(r, s + 3, gain)
                    if s + 2 < UPT:
                        norm_lo(r, s + 2)

            def low_h(src, s, done):
                dve.wait_ge(h_hi_ready, done + s + 1)
                dve.tensor_tensor(h_lo[:, KG * s:KG * s + KG, :], src[:, KG * s:KG * s + KG, :],
                                  h_hi[:, KG * s:KG * s + KG, :].bitcast(F32), ALU.subtract).then_inc(h_lo_ready, 1)

            def pick_mod(r, j, y):
                n = 2 * (8 * (r - 1) + j)
                dve.wait_ge(mod_rows, SUMS_MOD[r] + j + 1)
                if j:
                    dve.wait_ge(mod_picked, n)
                own = two(y[:, T - 1, D - CH:D], CH // P)
                dve.tensor_tensor(own, two(banks[SCORES + j % 4][:, :], CH // P),
                                  ident.unsqueeze(1).to_broadcast([P, CH // P, P]), ALU.mult).then_inc(mod_picked, 1)
                dve.wait_ge(mod_picked, n + 1)
                columns = pre_gain if of_scale(r, j) else pre_shift
                dve.tensor_reduce(columns[:, j % 4 * CH // P:(j % 4 + 1) * CH // P], own, AX.X, ALU.add)\
                    .then_inc(mod_picked, 1)

            def read_scale(r):
                dve.wait_ge(mod_picked, r * 16)
                gain = (V_MIX, V_FFN)[r - 1]
                dve.scalar_tensor_tensor(pre_gain[:, :], pre_gain[:, :], 1.0, vecs[:, gain:gain + KT], ALU.add,
                                         ALU.mult).then_inc(mod_ready, 1)

            def gate_gain(n, q, bank):
                dve.wait_ge(gain_loaded[n + 1], 16)
                dve.wait_ge(mod_rows, SUMS_GATE[n] + q + 1)
                part = post_gain[:, q * CH:(q + 1) * CH]
                dve.tensor_tensor(part, banks[bank][:, :], part, ALU.mult).then_inc(gain_ready, 1)

            def chunk_result(t, turn, chunk):
                if t == 0:
                    dve.wait_ge(front_done, chunk + 1)
                else:
                    dve.wait_ge(mm_done, unit_of(turn, UPT))

            def scale_y(p, t, n, col, y):
                dve.wait_ge(y_squared, n)
                dve.tensor_tensor(y[:, t, col * CH:(col + 1) * CH], pair[p][t][:, :],
                                  post_gain[:, col * CH:(col + 1) * CH], ALU.mult).then_inc(evicted[p][t], 1)

            dve.sem_inc(s1_masked, 2)
            dve.sem_inc(o1_kept, 1)
            dve.sem_inc(y_tok_ready, T)
            dve.sem_inc(o2_kept, 1)
            dve.wait_ge(cond_sig, 1)
            dve.tensor_tensor(cond[:, :], cond[:, :], vecs[:, V_C:V_C + KT], ALU.mult).then_inc(cond_ready, 1)
            dve.wait_ge(ident_loaded, 16)
            for s in range(AHEAD):
                norm_scale(0, s, vecs[:, V_PRE:V_PRE + KT])
                if s < 2:
                    norm_lo(0, s)
                split(TURN_KV, s)
            norm_turn(0, TURN_KV, vecs[:, V_PRE:V_PRE + KT])
            norm_stats(0)
            dve.wait_ge(x_stat, 3)
            dve.wait_ge(cond_ready, 1)
            for n in range(2):
                dve.wait_ge(acc_init[n], 16)
            dve.wait_ge(sink_loaded, 16)
            dve.tensor_scalar(sink_sc[:, :], sink[:, :], 1.0 / SCALE_A, None, ALU.mult).then_inc(sink_scaled, 1)
            dve.wait_ge(consts_loaded, 16)
            dve.wait_ge(sink_scaled, 1)

            def set_heads(i):
                dve.tensor_copy(slope_cur[:, :], consts[:, bass.ds(i * GROUP_A + C_SLOPE, GROUP_A)])
                dve.tensor_copy(sink_raw_cur[:, :], sink[:, bass.ds(i * GROUP_A, GROUP_A)])
                dve.tensor_copy(sink_cur[:, :], sink_sc[:, bass.ds(i * GROUP_A, GROUP_A)]).then_inc(heads_cur, 1)

            def attn1_scores(i, j):
                h = i * GROUP_A + j
                dve.wait_ge(bias_ready, h + 1)
                dve.wait_ge(s1_ready, h + 1)
                if j == 0:
                    dve.wait_ge(heads_cur, i + 1)
                dve.sem_inc(s1_seen, 1)
                for t, (c0, c1) in enumerate(((0, P), (P, MASK_W))):
                    ins = dve.tensor_tensor_reduce(s1[:, j % 2, c0:c1], banks[SCORES + j % 2][:, c0:c1],
                                                   bias1[:, j % 2, c0:c1], 1.0, LOWEST, ALU.add, ALU.max,
                                                   m1[:, j % 2, t:t + 1])
                ins.then_inc(s1_masked, 1)
                dve.wait_ge(s1_masked, h + 3)
                dve.tensor_scalar(neg_cur[:, j, :], m1[:, j % 2, :], sink_cur[:, j:j + 1], -SCALE_A, ALU.max, ALU.mult)\
                    .then_inc(neg1_ready, 1)

            def sums1(i):
                dve.wait_ge(p1_ready, i * GROUP_A + GROUP_A)
                dve.tensor_tensor(sink_e[:, :, :], neg_cur[:, :, :],
                                  sink_raw_cur[:, :].unsqueeze(2).to_broadcast([P, GROUP_A, T]), ALU.add)\
                    .then_inc(l1_step, 1)

            def gate_z(i):
                for t in range(T):
                    dve.wait_ge(z_sig, i * T + t + 1)
                    dve.scalar_tensor_tensor(z_silu[:, t, :], pair[PAIR_A][t][:, :], x_rstd[:, t:t + 1], z_silu[:, t, :],
                                             ALU.mult, ALU.mult).then_inc(evicted[PAIR_A][t], 1)

            def gate_o(i):
                dve.wait_ge(sink_exp, i + 1)
                dve.tensor_tensor(l_cur[:, :, :], l_cur[:, :, :], sink_e[:, :, :], ALU.add).then_inc(l1_step, 1)
                dve.wait_ge(l1_step, i * 3 + 2)
                dve.reciprocal(l_cur[:, :, :], l_cur[:, :, :]).then_inc(l1_step, 1)
                dve.wait_ge(o1_kept, i * 2 + 3)
                dve.wait_ge(l1_step, i * 3 + 3)
                for t in range(T):
                    part = o[:, t, :].rearrange("p (j d) -> p j d", d=DH_A)
                    inv = l_cur[:, :, t:t + 1].to_broadcast([P, GROUP_A, DH_A])
                    dve.tensor_tensor(part, part, inv, ALU.mult).then_inc(o_step, 1)
                gate_z(i)
                for t in range(T):
                    dve.wait_ge(o_step, i * T + t + 1)
                    dve.wait_ge(evicted[PAIR_A][t], i + 2)
                    dve.tensor_tensor(z_silu[:, t, :], o[:, t, :], z_silu[:, t, :], ALU.mult).then_inc(o_gated, 1)

            def attn1_slot(i, n, steps, sums, gate, turn):
                for k, at in enumerate(steps[0:GROUP_A]):
                    if at == n:
                        attn1_scores(i, k)
                split(turn, n % UPT + AHEAD)
                if n == sums:
                    sums1(i)
                if n == gate:
                    gate_o(i)

            set_heads(0)
            for s in range(UPT):
                split(TURN_Q, s + AHEAD)
                ada(0, s, acc_a, s // 2)
            with dve.Fori(0, CHUNKS - 1) as i:
                for s in range(UPT):
                    attn1_slot(i, s, STEPS, SLOT_SUMS, SLOT_GATE, i * 2 + TURN_ZQ)
                    if s >= 4:
                        ada(i * 12 + 8, s - 4, acc_b, i * 2 + (s - 4) // 2)
                for s in range(UPT):
                    attn1_slot(i, UPT + s, STEPS, SLOT_SUMS, SLOT_GATE, i * 2 + TURN_ZQ + 1)
                    if UPT + s == SLOT_GATE:
                        set_heads(i + 1)
                    ada(i * 12 + 12, s, acc_a, i * 4 + 4 + s // 2)
            last = CHUNKS - 1
            for s in range(UPT):
                attn1_slot(last, s, STEPS_LAST, SUMS_LAST, GATE_LAST, TURN_Z_LAST)
                if s >= 2:
                    low_h(o_gated_t, s - 2, 0)
                if s >= 4:
                    ada(44, s - 4, acc_b, 6 + (s - 4) // 2)

            for n in range(CHUNKS - 1):
                for s in range(UPT):
                    if n == 0:
                        attn1_slot(last, UPT + s, STEPS_LAST, SUMS_LAST, GATE_LAST, TURN_OUT)
                    else:
                        split(TURN_OUT + n, s + AHEAD)
                    if n == 0:
                        if UPT + s == TURN_LAST:
                            for k in (6, 7):
                                low_h(o_gated_t, k, 0)
                    if s in ADA_OUT[n]:
                        n_ada = ADA_OUT_UNITS.index((n, s))
                        ada(48, n_ada, acc_b, 8 + n_ada // 2)
                    if n == CHUNKS - 2 and s >= 5:
                        pick_mod(1, s - 5, y1)
                if n == 0:
                    dve.wait_ge(gain_loaded[0], 16)
                for t in range(T):
                    scale_y((n + 1) % 2, t, n * T + t + 2, n, y1)
            residual_turn(1, TURN_QI - 1, PAIR_A, (7, 6), y1)

            def rope(src, dst, p, t, use, n, heads, half, cos0, sin0, copies=1):
                cols = heads * 2 * half
                cos = consts[:, cos0 + t * half:cos0 + (t + 1) * half]
                sin = consts[:, sin0 + t * half:sin0 + (t + 1) * half]
                xin = src.rearrange("p (h r d) -> p h r d", h=heads, r=2)
                ra = rope_a[:, 0:cols].rearrange("p (h r d) -> p h r d", h=heads, r=2)
                rb = rope_b[:, 0:cols].rearrange("p (h r d) -> p h r d", h=heads, r=2)

                def wide(tab):
                    return tab.unsqueeze(1).to_broadcast([P, heads, half])

                if not (isinstance(n, int) and n + t == 0):
                    dve.wait_ge(rot_ready, n * T + t)
                for r in range(2):
                    dve.tensor_tensor(ra[:, :, r, :], xin[:, :, r, :], wide(cos), ALU.mult)
                for r in range(2):
                    ins = dve.tensor_tensor(rb[:, :, r, :], xin[:, :, 1 - r, :], wide(sin), ALU.mult)
                ins.then_inc(evicted[p][t], 1)
                dve.wait_ge(evicted[p][t], use + 1)
                rows = dst.rearrange("p (h r d) -> p h r d", h=heads * copies, r=2)
                for c in range(copies):
                    for r in range(2):
                        ins = dve.tensor_tensor(rows[:, c * heads:(c + 1) * heads, r, :], ra[:, :, r, :], rb[:, :, r, :],
                                                (ALU.subtract, ALU.add)[r])
                ins.then_inc(rot_ready, 1)

            def index_add(h):
                dve.wait_ge(i_relu, h + 1)
                if h:
                    dve.wait_ge(i_added, h)
                for t, (c0, c1) in enumerate(((0, P), (P, MASK_W))):
                    base = (score if h else causal)[:, c0:c1]
                    ins = dve.scalar_tensor_tensor(score[:, c0:c1], s2[:, h % 2, c0:c1], w_idx[:, t, h:h + 1], base,
                                                   ALU.mult, ALU.add)
                ins.then_inc(i_added, 1)

            def top_round(r):
                if r:
                    dve.wait_ge(top_step, 2 * r)
                for t, (c0, c1) in enumerate(((0, P), (P, MASK_W))):
                    ins = dve.max(top8[:, t, :], score[:, c0:c1])
                ins.then_inc(top_step, 1)
                dve.wait_ge(top_step, 2 * r + 1)
                for t, (c0, c1) in enumerate(((0, P), (P, MASK_W))):
                    ins = dve.match_replace(score[:, c0:c1], top8[:, t, :], score[:, c0:c1], PICKED)
                ins.then_inc(top_step, 1)

            norm_turn(1, TURN_QI, pre_gain)
            def rope_index(turn, t):
                n = 0 if turn == TURN_QI else 2
                chunk_result(t, turn, turn)
                rope(pair[PAIR_A][t][:, :], rot[:, t, :], PAIR_A, t, 7 + n // 2, n, CH // IDX_DIM, IDX_DIM // 2, C_COSI,
                     C_SINI)

            for t in range(T):
                rope_index(TURN_QI, t)
            for s in range(2 * UPT):
                split(TURN_KI, s + AHEAD)
            for t in range(T):
                chunk_result(t, TURN_QI_2, TURN_KI)
                ki = pair[PAIR_B][t]
                dve.tensor_scalar(w_idx[:, t, :], ki[:, IDX_DIM:KI_COLS], IDX_SCALE, None, ALU.mult)\
                    .then_inc(w_idx_ready, 1)
                rope(ki[:, 0:IDX_DIM], rot_key[:, t, :], PAIR_B, t, 6, 1, 1, IDX_DIM // 2, C_COSI, C_SINI, 2)
            dve.wait_ge(i_turned, T)
            for t in range(T):
                rope_index(TURN_QI_2, t)
            dve.wait_ge(w_idx_ready, T)

            def rope_chunk(p, turn, use, n):
                for t in range(T):
                    chunk_result(t, turn, turn)
                    rope(pair[p][t][:, :], rot[:, t, :], p, t, use, n, 4, DH_2 // 2, C_COS, C_SIN)

            def attn2_norm(g, k):
                h = g * 4 + k
                if 1 <= k <= 4:
                    b = (k - 1) % 2
                    dve.wait_ge(p2_ready, h)
                    dve.reciprocal(l2_inv[:, :], l2[:, b, :]).then_inc(l2_ready, 1)
                    dve.wait_ge(l2_ready, h)
                    dve.tensor_scalar(s2[:, b, 0:P], s2[:, b, 0:P], l2_inv[:, 0:1], None, ALU.mult)
                    dve.tensor_scalar(s2[:, b, P:MASK_W], s2[:, b, P:MASK_W], l2_inv[:, 1:2], None, ALU.mult)\
                        .then_inc(p2_normed, 1)

            def attn2_scores(g, k):
                h = g * 4 + k
                if k < 4:
                    dve.wait_ge(s2_ready, h + 1)
                    if k == 0:
                        dve.wait_ge(mask_set, g + 1)
                    dve.sem_inc(s2_seen, 1)
                    for t, (c0, c1) in enumerate(((0, P), (P, MASK_W))):
                        ins = dve.tensor_tensor_reduce(s2[:, k % 2, c0:c1], banks[SCORES + k % 2][:, c0:c1],
                                                       mask_cur[:, c0:c1], 1.0, LOWEST, ALU.add, ALU.max,
                                                       m2[:, k % 2, t:t + 1])
                    ins.then_inc(s2_masked, 1)
                    dve.wait_ge(s2_masked, h + 1)
                    dve.tensor_scalar(m2[:, k % 2, :], m2[:, k % 2, :], -SCALE_2, None, ALU.mult).then_inc(neg2_ready, 1)

            def attn2_out(g, k):
                h = g * 4 + k
                if k >= 2:
                    dve.wait_ge(o2_hi, h - 1)
                    dve.tensor_tensor(o_lo[:, bass.ds(h - 2, 1), :], banks[OUTS][:, 0:SEQ].unsqueeze(1),
                                      o_hi[:, bass.ds(h - 2, 1), :].bitcast(F32), ALU.subtract).then_inc(o2_kept, 1)

            def group_rest(g, with_top=False):
                if with_top:
                    dve.wait_ge(i_turned, 3 * T)
                else:
                    dve.wait_ge(qk_turned, g * 2 * T)
                rope_chunk(PAIR_B, g * 3 + TURN_GRP, g * 2 + 7, g * 2 + 3)
                for s in range(UPT):
                    split(g * 3 + TURN_GRP + 1, s + AHEAD)
                    if with_top and s % 2 == 0:
                        top_round(s // 2)
                    if s % 2:
                        ada(g * 8 + 64, s // 2, acc_a, g * 4 + s // 4)
                dve.wait_ge(qk_turned, g * 2 * T + T)
                rope_chunk(PAIR_A, g * 3 + TURN_GRP + 1, g + 9, g * 2 + 4)
                for s in range(UPT):
                    split(g * 3 + TURN_GRP + 2, s + AHEAD)
                    if with_top and s % 2 == 0:
                        top_round(4 + s // 2)
                    if s % 2:
                        ada(g * 8 + 64, 4 + s // 2, acc_a, g * 4 + 2 + s // 4)

            def attn2_turn(g, turn):
                for s in range(UPT):
                    if 1 <= s <= 6:
                        attn2_norm(g, s - 1)
                        attn2_scores(g, s - 1)
                    split(turn, s + AHEAD)
                    if s == 0:
                        dve.tensor_copy(mask_cur[:, :], masks[:, bass.ds(dve.snap(g >> 1, min_val=0, max_val=1), 1), :]
                                        if not isinstance(g, int) else masks[:, g // 2, :]).then_inc(mask_set, 1)
                    if 1 <= s <= 6:
                        attn2_out(g, s - 1)

            for s in range(UPT):
                split(TURN_GRP, s + AHEAD)
                for h in INDEX_AT.get(s, ()):
                    index_add(h)
            dve.wait_ge(acc_init[2], 16)
            dve.wait_ge(i_added, IDX_HEADS)
            dve.tensor_copy(masks[:, 0, :], causal).then_inc(mask_ready, 1)
            group_rest(0, with_top=True)
            dve.wait_ge(top_step, TOPK // 4)
            dve.tensor_scalar(score[:, :], score[:, :], PICKED_BELOW, MASKED, ALU.is_gt, ALU.mult).then_inc(mask_ready, 1)
            dve.wait_ge(mask_ready, 2)
            dve.tensor_tensor(masks[:, 1, :], score[:, :], causal, ALU.add).then_inc(mask_ready, 1)
            dve.wait_ge(mask_ready, 3)
            with dve.Fori(1, 4) as g:
                attn2_turn(g - 1, g * 3 + TURN_GRP)
                group_rest(g)

            attn2_turn(3, TURN_GATE)
            dve.wait_ge(acc_init[3], 16)
            for s in range(UPT):
                split(TURN_GATE + 1, s + AHEAD)
                if 2 <= s <= 5:
                    gate_gain(0, s - 2, SCORES + s - 2)
                ada(96, s, acc_b, s // 2)
            dve.wait_ge(acc_init[4], 16)

            def gate_ya(c):
                for t in range(T):
                    dve.wait_ge(y_turned, c * T + t + 1)
                    dve.wait_ge(evicted[PAIR_A][t], c * 2 + 14)
                    dve.wait_ge(front_done, c * 4 + CHUNK_YAB + 1)
                    if t:
                        dve.wait_ge(mm_done, c * 3 * UPT + TURN_YAB * UPT + UPT // 2)
                    dve.tensor_tensor(y_tok[:, t, :], pair[PAIR_A][t][:, :], gate_a[:, t, :], ALU.mult)\
                        .then_inc(evicted[PAIR_A][t], 1)

            def gate_y(c):
                for t in range(T):
                    chunk_result(t, c * 3 + TURN_YAB, c * 4 + CHUNK_YAB + 1)
                    dve.wait_ge(evicted[PAIR_B][t], c * 2 + 16)
                    dve.tensor_tensor(gate_b[:, t, :], pair[PAIR_B][t][:, :], gate_b[:, t, :], ALU.mult)\
                        .then_inc(evicted[PAIR_B][t], 1)
                for t in range(T):
                    dve.wait_ge(evicted[PAIR_A][t], c * 2 + 15)
                    dve.wait_ge(evicted[PAIR_B][t], c * 2 + 17)
                    dve.tensor_tensor(y_tok[:, t, :], y_tok[:, t, :], gate_b[:, t, :], ALU.add).then_inc(y_tok_ready, 1)

            with dve.Fori(0, CHUNKS - 1) as c:
                for s in range(UPT):
                    split(c * 3 + TURN_YAB, s + AHEAD)
                    if s % 2:
                        ada(c * 12 + 104, s // 2, acc_a, c * 2 + s // 4)
                    if s == 6:
                        gate_ya(c)
                gate_y(c)
                for part in range(2):
                    for s in range(UPT):
                        split(c * 3 + TURN_YAB + 1 + part, s + AHEAD)
                        if s % 2:
                            ada(c * 12 + 108 + part * 4, s // 2, acc_b, c * 4 + 4 + part * 2 + s // 4)
            for s in range(UPT):
                split(TURN_YAB_LAST, s + AHEAD)
                if s < 6:
                    low_h(y_t, s, UPT)
                if s % 2:
                    ada(140, s // 2, acc_a, 6 + s // 4)
                if s == 6:
                    gate_ya(CHUNKS - 1)
            gate_y(CHUNKS - 1)

            dve.wait_ge(gain_ready, 4)
            for n in range(CHUNKS - 1):
                for s in range(UPT):
                    split(TURN_WO + n, s + AHEAD)
                    if n == 0 and s == 2:
                        for k in (6, 7):
                            low_h(y_t, k, UPT)
                    if s in ADA_WO[n]:
                        n_ada = ADA_WO_UNITS.index((n, s))
                        ada(144, n_ada, acc_a, 8 + n_ada // 2)
                    if n == CHUNKS - 2 and s >= 5:
                        pick_mod(2, s - 5, y2)
                for t in range(T):
                    scale_y(n % 2, t, (CHUNKS + n) * T + t + 2, n, y2)
            residual_turn(2, TURN_FF1 - 1, PAIR_B, (23, 25), y2)

            def square(p, use):
                for t in range(T):
                    dve.wait_ge(evicted[p][t], use + 1)
                    dve.tensor_tensor(f_tok[:, t, :], f_tok[:, t, :], f_tok[:, t, :], ALU.mult).then_inc(f_sq, 1)

            def keep_f(c):
                dve.wait_ge(f_turned, c * T + 2 + T)
                dve.tensor_copy(f_t[:, bass.ds(c * 4, 4), P:SEQ], two(banks[OUTS][:, :], 4)).then_inc(f_t_ready[1], 1)

            norm_turn(2, TURN_FF1, pre_gain)
            square(PAIR_A, 23)
            dve.wait_ge(acc_init[5], 16)

            with dve.Fori(0, 7) as it:
                for b in range(2):
                    for s in range(UPT):
                        split(it * 2 + 1 + b + TURN_FF1, s + AHEAD)
                        if s == 4:
                            keep_f(it * 2 + b)
                        if s in (1, 6):
                            n = 2 * b + s // 6
                            ada(it * 4 + 160, n, acc_a, it * 2 + b)
                    square(1 - b, it + 25 - b)
            def low_f(c, b):
                dve.wait_ge(f_hi_ready, c + 1)
                dve.tensor_tensor(h_lo[:, 4 * b:4 * b + 4, :], f_t[:, bass.ds(c * 4, 4), :],
                                  h_hi[:, 4 * b:4 * b + 4, :].bitcast(F32), ALU.subtract).then_inc(f_lo_ready, 1)

            for s in range(UPT):
                split(TURN_FF2 - 1, s + AHEAD)
                if s < 4:
                    ada(188, s, acc_a, 14 + s // 2)
                if s == 3:
                    dve.wait_ge(f_t_ready[1], 1)
                    low_f(0, 0)
                if s == 4:
                    keep_f(14)
                if s >= 6:
                    gate_gain(1, s - 6, SCORES + s % 2)
            gate_gain(1, 2, SCORES)
            square(PAIR_B, 32)
            gate_gain(1, 3, SCORES + 1)

            def ff2_turn(c, b, last=False):
                for s in range(UPT):
                    if not last or s + AHEAD < UPT:
                        split(c + TURN_FF2, s + AHEAD)
                    if s == 4 and not last:
                        low_f(c + 1, 1 - b)

            split(TURN_FF2, AHEAD)
            keep_f(15)
            dve.wait_ge(f_t_ready[1], D_FF // CH)
            for s in range(1, UPT):
                split(TURN_FF2, s + AHEAD)
                if s == 4:
                    low_f(1, 1)
            ff2_turn(1, 1)
            with dve.Fori(1, 7) as it:
                for b in range(2):
                    ff2_turn(it * 2 + b, b)
            ff2_turn(14, 0)
            ff2_turn(15, 1, last=True)
            dve.wait_ge(gain_ready, 8)
            for n, (t, c) in enumerate(LAST_BANKS):
                if c == CHUNKS - 1:
                    y_stats(3, t, 2 * T * CHUNKS + n + 2)
                dve.wait_ge(y_squared, 2 * T * CHUNKS + n + 2)
                dve.tensor_tensor(y2[:, t, c * CH:(c + 1) * CH], banks[t * CHUNKS + c][:, :],
                                  post_gain[:, c * CH:(c + 1) * CH], ALU.mult).then_inc(y_scaled, 1)
                if c == CHUNKS - 1:
                    dve.wait_ge(y_scaled, n + 1)
                    add_residual(3, t, y2)

        @block.tensor
        def _(pe):
            def three(out_ap, hi, lo, rhs_hi, rhs_lo, start, stop):
                pe.matmul(out_ap, hi, rhs_hi, start=start, stop=False)
                pe.matmul(out_ap, hi, rhs_lo, start=False, stop=False)
                return pe.matmul(out_ap, lo, rhs_hi, start=False, stop=stop)

            def unit_tile(s, t, hi, lo, k0, p, first, last, cols=CH):
                for kk in range(KG):
                    w = slice(kk * CH, kk * CH + cols)
                    mm = three(pair[p][t][:, 0:cols], hi[:, k0 + kk, t * P:(t + 1) * P],
                               lo[:, k0 + kk, t * P:(t + 1) * P], w_hi[:, s % SLOTS, w], w_lo[:, s % SLOTS, w],
                               first and kk == 0, last and kk == KG - 1)
                return mm

            def unit(turn, s, hi, lo, k0, p, use, first, last, cols=CH):
                pe.wait_ge(lo_ready, unit_of(turn, s) + 1)
                for t in range(T):
                    if first and not (isinstance(use, int) and use == 0):
                        pe.wait_ge(evicted[p][t], use)
                    mm = unit_tile(s, t, hi, lo, k0, p, first, last, cols)
                    if last and t == 0:
                        mm.then_inc(front_done, 1)
                mm.then_inc(mm_done, 1)

            def chunk_unit(turn, s, p, use, h=None, cols=CH):
                if h is not None:
                    pe.wait_ge(h_lo_ready, h + s + 1)
                unit(turn, s, h_hi, h_lo, KG * s, p, use, s == 0, s == UPT - 1, cols)

            def mod_sum(r, j):
                if j >= 4:
                    pe.wait_ge(mod_picked, 2 * (8 * (r - 1) + j - 4) + 1)
                rows(SUMS_MOD[r] + j, SCORES + j % 4)

            def residual_turn(r, turn, p, use):
                for s in range(TILE_FROM):
                    chunk_unit(turn, s, p, use)
                    mod_sum(r, s + 4)
                for t in range(T):
                    for s in range(TILE_FROM, UPT):
                        if t == 0:
                            pe.wait_ge(lo_ready, unit_of(turn, s) + 1)
                        mm = unit_tile(s, t, h_hi, h_lo, KG * s, p, False, s == UPT - 1)
                        if t == 0 and s == UPT - 1:
                            mm.then_inc(front_done, 1)
                        elif t:
                            mm.then_inc(mm_done, 1)

            def turn_rows(src, t, n, dst, ready):
                for b in range(n):
                    ins = pe.transpose(dst[:, b * P:(b + 1) * P], src[:, t, b * P:(b + 1) * P], ident)
                ins.then_inc(ready, 1)

            def norm_turned(r, s):
                if r:
                    pe.wait_ge(x_new, ((r - 1) * T + 1) * CHUNKS + KG * s * P // CH + 1)
                else:
                    pe.wait_ge(x_loaded[KG * s * P // CH], 16)
                if s >= 4:
                    pe.wait_ge(n_scaled, KT * r + KG * (s - 3))
                for kk in range(KG):
                    for t in range(T):
                        k = KG * s + kk
                        ins = pe.transpose(banks[SCORES + s % 4][:, kk * SEQ + t * P:kk * SEQ + (t + 1) * P],
                                           x[:, t, k * P:(k + 1) * P], ident)
                ins.then_inc(n_turned, 1)

            def norm_turn(r, turn, p, use, h):
                ahead = 4 if r else 3
                for s in range(ahead):
                    norm_turned(r, s)
                if r:
                    pe.wait_ge(x_stat, X_STATS[r] + 4)
                    for t in range(T):
                        ins = pe.matmul(pair[PAIR_B][0][:, t * P:(t + 1) * P], ones, rstd_diag[:, t, :],
                                        start=True, stop=True)
                    ins.then_inc(rstd_spread, 1)
                for s in range(UPT):
                    chunk_unit(turn, s, p, use, h)
                    if s + ahead < UPT:
                        norm_turned(r, s + ahead)

            def rows(n, bank):
                pe.wait_ge(sum_hi_ready, n + 1)
                pe.matmul(banks[bank][:, :], ones_r[:, :], sum_hi[:, n % 2, :], start=True, stop=False)
                pe.wait_ge(sum_lo_ready, n + 1)
                pe.matmul(banks[bank][:, :], ones_r[:, :], sum_lo[:, :], start=False, stop=True)\
                    .then_inc(mod_rows, 1)

            for credit in (og_turned, y_turned, f_turned):
                pe.sem_inc(credit, T)
            pe.wait_ge(ident_loaded, 16)
            pe.wait_ge(ones_ready, 1)
            norm_turn(0, TURN_KV, PAIR_A, 0, H_NORM0)
            for s in range(UPT):
                chunk_unit(TURN_Q, s, PAIR_B, 0)
                if s == 2:
                    for t in range(T):
                        pe.wait_ge(kv_tok, t + 1)
                        turn_rows(q1_tok, t, KV_A, banks[TURNED + t], k1_turned)

            def turn_q1(i):
                pe.wait_ge(og_ready, i * T + T)
                for t in range(T):
                    pe.wait_ge(evicted[PAIR_B][t], i + 1)
                    turn_rows(q1_tok, t, 4, banks[TURNED + t], q1_turned)

            def attn1(i, k):
                if k < GROUP_A:
                    if k == 0:
                        pe.wait_ge(q1_t_ready, i * T + T)
                        pe.wait_ge(kv_cur_ready, i * 2 + 2)
                    lane = slice((k % 2) * DH_A, (k % 2 + 1) * DH_A)
                    q = q1_t[lane, k // 2, :]
                    pe.matmul(banks[SCORES + k % 2][:, 0:P], q[:, 0:P], k1_cur[lane, 0:P], start=True, stop=True)
                    pe.matmul(banks[SCORES + k % 2][:, P:MASK_W], q[:, P:SEQ], k1_cur[lane, :], start=True, stop=True)\
                        .then_inc(s1_ready, 1)
                if k >= 2:
                    j = k - 2
                    pe.wait_ge(p1_t_ready, i * GROUP_A + j + 1)
                    if j % 4 == 0:
                        pe.wait_ge(o1_kept, i * 2 + j // 4 + 1)
                    out0 = banks[OUTS][:, (j % 4) * DH_A:(j % 4 + 1) * DH_A]
                    out1 = banks[OUTS][:, CH // 2 + (j % 4) * DH_A:CH // 2 + (j % 4 + 1) * DH_A]
                    pe.matmul(out0, p1_t[:, 0:P], v1_cur[:, 0, :], start=True, stop=True)
                    pe.matmul(out1, p1_t[:, P:SEQ], v1_cur[:, 0, :], start=True, stop=False)
                    ins = pe.matmul(out1, p1_t[:, SEQ:MASK_W], v1_cur[:, 1, :], start=False, stop=True)
                    if j % 4 == 3:
                        ins.then_inc(o1_ready, 1)
                if 1 <= k <= GROUP_A:
                    pe.wait_ge(p1_ready, i * GROUP_A + k)
                    for b in range(3):
                        ins = pe.transpose(banks[TURNED][:, b * P:(b + 1) * P],
                                           s1[:, (k - 1) % 2, b * P:(b + 1) * P], ident)
                    ins.then_inc(p1_turned, 1)

            def turn_og(c):
                for t in range(T):
                    pe.wait_ge(o_gated, c * T + t + 1)
                    turn_rows(z_silu, t, 4, banks[TURNED + t], og_turned)

            def attn1_slot(i, n, steps, turn):
                if n == 1:
                    turn_q1(i)
                for k, at in enumerate(steps):
                    if at == n:
                        attn1(i, k)
                if n == turn:
                    turn_og(i)

            pe.wait_ge(k1_ready, T)
            with pe.Fori(0, CHUNKS - 1) as i:
                for s in range(UPT):
                    chunk_unit(i * 2 + TURN_ZQ, s, PAIR_A, i + 1)
                    attn1_slot(i, s, STEPS, SLOT_TURN)
                for s in range(UPT):
                    chunk_unit(i * 2 + TURN_ZQ + 1, s, PAIR_B, i + 1)
                    attn1_slot(i, UPT + s, STEPS, SLOT_TURN)
            last = CHUNKS - 1
            for s in range(UPT):
                chunk_unit(TURN_Z_LAST, s, PAIR_A, CHUNKS)
                attn1_slot(last, s, STEPS_LAST, TURN_LAST)
            for n in range(CHUNKS - 1):
                for s in range(UPT):
                    chunk_unit(TURN_OUT + n, s, (n + 1) % 2, CHUNKS + (n + 1) // 2, H_OUT)
                    if n == 0:
                        attn1_slot(last, UPT + s, STEPS_LAST, TURN_LAST)
                    if n == CHUNKS - 2 and s >= 4:
                        mod_sum(1, s - 4)
            residual_turn(1, TURN_QI - 1, PAIR_A, CHUNKS + 2)

            ki_t = v2[:, 0:1, 0:SEQ]

            def turn_index(n, blocks):
                for t in range(T):
                    pe.wait_ge(rot_ready, n * T + t + 1)
                    turn_rows(rot_key if n == 1 else rot, t, blocks, banks[TURNED + t], i_turned)

            def index_scores(h):
                if h >= 2:
                    pe.wait_ge(i_relu, h - 1)
                if h % 8 == 0:
                    pe.wait_ge(i_t_ready, 2 * T + h // 8 * T)
                lane = slice((h % 2) * IDX_DIM, (h % 2 + 1) * IDX_DIM)
                q = (q2_t, k2_t)[h // 8][lane, h // 2 % 4, :]
                keys = ki_t[lane, 0, :]
                pe.matmul(banks[SCORES + h % 2][:, 0:P], q[:, 0:P], keys[:, 0:P], start=True, stop=True)
                pe.matmul(banks[SCORES + h % 2][:, P:MASK_W], q[:, P:SEQ], keys, start=True, stop=True)\
                    .then_inc(i_scores, 1)

            norm_turn(1, TURN_QI, PAIR_A, 7, H_NORM1)
            for s in range(2 * UPT):
                p, use, cols = (PAIR_A, 8, CH) if s % 2 else (PAIR_B, 6, KI_COLS)
                unit(TURN_KI, s, h_hi, h_lo, KG * (s // 2), p, use, s < 2, s >= 2 * UPT - 2, cols)
                if s == 6:
                    turn_index(0, 4)

            def turn_qk(n):
                for t in range(T):
                    pe.wait_ge(rot_ready, (n + 3) * T + t + 1)
                    turn_rows(rot, t, 4, banks[TURNED + t], qk_turned)

            def attn2(g, k):
                h = g * 4 + k
                if k < 4:
                    if k == 0:
                        pe.wait_ge(qk_ready, (g + 1) * 2 * T)
                        for t in range(T):
                            pe.wait_ge(evicted[PAIR_B][t], g * 2 + 9)
                    bank = banks[SCORES + k % 2]
                    pe.matmul(bank[:, 0:P], q2_t[:, k, 0:P], k2_t[:, k, 0:P], start=True, stop=True)
                    pe.matmul(bank[:, P:MASK_W], q2_t[:, k, P:SEQ], k2_t[:, k, :], start=True, stop=True)\
                        .then_inc(s2_ready, 1)
                if k >= 2:
                    pe.wait_ge(p2_t_ready, h - 1)
                    pe.wait_ge(o2_kept, h - 1)
                    head = slice((k - 2) * DH_2, (k - 1) * DH_2)
                    pe.matmul(banks[OUTS][:, 0:SEQ], v2[:, 0, head], p2_t[:, 0:SEQ], start=True, stop=False)
                    pe.matmul(banks[OUTS][:, P:SEQ], v2[:, 1, head], p2_t[:, SEQ:MASK_W], start=False, stop=True)\
                        .then_inc(o2_ready, 1)
                if 1 <= k <= 4:
                    pe.wait_ge(p2_normed, h)
                    for b in range(3):
                        ins = pe.transpose(banks[TURNED][:, b * P:(b + 1) * P], s2[:, (k - 1) % 2, b * P:(b + 1) * P],
                                           ident)
                    ins.then_inc(p2_turned, 1)

            def group_rest(g):
                for s in range(UPT):
                    chunk_unit(g * 3 + TURN_GRP + 1, s, PAIR_A, g + 9)
                    if s == 3:
                        pe.wait_ge(o2_kept, g * 4 + 1)
                        turn_qk(g * 2)
                for s in range(UPT):
                    chunk_unit(g * 3 + TURN_GRP + 2, s, PAIR_B, g * 2 + 8)
                    if s == 3:
                        turn_qk(g * 2 + 1)

            def attn2_turn(g, turn, p, use):
                for s in range(UPT):
                    chunk_unit(turn, s, p, use)
                    if 1 <= s <= 6:
                        attn2(g, s - 1)

            for s in range(UPT):
                chunk_unit(TURN_GRP, s, PAIR_B, 7)
                if s == 1:
                    pe.wait_ge(i_t_ready, T)
                    turn_index(1, 1)
                if s == 3:
                    turn_index(2, 4)
                for h in INDEX_AT.get(s, ()):
                    index_scores(h)
            pe.wait_ge(i_relu, IDX_HEADS)
            group_rest(0)
            with pe.Fori(1, 4) as g:
                attn2_turn(g - 1, g * 3 + TURN_GRP, PAIR_B, g * 2 + 7)
                group_rest(g)

            attn2_turn(3, TURN_GATE, PAIR_A, 13)
            pe.wait_ge(o2_kept, 2 * HEADS_2 + 1)
            for s in range(UPT):
                chunk_unit(TURN_GATE + 1, s, PAIR_B, 15)
                if 1 <= s <= 4:
                    rows(SUMS_GATE[0] + s - 1, SCORES + s - 1)

            def out_units(c):
                for s in range(UPT):
                    p = s // (UPT // 2)
                    at = s % (UPT // 2)
                    unit(c * 3 + TURN_YAB, s, o_hi, o_lo, KG * s, p, c * 2 + 14 + 2 * p, at == 0, at == UPT // 2 - 1)

            def turn_y(c):
                for t in range(T):
                    pe.wait_ge(y_tok_ready, c * T + T + t + 1)
                    turn_rows(y_tok, t, 4, banks[TURNED + t], y_turned)

            with pe.Fori(0, D // CH - 1) as c:
                out_units(c)
                for s in range(UPT):
                    chunk_unit(c * 3 + TURN_YAB + 1, s, PAIR_A, c * 2 + 15)
                    if s == 5:
                        turn_y(c)
                for s in range(UPT):
                    chunk_unit(c * 3 + TURN_YAB + 2, s, PAIR_B, c * 2 + 17)
            out_units(CHUNKS - 1)
            for n in range(CHUNKS - 1):
                for s in range(UPT):
                    chunk_unit(TURN_WO + n, s, n % 2, 21 + n // 2 + 2 * (n % 2), H_WO)
                    if n == 0 and s == 1:
                        turn_y(CHUNKS - 1)
                    if n == CHUNKS - 2 and s >= 4:
                        mod_sum(2, s - 4)
            residual_turn(2, TURN_FF1 - 1, PAIR_B, 24)

            def turn_f(c):
                for t in range(T):
                    pe.wait_ge(f_sq, c * T + t + 1)
                    turn_rows(f_tok, t, 4, banks[TURNED + t], f_turned)

            def ff1_turn(c, p, use):
                for s in range(UPT):
                    chunk_unit(c + TURN_FF1, s, p, use)
                    if s == 3:
                        turn_f(c - 1)

            def gate_sums(q):
                if q >= 2:
                    pe.wait_ge(gain_ready, 4 + q - 1)
                rows(SUMS_GATE[1] + q, SCORES + q % 2)

            norm_turn(2, TURN_FF1, PAIR_A, 23, H_NORM2)
            with pe.Fori(0, 7) as it:
                for b in range(2):
                    ff1_turn(it * 2 + 1 + b, 1 - b, it + 25 - b)
            for s in range(UPT):
                chunk_unit(TURN_FF2 - 1, s, PAIR_B, 32)
                if s == 3:
                    turn_f(14)
                if s >= 5:
                    gate_sums(s - 5)

            def ff2_half(s, t, b, start=False, stop=False):
                k = 4 * b + s // 2
                for cc in range(KG):
                    w = slice(cc * CH, (cc + 1) * CH)
                    mm = three(banks[t * CHUNKS + s % 2 * KG + cc][:, :], h_hi[:, k, t * P:(t + 1) * P],
                               h_lo[:, k, t * P:(t + 1) * P], w_hi[:, s % SLOTS, w], w_lo[:, s % SLOTS, w],
                               start and s < 2, stop and s >= UPT - 2)
                return mm

            def ff2_turn(c, b, first_unit=0, units=UPT):
                pe.wait_ge(f_lo_ready, c + 1)
                for s in range(first_unit, units):
                    pe.wait_ge(lo_ready, unit_of(c + TURN_FF2, s) + 1)
                    for t in range(T):
                        mm = ff2_half(s, t, b)
                    mm.then_inc(mm_done, 1)

            pe.wait_ge(f_lo_ready, 1)
            for t in range(T):
                pe.wait_ge(evicted[PAIR_A][t], 31)
            pe.wait_ge(lo_ready, unit_of(TURN_FF2, 0) + 1)
            ff2_half(0, 0, 0, start=True)
            gate_sums(3)
            pe.wait_ge(lo_ready, unit_of(TURN_FF2, 1) + 1)
            for t in range(T):
                pe.wait_ge(evicted[PAIR_B][t], 33)
            ff2_half(1, 0, 0, start=True)
            turn_f(15)
            pe.wait_ge(gain_ready, 8)
            ff2_half(0, 1, 0, start=True).then_inc(mm_done, 1)
            for t in range(T):
                pe.wait_ge(f_t_ready[t], D_FF // CH)
            ff2_half(1, 1, 0, start=True).then_inc(mm_done, 1)
            ff2_turn(0, 0, 2)
            ff2_turn(1, 1)
            with pe.Fori(1, 7) as it:
                for b in range(2):
                    ff2_turn(it * 2 + b, b)
            ff2_turn(14, 0)
            ff2_turn(15, 1, units=TILE_FROM)
            for t in range(T):
                for s in range(TILE_FROM, UPT):
                    if t == 0:
                        pe.wait_ge(lo_ready, unit_of(TURNS - 1, s) + 1)
                    mm = ff2_half(s, t, 1, stop=True)
                    if s >= UPT - 2:
                        mm.then_inc(y_last, 1)


_OUT = (1, SEQ, D)


def kernel(x, g_pre, g_post, w_in_a, w_out_a, sinks_a, w_in_b, w_out_b, w_in_c, b_f_c, w_out_c, c_2,
           w_ada_2, b_ada_2, g_pre_mix_2, g_post_mix_2, w_in_2, w_moba_out_2, w_dsa_out_2, w_o_2,
           g_pre_ffn_2, g_post_ffn_2, w_ff1_2, w_ff2_2):
    import concourse.bacc as bacc
    from concourse.bass_utils import run_bass_kernel_spmd

    def columns(v):
        return np.asarray(v).reshape(KT, P).T

    arrays = {
        "x": np.asarray(x)[0],
        "w_in_a": np.asarray(w_in_a)[0],
        "w_out_a": np.asarray(w_out_a)[0],
        "w_ada": np.asarray(w_ada_2)[0],
        "w_in_2": np.asarray(w_in_2)[0],
        "w_moba": np.asarray(w_moba_out_2)[0],
        "w_dsa": np.asarray(w_dsa_out_2)[0],
        "w_o": np.asarray(w_o_2)[0],
        "w_ff1": np.asarray(w_ff1_2)[0],
        "w_ff2": np.asarray(w_ff2_2)[0],
        "b_ada": np.asarray(b_ada_2),
        "g_post": np.asarray(g_post)[0],
        "g_post_mix": np.asarray(g_post_mix_2)[0],
        "g_post_ffn": np.asarray(g_post_ffn_2)[0],
        "sinks": np.asarray(sinks_a)[0],
        "vecs": np.concatenate([columns(v) for v in (g_pre, g_pre_mix_2, g_pre_ffn_2, c_2)], axis=1),
        "consts": shape_constants(),
    }
    arrays = {n: np.ascontiguousarray(a) for n, a in arrays.items()}
    nc = bacc.Bacc("TRN2", target_bir_lowering=False, num_devices=1)
    args = [nc.dram_tensor("in_" + n, a.shape, F32, kind="ExternalInput").ap() for n, a in arrays.items()]
    out = nc.dram_tensor("out", (SEQ, D), F32, kind="ExternalOutput").ap()
    two_block_kernel(nc, *args, out)
    got = run_bass_kernel_spmd(nc, [{"in_" + n: a for n, a in arrays.items()}], core_ids=[0]).results[0]["out"]
    return got.reshape(_OUT)
```
